# Optimizing a Trainium2 kernel written in Bass

```python
import math
import jax, jax.numpy as jnp
from jax import lax
import numpy as np

D_MODEL = 1024
BATCH = 1
SEQ = 1024
DEPTH = 2

N_META = 16
HEAD_DIM = 64
N_Q_HEADS = 16
N_KV_HEADS = 4
Q_PER_KV = N_Q_HEADS // N_KV_HEADS
D_ATTN = N_Q_HEADS * HEAD_DIM
D_KV = N_KV_HEADS * HEAD_DIM
WINDOW = 128
BLOCK = 128
ROPE_THETA = 10000.0
ATTN_SCALE = HEAD_DIM ** -0.5
NEG_INF = -1e30
D_SSM = D_MODEL // 2
SSM_GROUP = 16
N_SSM_GROUPS = D_SSM // SSM_GROUP
SSM_STATE = 64
DT_MIN = 1e-3
DT_MAX = 1e-1
D_FF = 4 * D_MODEL
RMS_EPS = 1e-6
D_IN = D_SSM + D_ATTN + 2 * D_KV + 2 * D_MODEL

kernel_name = "hybrid_s5_swa_sink_gated_block"

def rmsnorm(x, gain):
    xf = x.astype(jnp.float32)
    xf = xf * lax.rsqrt(jnp.mean(xf * xf, axis=-1, keepdims=True) + RMS_EPS)
    return (xf * gain.astype(jnp.float32)).astype(x.dtype)

def rotary(t, pos):
    inv_freq = 1.0 / (ROPE_THETA ** (jnp.arange(0, HEAD_DIM, 2, dtype=jnp.float32) / HEAD_DIM))
    ang = pos.astype(jnp.float32)[:, None] * inv_freq[None, :]
    ang = jnp.concatenate([ang, ang], axis=-1)[None, :, None, :]
    tf = t.astype(jnp.float32)
    half = HEAD_DIM // 2
    rot = jnp.concatenate([-tf[..., half:], tf[..., :half]], axis=-1)
    return (tf * jnp.cos(ang) + rot * jnp.sin(ang)).astype(t.dtype)

def s5_branch(u, a_re, a_im, log_dt, b_re, b_im, c_re, c_im, d_skip, w_glu, b_glu):
    bsz, seq_len, _ = u.shape
    f32 = jnp.float32
    uf = u.astype(f32).reshape(bsz, seq_len, N_SSM_GROUPS, SSM_GROUP)
    a = lax.complex(a_re.astype(f32), a_im.astype(f32))
    dt = jnp.exp(log_dt.astype(f32))[:, None]
    a_bar = jnp.exp(a * dt)
    b = lax.complex(b_re.astype(f32), b_im.astype(f32))
    b_bar = ((a_bar - 1.0) / a)[..., None] * b
    bu = jnp.einsum('blgc,gnc->blgn', uf.astype(jnp.complex64), b_bar)

    def combine(e1, e2):
        a1, s1 = e1
        a2, s2 = e2
        return a1 * a2, a2 * s1 + s2

    a_seq = jnp.broadcast_to(a_bar, bu.shape)
    _, states = lax.associative_scan(combine, (a_seq, bu), axis=1)
    c = lax.complex(c_re.astype(f32), c_im.astype(f32))
    y = jnp.einsum('blgn,gcn->blgc', states, c).real + d_skip.astype(f32) * uf
    y = y.reshape(bsz, seq_len, D_SSM)
    z = jax.nn.gelu(y)
    z = z * jax.nn.sigmoid(z @ w_glu.astype(f32) + b_glu.astype(f32))
    return z.astype(u.dtype)

def sliding_window_attention(q, k, v, sinks):
    bsz, seq_len = q.shape[0], q.shape[1]
    pad = (-seq_len) % BLOCK
    n_blk = (seq_len + pad) // BLOCK
    qb = jnp.pad(q, ((0, 0), (pad, 0), (0, 0), (0, 0))).reshape(
        bsz, n_blk, BLOCK, N_KV_HEADS, Q_PER_KV, HEAD_DIM)
    front = ((0, 0), (pad + BLOCK, 0), (0, 0), (0, 0))
    kb = jnp.pad(k, front).reshape(bsz, n_blk + 1, BLOCK, N_KV_HEADS, HEAD_DIM)
    vb = jnp.pad(v, front).reshape(bsz, n_blk + 1, BLOCK, N_KV_HEADS, HEAD_DIM)
    k_win = jnp.concatenate([kb[:, :-1], kb[:, 1:]], axis=2)
    v_win = jnp.concatenate([vb[:, :-1], vb[:, 1:]], axis=2)
    k_meta, v_meta = k[:, :N_META], v[:, :N_META]

    s_meta = jnp.einsum('bnqkgd,bskd->bnkgqs', qb, k_meta, preferred_element_type=jnp.float32)
    s_win = jnp.einsum('bnqkgd,bnskd->bnkgqs', qb, k_win, preferred_element_type=jnp.float32)
    s = jnp.concatenate([s_meta, s_win], axis=-1) * ATTN_SCALE

    q_idx = (jnp.arange(n_blk)[:, None] * BLOCK + jnp.arange(BLOCK)[None, :])[:, :, None]
    kw_idx = ((jnp.arange(n_blk)[:, None] - 1) * BLOCK + jnp.arange(2 * BLOCK)[None, :])[:, None, :]
    km_idx = (pad + jnp.arange(N_META))[None, None, :]
    win_ok = (kw_idx >= pad) & (kw_idx <= q_idx) & (q_idx - kw_idx < WINDOW)
    meta_ok = (km_idx <= q_idx) & (q_idx - km_idx >= WINDOW)
    ok = jnp.concatenate([jnp.broadcast_to(meta_ok, (n_blk, BLOCK, N_META)), win_ok], axis=-1)
    s = jnp.where(ok[None, :, None, None], s, NEG_INF)

    sink = sinks.astype(jnp.float32).reshape(N_KV_HEADS, Q_PER_KV)[None, None, :, :, None, None]
    m = jnp.maximum(jnp.max(s, axis=-1, keepdims=True), sink)
    p = jnp.exp(s - m)
    p = p / (jnp.sum(p, axis=-1, keepdims=True) + jnp.exp(sink - m))
    p = p.astype(v.dtype)
    o = (jnp.einsum('bnkgqs,bskd->bnqkgd', p[..., :N_META], v_meta)
         + jnp.einsum('bnkgqs,bnskd->bnqkgd', p[..., N_META:], v_win))
    return o.reshape(bsz, n_blk * BLOCK, D_ATTN)[:, pad:]

def hybrid_mixer(h, pos, w_in, a_re, a_im, log_dt, b_re, b_im, c_re, c_im, d_skip, w_glu, b_glu,
                 sinks, w_o_ssm, w_o_attn, w_out):
    bsz, seq_len, _ = h.shape
    proj = h @ w_in
    cuts = [D_SSM, D_SSM + D_ATTN, D_SSM + D_ATTN + D_KV, D_SSM + D_ATTN + 2 * D_KV,
            D_SSM + D_ATTN + 2 * D_KV + D_MODEL]
    u, q, k, v, g_ssm, g_attn = jnp.split(proj, cuts, axis=-1)
    y_ssm = s5_branch(u, a_re, a_im, log_dt, b_re, b_im, c_re, c_im, d_skip, w_glu, b_glu)
    q = rotary(q.reshape(bsz, seq_len, N_Q_HEADS, HEAD_DIM), pos)
    k = rotary(k.reshape(bsz, seq_len, N_KV_HEADS, HEAD_DIM), pos)
    v = v.reshape(bsz, seq_len, N_KV_HEADS, HEAD_DIM)
    y_attn = sliding_window_attention(q, k, v, sinks)
    merged = jax.nn.sigmoid(g_ssm) * (y_ssm @ w_o_ssm) + jax.nn.sigmoid(g_attn) * (y_attn @ w_o_attn)
    return merged @ w_out

def setup_inputs(seed: int = 0) -> dict:
    key = jax.random.key(seed)
    ks = jax.random.split(key, 24)
    f32 = jnp.float32

    def nrm(k, shape, std):
        return std * jax.random.normal(k, shape, f32)

    G, N, C = N_SSM_GROUPS, SSM_STATE, SSM_GROUP
    a_im_init = math.pi * jnp.arange(N, dtype=f32)[None, None, :]
    return {
        "x": nrm(ks[0], (BATCH, SEQ, D_MODEL), 1.0),
        "meta_tokens": nrm(ks[1], (N_META, D_MODEL), 1.0),
        "norm_mix_pre": 1.0 + nrm(ks[2], (DEPTH, D_MODEL), 0.02),
        "norm_mix_post": 1.0 + nrm(ks[3], (DEPTH, D_MODEL), 0.02),
        "norm_mlp_pre": 1.0 + nrm(ks[4], (DEPTH, D_MODEL), 0.02),
        "norm_mlp_post": 1.0 + nrm(ks[5], (DEPTH, D_MODEL), 0.02),
        "w_in": nrm(ks[6], (DEPTH, D_MODEL, D_IN), D_MODEL ** -0.5),
        "ssm_a_re": -0.5 + nrm(ks[7], (DEPTH, G, N), 0.01),
        "ssm_a_im": a_im_init + nrm(ks[8], (DEPTH, G, N), 0.01),
        "ssm_log_dt": jax.random.uniform(ks[9], (DEPTH, G), f32, math.log(DT_MIN), math.log(DT_MAX)),
        "ssm_b_re": nrm(ks[10], (DEPTH, G, N, C), (2.0 * C) ** -0.5),
        "ssm_b_im": nrm(ks[11], (DEPTH, G, N, C), (2.0 * C) ** -0.5),
        "ssm_c_re": nrm(ks[12], (DEPTH, G, C, N), 0.5),
        "ssm_c_im": nrm(ks[13], (DEPTH, G, C, N), 0.5),
        "ssm_d": nrm(ks[14], (DEPTH, G, C), 1.0),
        "w_glu": nrm(ks[15], (DEPTH, D_SSM, D_SSM), D_SSM ** -0.5),
        "b_glu": nrm(ks[16], (DEPTH, D_SSM), 0.01),
        "attn_sinks": nrm(ks[17], (DEPTH, N_Q_HEADS), 0.5),
        "w_o_ssm": nrm(ks[18], (DEPTH, D_SSM, D_MODEL), D_SSM ** -0.5),
        "w_o_attn": nrm(ks[19], (DEPTH, D_ATTN, D_MODEL), D_ATTN ** -0.5),
        "w_out": nrm(ks[20], (DEPTH, D_MODEL, D_MODEL), D_MODEL ** -0.5),
        "w_up": nrm(ks[21], (DEPTH, D_MODEL, D_FF), D_MODEL ** -0.5),
        "w_down": nrm(ks[22], (DEPTH, D_FF, D_MODEL), D_FF ** -0.5),
    }

def reference(x, meta_tokens, norm_mix_pre, norm_mix_post, norm_mlp_pre, norm_mlp_post, w_in,
              ssm_a_re, ssm_a_im, ssm_log_dt, ssm_b_re, ssm_b_im, ssm_c_re, ssm_c_im, ssm_d,
              w_glu, b_glu, attn_sinks, w_o_ssm, w_o_attn, w_out, w_up, w_down):
    bsz = x.shape[0]
    meta = jnp.broadcast_to(meta_tokens[None].astype(x.dtype), (bsz, N_META, D_MODEL))
    hres = jnp.concatenate([meta, x], axis=1)
    pos = jnp.arange(hres.shape[1], dtype=jnp.int32)
    for l in range(DEPTH):
        h = rmsnorm(hres, norm_mix_pre[l])
        mix = hybrid_mixer(h, pos, w_in[l], ssm_a_re[l], ssm_a_im[l], ssm_log_dt[l], ssm_b_re[l],
                           ssm_b_im[l], ssm_c_re[l], ssm_c_im[l], ssm_d[l], w_glu[l], b_glu[l],
                           attn_sinks[l], w_o_ssm[l], w_o_attn[l], w_out[l])
        hres = hres + rmsnorm(mix, norm_mix_post[l])
        h = rmsnorm(hres, norm_mlp_pre[l])
        ff = jnp.square(jax.nn.relu(h @ w_up[l])) @ w_down[l]
        hres = hres + rmsnorm(ff, norm_mlp_post[l])
    return hres[:, N_META:]


_drawn_inputs = setup_inputs


def setup_inputs(seed=0):
    import zlib

    import numpy as np

    out = dict(_drawn_inputs(seed))
    spreads = {}
    factors = {'norm_mix_post': 3.07,
     'norm_mlp_pre': 8.975,
     'norm_mlp_post': 9.74,
     'ssm_a_re': 64.0,
     'b_glu': 8.0,
     'attn_sinks': 8.0}
    for name, (base, spread) in spreads.items():
        noise = np.random.default_rng([zlib.crc32(name.encode()), seed]).standard_normal(out[name].shape)
        drawn = base * np.exp(spread * noise) if base else spread * noise
        out[name] = __import__('jax').numpy.asarray(drawn.astype(out[name].dtype))
    for name, factor in factors.items():
        out[name] = (out[name] * factor).astype(out[name].dtype)
    return out
```

```python
from contextlib import ExitStack

import numpy as np
import concourse.bass as bass
from concourse import mybir

P = 128
D = 1024
SEQ = 1024
NMETA = 16
DEPTH = 2
KD = D // P
L = SEQ + NMETA
NC3 = 3
CW = 348
LP = NC3 * CW
NBLK = SEQ // P
NH = 16
NKV = 4
HD = 64
G_S = 32
CG = 16
NS = 64
NP = G_S // 2
CT = 8
NCH = L // CT
SEG, RUN = 13, 10
assert SEG * RUN == NCH and (SEG - 1) % 3 == 0 and (RUN - 1) % 3 == 0
NB = 4
DFF = 4 * D
EPS = 1e-6
SCALE = HD ** -0.5
KEYS = 288
KOFF = 144
NEG = -1e30

S_U, S_Q, S_K, S_V, S_G = 0, 4, 12, 14, 16
S_OA, S_GLU, S_OS, S_OUT, S_FF = 32, 40, 44, 52, 60
STRIPS = 124
A_PER, B_PER = 74, 54
A_INIT, B_INIT = 4, 4

F32 = mybir.dt.float32
F32R = mybir.dt.float32r
ALU = mybir.AluOpType
ACT = mybir.ActivationFunctionType
AX = mybir.AxisListType
ds = bass.ds


def a_use(s):
    if s < 16:
        return 1 + s // 2 if s % 2 == 0 else None
    if s < 32:
        return 9 + s - 16
    if s < 60:
        return 25 + (s - 32) // 2 if s % 2 == 0 else None
    return 41 + (s - 60) // 2 if s % 2 == 0 else None


def b_use(s):
    if s < 16:
        return (s - 1) // 2
    if s < 60:
        return 8 + (s - 33) // 2
    return 22 + (s - 61) // 2


EVF, EVH = 16, 48
A_PRE1, A_POST1, A_PRE2, A_POST2 = 0, 39, 40, 73


def build(nc, x, meta, norms, w_in, a_re, a_im, log_dt, b_re, b_im, c_re, c_im, d_skip, w_glu, b_glu, sinks,
          w_o_ssm, w_o_attn, w_out, w_up, w_down, cos_t, sin_t, mask_t, mask0_t, ident_t, out):
    with ExitStack() as ctx:
        base = (nc.sbuf_base + 31) // 32 * 32

        def at(name, shape, off, dt=F32):
            return nc.alloc_sbuf_tensor_at(name, shape, dt, offset=base + 4 * off, align_bytes=4)

        TL = KD * LP
        HH, HL = at("h_hi", [P, KD, LP], 0, F32R), at("h_lo", [P, KD, LP], TL, F32R)
        BH, BL = at("b_hi", [P, KD, LP], 2 * TL, F32R), at("b_lo", [P, KD, LP], 3 * TL, F32R)
        X, XR = at("x_res", [P, KD, LP], 4 * TL), at("z2_split", [P, KD, LP], 4 * TL, F32R)
        WRAW = at("w_raw", [P, 2, KD, P], 5 * TL)
        WHI, WLO = at("w_hi", [P, 2, KD, P], 5 * TL + 2048, F32R), at("w_lo", [P, 2, KD, P], 5 * TL + 4096, F32R)
        M0 = 5 * TL + 6144
        ident = at("ident", [P, P], M0)
        ones = at("ones", [P, P], M0 + 128)
        gains = at("gains", [P, DEPTH, 4, KD], M0 + 256)
        bglu = at("bglu", [P, DEPTH, 4], M0 + 320)
        sink = at("sink", [P, DEPTH, NH], M0 + 328)
        mask0 = at("mask0", [P, NMETA], M0 + 360)
        bgluh = at("bgluh", [P, DEPTH, 4], M0 + 376)
        stat = at("att_stat", [P, 6, NH], M0 + 384)
        M1 = M0 + 480
        MT = at("m_tiles", [P, 4, LP], M1)
        s_sb = at("s_sb", [P, 4, KEYS], M1)
        mask_cur = at("mask_cur", [P, KEYS], M1 + 1152)
        mask_rest = at("mask_rest", [P, KEYS], M1 + 1440)
        pt_sb = at("pt_sb", [P, 2, 4, P], M1 + 1728)
        PW = at("pw", [P, CT + 1, NP, 2], M1 + 2752)
        PWs = at("pw_s", [P, CT + 1, NP, 2], M1 + 3040)
        P8 = at("p8", [P, RUN + 1, NP, 2], M1 + 3328)
        P8s = at("p8_s", [P, RUN + 1, NP, 2], M1 + 3776)
        FB = at("f_b", [P, NP, 2], M1 + 4224)
        FBs = at("f_bs", [P, NP, 2], M1 + 4256)
        BB = at("b_bar", [P, 4, 2, CG], M1 + 4288)
        T1p = at("pool_t1", [P, P], M1 + 4416)
        T2p = at("pool_t2", [P, P], M1 + 4544)
        pm_sb = at("pm_sb", [P, 4, 32], M1 + 4672)
        assert M0 + 480 + 4800 <= (nc.sbuf_usable_end - base) // 4 - 8, (M1 + 4672, nc.sbuf_usable_end - base)
        QY = at("qy", [P, KD, LP], 2 * TL)
        R1 = 3 * TL
        cosb, sinb = at("cosb", [P, LP], R1), at("sinb", [P, LP], R1 + LP)
        rot = at("rot", [P, LP], R1 + 2 * LP)
        rt1, rt2 = at("rt1", [P, LP], R1 + 3 * LP), at("rt2", [P, LP], R1 + 4 * LP)
        ut = at("u_tok", [P, LP], R1 + 5 * LP)
        ust = at("u_stage", [P, 2, CT, NCH], R1 + 6 * LP)
        Uch = at("u_chunk", [P, 8, NCH], R1)
        St = at("s5_state", [P, 4, 2, NCH + 1], R1 + 1040)
        MinT = at("m_in_t", [P, 4, 2, CT * CG], R1 + 2088)
        Min = at("m_in", [P, 4, 2, P], R1 + 3112)
        Mtoe = at("m_toe", [P, 8, P], R1 + 4136)
        W9 = at("w9", [P, 4, 2, (CT + 1) * CG], R1 + 5160)
        dsk = at("d_skip", [P, 8], R1 + 6312)
        Gs = at("g_small", [P, 8, P], R1 + 2088)
        nv, ny, nt, rstd = (at(f"n_{k}", [P, LP], 2 * TL + i * LP) for i, k in enumerate(("v", "y", "t", "rstd")))
        sqr = at("sq_ring", [P, 2, LP], 2 * TL + 4 * LP)
        nx = at("n_x", [P, 2, LP], 2 * TL + 6 * LP)
        R2 = 4 * TL
        kbuf = at("kbuf", [P, 2, KOFF + SEQ], R2)
        Vb = at("vb", [P, NBLK + 1, 256], R2 + 2336)
        vmeta = at("vmeta", [P, 256], R2 + 4640)
        kst = at("kst", [P, NKV, KEYS], R2 + 4896)
        qst = at("qst", [P, KD, P], R2 + 6048)
        vst = at("vst", [P, 2, 256], R2 + 7072)
        ptm_sb = at("ptm_sb", [P, 4, P], R2 + 7584)
        Bx = at("b_raw", [P, 4, 2, CG], R2 + 8096)
        Cc = at("c_conj", [P, 4, 2, CG], R2 + 8224)
        gst = at("gate_stage", [P, LP], R1 + 6320)
        Craw = at("c_raw", [P, 2, P], R1 + 7364)
        XT = at("x_tok", [P, NBLK + 1, D], 0)
        OT = at("o_tok", [P, 2, D], 0)

        PA = ctx.enter_context(nc.psum_tensor("ps_a", [P, 3, 512], F32))
        PB = ctx.enter_context(nc.psum_tensor("ps_b", [P, 3, 512], F32))
        PC = ctx.enter_context(nc.psum_tensor("ps_c", [P, 2, 512], F32))
        PS = [PB[:, 0, :], PB[:, 1, :]]
        PT = [PB[:, 2, :], PC[:, 0, :]]
        PO = PC[:, 1, :]
        BK4 = [PB[:, 0, :], PB[:, 1, :], PB[:, 2, :], PC[:, 0, :]]

        def dram(name, shape):
            return nc.dram_tensor(name, shape, F32, kind="Internal").ap()

        xd = dram("x_spill", (KD, P, LP))
        gd = dram("gate_spill", (16, P, LP))
        ud = dram("u_spill", (512, CT, NCH))
        yd = dram("y_spill", (512, CT, NCH))

        def sem(name):
            return ctx.enter_context(nc.semaphore(name))

        const_loaded = sem("const_loaded")
        xtok_loaded = sem("xtok_loaded")
        w_loaded = [sem("w_loaded0"), sem("w_loaded1")]
        w_hi = sem("w_hi")
        w_split = sem("w_split")
        strip_done = sem("strip_done")
        free_a = sem("free_a")
        free_b = sem("free_b")
        init_tr = sem("init_tr")
        x_ready = sem("x_ready")
        sq_ready = sem("sq_ready")
        sq_used = sem("sq_used")
        stat_done = sem("stat_done")
        var_done = sem("var_done")
        rs0_done = sem("rs0_done")
        hx_ready = sem("hx_ready")
        hx_hi = sem("hx_hi")
        h_ready = sem("h_ready")
        mix_sq = sem("mix_sq")
        mix_acc = sem("mix_acc")
        xo_loaded = [sem("xo_loaded0"), sem("xo_loaded1")]
        x_stored = sem("x_stored")
        tab_loaded = sem("tab_loaded")
        u_copied = sem("u_copied")
        u_stored = [sem("u_stored0"), sem("u_stored1")]
        rot_ready = sem("rot_ready")
        rope_done = sem("rope_done")
        pool_init = sem("pool_init")
        v_ready = sem("v_ready")
        stage_qk = sem("stage_qk")
        scores_done = sem("scores_done")
        stt_done = sem("stt_done")
        m_ready = sem("m_ready")
        exp_done = sem("exp_done")
        p_ready = sem("p_ready")
        tr_done = sem("tr_done")
        pt_act = sem("pt_act")
        pt_dve = sem("pt_dve")
        pv_done = sem("pv_done")
        y_out = sem("y_out")
        m0_done = [sem(f"meta_{k}") for k in ("scores", "max", "exp", "p", "tr", "pt", "pv", "y")]
        g_stored = sem("g_stored")
        s5_coef = sem("s5_coef")
        s5_e = [sem(f"s5_e{i}") for i in range(6)]
        b_loaded = sem("b_loaded")
        s5_min = sem("s5_min")
        s5_w = sem("s5_w")
        s5_cc = sem("s5_cc")
        s5_pe = sem("s5_pe")
        s5_ev = sem("s5_ev")
        s5_out = sem("s5_out")
        s5_out_ev = sem("s5_out_ev")
        s5_g = sem("s5_g")
        toe_loaded = sem("toe_loaded")
        u_loaded = sem("u_loaded")
        s5_scan = sem("s5_scan")
        y_stored = sem("y_stored")
        yr_loaded = sem("yr_loaded")
        ys_hi = sem("ys_hi")
        ys_ready = sem("ys_ready")
        ge = [sem(f"gelu_{i}") for i in range(4)]
        z_ready = sem("z_ready")
        gate_loaded = [sem("gate_loaded0"), sem("gate_loaded1")]
        gate_used = sem("gate_used")
        ev_t = sem("ev_t")
        ev_f = sem("ev_f")
        ev_hi = sem("ev_hi")
        z2_ready = sem("z2_ready")
        mg_ready = sem("mg_ready")
        hid_ready = sem("hid_ready")
        relu_done = sem("relu_done")
        acc_done = sem("acc_done")
        passed = sem("passed")
        out_tr = sem("out_tr")
        out_ev = sem("out_ev")
        out_stored = [sem("out_stored0"), sem("out_stored1")]

        block = ctx.enter_context(nc.Block())
        W = dict(
            w_in=w_in.rearrange("l r c -> (l r) c"), w_oa=w_o_attn.rearrange("l r c -> (l r) c"),
            w_os=w_o_ssm.rearrange("l r c -> (l r) c"), w_glu=w_glu.rearrange("l r c -> (l r) c"),
            w_out=w_out.rearrange("l r c -> (l r) c"), w_up=w_up.rearrange("l r c -> (l r) c"),
            w_down=w_down.rearrange("l r c -> (l r) c"))

        a_pn = [a.rearrange("l (p g) n -> l (g n) p", g=2) for a in (a_re, a_im)]
        dt_v = log_dt.rearrange("l (p g) -> l g p", g=2)
        b_v = [t.rearrange("l (k p g) n c -> (l k) (g n) p c", k=NB, g=2) for t in (b_re, b_im)]
        c_v = [t.rearrange("l (k g) c n -> (l k) (g c) n", k=NB) for t in (c_re, c_im)]
        d_v = d_skip.rearrange("l (k g) c -> (l k) c g", k=NB)

        def v3(t):
            return t.rearrange("p (c w) -> p c w", c=NC3)

        def pset(s):
            return PA if a_use(s) is not None else PB

        @block.sync
        def _(sp):
            sp.dma_start(ident[:, :], ident_t).then_inc(const_loaded, 16)
            sp.dma_start(XT[0:NMETA, 0, :], meta).then_inc(xtok_loaded, 16)
            for n in range(NBLK):
                sp.dma_start(XT[:, n + 1, :], x[n * P:(n + 1) * P, :]).then_inc(xtok_loaded, 16)
            for l in range(DEPTH):
                for i in range(4):
                    sp.dma_start(gains[:, l, i, :], norms[i][l].rearrange("(k p) -> p k", p=P), allow_slow_non_contiguous=True).then_inc(const_loaded, 16)
                sp.dma_start(bglu[:, l, :], b_glu[l].rearrange("(k p) -> p k", p=P), allow_slow_non_contiguous=True).then_inc(const_loaded, 16)
                sp.dma_start(sink[:, l, :], sinks[l].partition_broadcast(P)).then_inc(const_loaded, 16)
            sp.dma_start(mask0[0:NMETA, :], mask0_t).then_inc(const_loaded, 16)

            sp.wait_ge(w_split, 1)
            sp.dma_start(WRAW[:, 0, :, :], W["w_in"][0:D, 0:P].rearrange("(k p) c -> p k c", p=P)).then_inc(w_loaded[0], 16)
            with sp.Fori(0, DEPTH) as l:
                S = l * STRIPS

                def strip(s, par, rows, row0, col0, ks):
                    sp.wait_ge(w_split, s + 1)
                    sp.sem_inc(passed, 1)
                    sp.dma_start(WRAW[:, par, 0:ks, :],
                                 rows[ds(row0, ks * P), ds(col0, P)].rearrange("(k p) c -> p k c", p=P)
                                 ).then_inc(w_loaded[par], 16)

                def tables():
                    sp.wait_ge(h_ready, l * 16 + 8)
                    sp.dma_start(cosb[:, :], cos_t).then_inc(tab_loaded, 16)
                    sp.dma_start(sinb[:, :], sin_t).then_inc(tab_loaded, 16)
                    sp.dma_start(mask_cur[:, :], mask_t[0]).then_inc(tab_loaded, 16)
                    sp.dma_start(mask_rest[:, :], mask_t[1]).then_inc(tab_loaded, 16)

                strip(S + 1, 1, W["w_in"], l * D, P, KD)
                tables()
                with sp.Fori(1, 8) as i:
                    for par in range(2):
                        strip(S + 2 * i + par, par, W["w_in"], l * D, (2 * i + par) * P, KD)

                def coef_loads(b):
                    one = lambda v: v[ds(b, 1), :, :].rearrange("o q n -> (o q) n")
                    for ri in range(2):
                        sp.dma_start(Bx[:, :, ri, :], b_v[ri][ds(b, 1), :, :, :].rearrange("o q p c -> (o q) p c")).then_inc(b_loaded, 16)
                        for dup in range(2):
                            sp.dma_start(Craw[:, ri, NS * dup:NS * dup + NS], one(c_v[ri])).then_inc(b_loaded, 16)
                    sp.dma_start(dsk[0:CG, :], one(d_v), allow_slow_non_contiguous=True).then_inc(b_loaded, 16)

                def gate_strips(i, lo, hi):
                    for j in range(lo, hi):
                        strip(S + S_G + 4 * i + j, j % 2, W["w_in"], l * D, (S_G + 4 * i + j) * P, KD)

                sp.wait_ge(x_stored, 16 * (KD + 16 * l))
                for k in range(2):
                    sp.wait_ge(u_stored[k], 16 * (2 * l + 2) + 16)
                sp.sem_inc(passed, 1)
                coef_loads(l * NB)

                def attention_loads(i, last=False):
                    b = l * NB + i
                    gate_strips(i, 0, 3)
                    sp.wait_ge(rope_done, l * 10 + 11)
                    sp.wait_ge(y_stored, 128 * b + 128)
                    sp.sem_inc(passed, 1)
                    for t in range(CT):
                        sp.dma_start(Uch[CG * t:CG * t + CG, :, :],
                                     ud[ds(i * P, P), t, :].rearrange("(g c) j -> c g j", g=8)).then_inc(u_loaded, 16)
                    gate_strips(i, 3, 4)
                    sp.wait_ge(s5_g, b + 1)
                    sp.sem_inc(passed, 1)
                    for t in range(CT):
                        sp.dma_start(Mtoe[CG * t:CG * t + CG, :, CG * t:P], Gs[0:CG, :, 0:P - CG * t]).then_inc(toe_loaded, 16)
                    if not last:
                        coef_loads(b + 1)

                with sp.Fori(0, NB - 1) as i:
                    attention_loads(i)
                attention_loads(NB - 1, last=True)
                with sp.Fori(0, 4) as i:
                    for par in range(2):
                        strip(S + S_OA + 2 * i + par, par, W["w_oa"], l * D, (2 * i + par) * P, KD)
                with sp.Fori(0, 2) as i:
                    for par in range(2):
                        strip(S + S_GLU + 2 * i + par, par, W["w_glu"], l * 512, (2 * i + par) * P, 4)
                with sp.Fori(0, 4) as i:
                    for par in range(2):
                        strip(S + S_OS + 2 * i + par, par, W["w_os"], l * 512, (2 * i + par) * P, 4)
                with sp.Fori(0, 4) as i:
                    for par in range(2):
                        strip(S + S_OUT + 2 * i + par, par, W["w_out"], l * D, (2 * i + par) * P, KD)
                with sp.Fori(0, 4) as q:
                    with sp.Fori(0, 4) as i:
                        for par in range(2):
                            strip(S + S_FF + 16 * q + 2 * i + par, par, W["w_up"], l * D,
                                  q * D + (2 * i + par) * P, KD)
                    with sp.Fori(0, 4) as i:
                        for par in range(2):
                            strip(S + S_FF + 16 * q + 8 + 2 * i + par, par, W["w_down"], l * DFF + q * D,
                                  (2 * i + par) * P, KD)
                strip(S + STRIPS, 0, W["w_in"], (1 - l) * D, 0, KD)

        @block.tensor
        def _(pe):
            pe.sem_inc(strip_done, 2)
            pe.sem_inc(sq_used, 2)
            pe.sem_inc(tr_done, 1)
            pe.wait_ge(const_loaded, 16 * 14)
            pe.wait_ge(xtok_loaded, 16 * (NBLK + 1))
            for k in range(KD):
                ps, fr = (PA, free_a) if k % 2 == 0 else (PB, free_b)
                pe.wait_ge(fr, k // 2 + 1)
                for n in range(NBLK):
                    pe.transpose(ps[:, n // 4, (n % 4) * P:(n % 4 + 1) * P], XT[:, n + 1, k * P:(k + 1) * P], ident[:, :])
                pe.transpose(ps[:, 2, 0:NMETA], XT[0:NMETA, 0, k * P:(k + 1) * P],
                             ident[0:NMETA, 0:NMETA]).then_inc(init_tr, 1)

            with pe.Fori(0, DEPTH) as l:
                S, A, B = l * STRIPS, l * A_PER + A_INIT, l * B_PER + B_INIT

                def pre_stats(a, q0):
                    pe.wait_ge(free_a, A + a + 1)
                    for k in range(KD):
                        pe.wait_ge(sq_ready, l * 16 + q0 + k + 1)
                        for c in range(NC3):
                            mm = pe.matmul(PA[:, c, 0:CW], ones[:, :], sqr[:, k % 2, c * CW:(c + 1) * CW],
                                           start=(k == 0), stop=(k == KD - 1))
                        mm.then_inc(sq_used, 1)

                def post_stats(a, n):
                    pe.wait_ge(free_a, A + a + 1)
                    pe.wait_ge(mix_acc, l * 16 + n + 1)
                    for c in range(NC3):
                        mm = pe.matmul(PA[:, c, 0:CW], ones[:, :], MT[:, 0, c * CW:(c + 1) * CW], start=True, stop=True)
                    mm.then_inc(stat_done, 1)

                def ksteps(ps, par, ks, rh, rl, k0, total, waits=None):
                    for k in ks:
                        if waits:
                            waits(k)
                        for t, (w, r) in enumerate(((WHI, rh), (WHI, rl), (WLO, rh))):
                            for c in range(NC3):
                                mm = pe.matmul(ps[:, c, 0:CW], w[:, par, k, :], r[:, k0 + k, c * CW:(c + 1) * CW],
                                               start=(k == 0 and t == 0), stop=(k == total - 1 and t == 2))
                    return mm

                def take(s_static, s, i2):
                    pe.wait_ge(w_split, S + s + 3)
                    if a_use(s_static) is not None:
                        pe.wait_ge(free_a, A + a_use(s_static) + i2 + 1)
                    else:
                        pe.wait_ge(free_b, B + b_use(s_static) + i2 + 1)

                def strips(s0, n, total, rh, rl, extra=0, waits=None):
                    with pe.Fori(0, n // 2) as i:
                        for par in range(2):
                            take(s0 + par, extra * 16 + s0 + 2 * i + par, i + extra * 8)
                            ksteps(pset(s0 + par), par, range(total), rh, rl, 0, total, waits).then_inc(strip_done, 1)

                pre_stats(A_PRE1, 0)
                strips(S_U, 14, KD, HH, HL, waits=lambda k: pe.wait_ge(h_ready, l * 16 + k + 1))
                for par in range(2):
                    take(S_V + par, S_V + par, 0)
                    ps = pset(S_V + par)
                    for n in range(NBLK + 1):
                        t0 = NMETA + n * P if n < NBLK else 0
                        dst = ps[:, n // 4, (n % 4) * P:(n % 4 + 1) * P]
                        for k in range(KD):
                            for t, (w, r) in enumerate(((WHI, HH), (WHI, HL), (WLO, HH))):
                                mm = pe.matmul(dst, r[:, k, t0:t0 + P], w[:, par, k, :],
                                               start=(k == 0 and t == 0), stop=(k == KD - 1 and t == 2))
                    mm.then_inc(strip_done, 1)

                pe.wait_ge(stage_qk, l * 9 + 1)
                pe.wait_ge(free_b, B + 8 + 1)
                pe.sem_inc(passed, 1)
                for h in range(NH):
                    kv, hb = h // 4, HD * (h % 2)
                    mm = pe.matmul(PS[h % 2][0:NMETA, (h // 2) * 16:(h // 2 + 1) * 16], QY[hb:hb + HD, h // 2, 0:NMETA],
                                   kst[hb:hb + HD, kv, 0:NMETA], start=True, stop=True)
                mm.then_inc(m0_done[0], 1)
                pe.wait_ge(m0_done[3], l + 1)
                pe.sem_inc(passed, 1)
                pflat = s_sb[:, :, :].rearrange("p a b -> p (a b)")
                for h in range(NH):
                    mm = pe.transpose(PT[0][0:NMETA, h * 16:(h + 1) * 16], pflat[0:NMETA, h * 16:(h + 1) * 16],
                                      ident[0:NMETA, 0:NMETA])
                mm.then_inc(m0_done[4], 1)
                pe.wait_ge(m0_done[5], l + 1)
                pe.sem_inc(passed, 1)
                ptm = pt_sb[:, 0, 0:2, :].rearrange("p a b -> p (a b)").rearrange("p (v j g q) -> p v g j q", v=4, j=2, g=2)
                for kv in range(NKV):
                    for g in range(2):
                        mm = pe.matmul(PO[HD * g:HD * g + HD, kv * 32:kv * 32 + 32], vmeta[0:NMETA, kv * HD:(kv + 1) * HD],
                                       ptm[0:NMETA, kv, g, :, :], start=True, stop=True)
                mm.then_inc(m0_done[6], 1)

                def scores(un, kv, n, ev=None):
                    if kv == 0:
                        pe.wait_ge(stage_qk, l * 9 + 2 + n)
                    if ev is not None:
                        pe.wait_ge(*ev)
                    for g in range(4):
                        hb = HD * (g % 2)
                        pe.wait_ge(stt_done, 4 * un + g + 1)
                        pe.matmul(PS[g % 2][:, 0:KEYS], qst[hb:hb + HD, 2 * kv + g // 2, :], kst[hb:hb + HD, kv, :],
                                  start=True, stop=True).then_inc(scores_done, 1)

                def transposes(un, ev=None):
                    pe.wait_ge(p_ready, un + 1)
                    if ev is not None:
                        pe.wait_ge(*ev)
                    for g in range(4):
                        pe.transpose(PT[0][:, g * P:(g + 1) * P], s_sb[:, g, 32:160], ident[:, :])
                        pe.transpose(PT[1][:, g * P:(g + 1) * P], s_sb[:, g, 160:288], ident[:, :])
                    pe.wait_ge(y_out, un + 1)
                    pe.transpose(PO[:, 256:384], pm_sb[:, :, :].rearrange("p a b -> p (a b)"), ident[:, :]).then_inc(tr_done, 1)

                def pv(un, kv):
                    pe.wait_ge(pt_act, un + 1)
                    pe.wait_ge(pt_dve, un + 1)
                    vc = slice(kv * HD, kv * HD + HD)
                    for hf in range(2):
                        o = PO[HD * hf:HD * hf + HD, 0:256]
                        for j in range(2):
                            pe.matmul(o, vst[:, j, vc], pt_sb[:, j, hf::2, :], start=(j == 0), stop=False)
                        mm = pe.matmul(o, vmeta[:, vc], ptm_sb[:, hf::2, :], start=False, stop=True)
                    mm.then_inc(pv_done, 1)

                def banks_free(un):
                    pe.wait_ge(stt_done, 4 * un + 6)
                    pe.wait_ge(pt_act, un)
                    pe.wait_ge(pt_dve, un)
                    pe.sem_inc(passed, 1)

                def s5_a0(b, un):
                    pe.wait_ge(b_loaded, 112 * (b + 1))
                    pe.wait_ge(stt_done, 4 * un + 6)
                    for ri in range(2):
                        mm = pe.transpose(PS[0][:, ri * P:(ri + 1) * P], Craw[:, ri, :], ident[:, :])
                    mm.then_inc(s5_pe, 1)

                def s5_a(b, un):
                    pe.wait_ge(s5_min, b + 1)
                    pe.wait_ge(s5_w, b + 1)
                    banks_free(un)
                    for p in range(4):
                        for ri in range(2):
                            i = 2 * p + ri
                            pe.transpose(PS[i // 4][:, (i % 4) * P:(i % 4 + 1) * P], MinT[:, p, ri, :], ident[:, :])
                    for g in range(8):
                        gb, p = NS * (g % 2), g // 2
                        for ri in range(2):
                            mm = pe.matmul(PT[g % 2][0:CG, p * P:(p + 1) * P], BB[gb:gb + NS, p, ri, :],
                                           W9[gb:gb + NS, p, ri, 0:P], start=(ri == 0), stop=(ri == 1))
                    mm.then_inc(s5_pe, 1)

                def s5_b(b, un):
                    pe.wait_ge(s5_ev, 3 * b + 2)
                    pe.wait_ge(u_loaded, 128 * (b + 1))
                    banks_free(un)
                    for p in range(4):
                        for g2 in range(2):
                            for ri in range(2):
                                mm = pe.matmul(BK4[p][NS * g2:NS * g2 + NS, ri * NCH:(ri + 1) * NCH],
                                               Min[:, p, ri, NS * g2:NS * g2 + NS], Uch[:, 2 * p + g2, :],
                                               start=True, stop=True)
                    mm.then_inc(s5_pe, 1)

                def s5_c(b):
                    pe.wait_ge(s5_scan, b + 1)
                    pe.wait_ge(toe_loaded, 128 * (b + 1))
                    pe.sem_inc(passed, 1)
                    for g in range(8):
                        p, gb = g // 2, NS * (g % 2)
                        o = BK4[2 * (g % 2) + p // 2][:, (p % 2) * NCH:(p % 2 + 1) * NCH]
                        pe.matmul(o, Mtoe[:, g, :], Uch[:, g, :], start=True, stop=False)
                        for ri in range(2):
                            mm = pe.matmul(o, W9[gb:gb + NS, p, ri, CG:CG + P], St[gb:gb + NS, p, ri, 0:NCH],
                                           start=False, stop=(ri == 1))
                    mm.then_inc(s5_out, 1)

                pe.wait_ge(m0_done[7], l + 1)
                pe.sem_inc(passed, 1)
                def attention(i, first=False):
                    b = l * NB + i
                    for u8 in range(8):
                        kv = u8 % NKV
                        un = l * 32 + 8 * i + u8
                        ev = {0: (s5_ev, 3 * b + 1), 3: (s5_ev, 3 * b + 2), 4: (s5_ev, 3 * b + 3)}
                        if not first:
                            ev[1] = (s5_out_ev, b)
                        scores(un, kv, 2 * i + u8 // NKV, ev.get(u8 - 1))
                        gi = u8 // 2
                        if u8 % 2 == 0:
                            pe.wait_ge(w_split, S + S_G + gi + 4 * i + 3)
                            pe.wait_ge(free_a, A + 9 + gi + 4 * i + 1)
                            ksteps(PA, gi % 2, range(0, 4), HH, HL, 0, KD)
                        else:
                            ksteps(PA, gi % 2, range(4, 8), HH, HL, 0, KD).then_inc(strip_done, 1)
                        if u8 == 0:
                            s5_a0(b, un)
                        elif u8 == 1 and not first:
                            banks_free(un)
                            s5_c(b - 1)
                        elif u8 == 3:
                            s5_a(b, un)
                        elif u8 == 4:
                            s5_b(b, un)
                        if not (first and u8 == 0):
                            pv(un - 1, (kv - 1) % NKV)
                        transposes(un, ev.get(u8) if u8 else None)

                attention(0, first=True)
                with pe.Fori(1, NB) as i:
                    attention(i)
                pv(l * 32 + 31, NKV - 1)
                s5_c(l * NB + NB - 1)
                pe.wait_ge(s5_out_ev, NB * (l + 1))
                pe.wait_ge(y_out, l * 32 + 33)
                pe.sem_inc(passed, 1)

                strips(S_OA, 8, KD, HH, HL, waits=lambda k: pe.wait_ge(ys_ready, l * KD + k + 1))
                zl = BL[:, 4:8, :]
                strips(S_GLU, 4, 4, BL, zl, waits=lambda k: pe.wait_ge(z_ready, l * 4 + k + 1))
                strips(S_OS, 8, 4, XR, XR[:, 4:8, :], waits=lambda k: pe.wait_ge(z2_ready, l * 4 + k + 1))
                strips(S_OUT, 8, KD, BH, BL, waits=lambda k: pe.wait_ge(mg_ready, l * KD + k + 1))
                post_stats(A_POST1, 8)
                pre_stats(A_PRE2, 8)

                def quarter(q):
                    strips(S_FF, 8, KD, HH, HL, extra=q, waits=lambda k: pe.wait_ge(h_ready, l * 16 + 8 + k + 1))
                    strips(S_FF + 8, 8, KD, BH, BL, extra=q,
                           waits=lambda k: pe.wait_ge(hid_ready, l * 32 + q * 8 + k + 2))

                with pe.Fori(0, 4) as q:
                    quarter(q)
                post_stats(A_POST2, 16)

            A, B = DEPTH * A_PER + A_INIT, DEPTH * B_PER + B_INIT
            pe.wait_ge(x_ready, 16 * DEPTH + 1)
            for n in range(NBLK):
                ps, fr, u0 = (PA, free_a, A) if n % 2 == 0 else (PB, free_b, B)
                pe.wait_ge(fr, u0 + n // 2 + 1)
                for k in range(KD):
                    mm = pe.transpose(ps[:, k // 4, (k % 4) * P:(k % 4 + 1) * P],
                                      X[:, k, NMETA + n * P:NMETA + (n + 1) * P], ident[:, :])
                mm.then_inc(out_tr, 1)

        @block.scalar
        def _(act):
            for k in range(2):
                act.sem_inc(u_stored[k], 16)
            act.sem_inc(g_stored, 16)

            def w_high(s, par):
                s2 = s[1]
                act.wait_ge(w_loaded[par], 16 * (s2 + 1))
                act.wait_ge(strip_done, s[0] + 1)
                act.activation(WHI[:, par, :, :], WRAW[:, par, :, :], ACT.Copy).then_inc(w_hi, 1)

            w_high((0, 0), 0)
            act.wait_ge(const_loaded, 16 * 14)
            act.activation(bgluh[:, :, :], bglu[:, :, :], ACT.Copy, scale=0.5)
            act.wait_ge(pool_init, 1)
            for k in range(KD):
                ps, fr = (PA, free_a) if k % 2 == 0 else (PB, free_b)
                act.wait_ge(init_tr, k + 1)
                act.activation(X[:, k, NMETA:L].rearrange("p (c w) -> p c w", c=2), ps[:, 0:2, :], ACT.Copy)
                act.activation(X[:, k, 0:NMETA], ps[:, 2, 0:NMETA], ACT.Copy).then_inc(fr, 1)
                act.wait_ge(fr, k // 2 + 2)
                act.drain()
                act.dma_start(xd[k], X[:, k, :]).then_inc(x_stored, 16)

            with act.Fori(0, DEPTH) as l:
                S, S2 = l * STRIPS, l * (STRIPS // 2)
                A, B = l * A_PER + A_INIT, l * B_PER + B_INIT

                def nxt(s, i):
                    w_high((S + s + 1 + 2 * i, S2 + (s + 1) // 2 + i), (s + 1) % 2)

                def freed(s):
                    return free_a if a_use(s) is not None else free_b

                def squares(q0):
                    for k in range(KD):
                        if q0 == 0:
                            act.wait_ge(x_ready, l * 16 + 1)
                        else:
                            act.wait_ge(x_ready, l * 16 + k + 2)
                        act.wait_ge(sq_used, l * 16 + q0 + k + 1)
                        act.activation(sqr[:, k % 2, :], X[:, k, :], ACT.Square).then_inc(sq_ready, 1)
                        if q0 == 8:
                            store_x(k)

                def store_x(k):
                    act.dma_start(xd[k], X[:, k, :]).then_inc(x_stored, 16)
                    if k + 2 < KD:
                        old_x(k + 2)

                def old_x(k):
                    act.dma_start(MT[:, 2 + k % 2, :], xd[k]).then_inc(xo_loaded[k % 2], 16)

                def rsqrt0(a):
                    act.wait_ge(free_a, A + a + 2)
                    act.activation(ny[:, :], nv[:, :], ACT.Ln)
                    act.drain()
                    act.activation(ny[:, :], ny[:, :], ACT.Exp, scale=-0.5).then_inc(rs0_done, 1)

                def h_high(q0):
                    for k in range(KD):
                        act.wait_ge(hx_ready, l * 16 + q0 + k + 1)
                        act.activation(HH[:, k, :], nx[:, k % 2, :], ACT.Copy).then_inc(hx_hi, 1)

                squares(0)
                rsqrt0(A_PRE1)
                h_high(0)
                with act.Fori(0, 2) as i:
                    for par in range(2):
                        nxt(S_U + par, i)
                        act.wait_ge(strip_done, S + S_U + par + 2 * i + 3)
                        act.activation(v3(ut[:, :]), pset(par)[:, :, 0:CW], ACT.Copy).then_inc(freed(par), 1)
                        act.drain()
                        act.wait_ge(u_stored[par], 16 * (2 * l + i) + 16)
                        act.activation(ust[:, par, :, :], ut[:, 0:L].rearrange("p (j t) -> p t j", t=CT),
                                       ACT.Copy).then_inc(u_copied, 1)
                        act.wait_ge(u_copied, l * 4 + 2 * i + par + 1)
                        act.dma_start(ud[ds((2 * i + par) * P, P), :, :], ust[:, par, :, :]).then_inc(u_stored[par], 16)
                act.wait_ge(s5_e[0], l + 1)
                act.activation(T2p[:, 0:16], T1p[:, 64:80], ACT.Sin)
                act.activation(T1p[:, 112:128], T1p[:, 64:80], ACT.Abs)
                act.drain()
                act.activation(T2p[:, 16:32], T1p[:, 112:128], ACT.Sin, scale=-1.0, bias=float(np.pi / 2)).then_inc(s5_e[1], 1)
                with act.Fori(0, 5) as i:
                    for par in range(2):
                        nxt(S_Q + par, i)
                        act.wait_ge(strip_done, S + S_Q + par + 2 * i + 3)
                        act.wait_ge(rope_done, l * 10 + 2 * i + par + 1)
                        for qd in range(4):
                            o, r = 32 * qd, 32 * (qd ^ 1)
                            act.activation(v3(rot[o:o + 32, :]), pset(par)[r:r + 32, :, 0:CW], ACT.Copy).then_inc(rot_ready, 1)
                act.wait_ge(pool_init, l * 5 + 6)
                for par in range(2):
                    nxt(S_V + par, 0)
                    act.wait_ge(strip_done, S + S_V + par + 3)
                    ps = pset(par)
                    act.activation(Vb[:, 1:NBLK + 1, par * P:(par + 1) * P],
                                   ps[:, 0:2, :].rearrange("p c (n w) -> p (c n) w", n=4), ACT.Copy)
                    for g in range(4):
                        mm = act.activation(vmeta[32 * g:32 * g + NMETA, par * P:(par + 1) * P], ps[0:NMETA, 2, 0:P], ACT.Copy)
                    mm.then_inc(freed(par), 1)
                act.wait_ge(rope_done, l * 10 + 11)
                for sh in range(2):
                    for dh in range(2):
                        mm = act.activation(kst[HD * dh:HD * dh + HD, sh::2, 0:NMETA],
                                            kbuf[HD * sh:HD * sh + HD, :, 0:NMETA], ACT.Copy)
                mm.then_inc(stage_qk, 1)

                def stage(n):
                    act.activation(qst[:, :, :], QY[:, :, ds(NMETA + n * P, P)], ACT.Copy)
                    for sh in range(2):
                        for dh in range(2):
                            mm = act.activation(kst[HD * dh:HD * dh + HD, sh::2, 32:KEYS],
                                                kbuf[HD * sh:HD * sh + HD, :, ds(NMETA + n * P, 2 * P)], ACT.Copy)
                    mm.then_inc(stage_qk, 1)

                pflat = s_sb[:, :, :].rearrange("p a b -> p (a b)")
                act.wait_ge(m0_done[1], l + 1)
                act.activation(pflat[0:NMETA, 0:256], pflat[0:NMETA, 0:256], ACT.Exp)
                act.activation(stat[0:NMETA, 5, :], stat[0:NMETA, 4, :], ACT.Exp).then_inc(m0_done[2], 1)
                act.wait_ge(m0_done[4], l + 1)
                act.activation(pt_sb[0:NMETA, 0, 0:2, :], PT[0][0:NMETA, 0:256].rearrange("p (a b) -> p a b", a=2),
                               ACT.Copy).then_inc(m0_done[5], 1)
                act.wait_ge(m0_done[6], l + 1)

                def s5_outputs(i):
                    b = l * NB + i
                    act.wait_ge(s5_out, b + 1)
                    for p in (2, 3, 0, 1):
                        g0 = 4 * (p % 2) + p // 2
                        mm = act.activation(Uch[:, g0:g0 + 3:2, :], BK4[p][:, 0:2 * NCH].rearrange(
                            "p (a b) -> p a b", a=2), ACT.Copy)
                    mm.then_inc(s5_out_ev, 1)
                    act.wait_ge(s5_out_ev, b + 1)
                    for t in range(CT):
                        act.dma_start(yd[ds(i * P, P), t, :].rearrange("(g c) j -> c g j", g=8),
                                      Uch[CG * t:CG * t + CG, :, :]).then_inc(y_stored, 16)

                def attention(i, first=False, last=False):
                    b = l * NB + i
                    for u8 in range(8):
                        kv = u8 % NKV
                        un = l * 32 + 8 * i + u8
                        act.wait_ge(m_ready, un + 1)
                        for g in range(4):
                            act.activation(s_sb[:, g, :], s_sb[:, g, :], ACT.Exp, bias=stat[:, 2, g:g + 1],
                                           accum_out=stat[:, 3, g:g + 1])
                        act.activation(stat[:, 5, 0:4], stat[:, 4, 0:4], ACT.Exp).then_inc(exp_done, 1)
                        if kv == NKV - 1 and not (last and u8 == 7):
                            act.wait_ge(scores_done, 4 * un + 4)
                            stage(2 * i + (u8 + 1) // NKV)
                        gi = u8 // 2
                        if u8 % 2 == 0:
                            w_high((S + S_G + gi + 4 * i + 1, S2 + S_G // 2 + (gi + 1) // 2 + 2 * i), (gi + 1) % 2)
                        else:
                            act.wait_ge(strip_done, S + S_G + gi + 4 * i + 3)
                            act.wait_ge(g_stored, 16 * (l * 16 + 4 * i + gi) + 16)
                            act.activation(v3(gst[:, :]), PA[:, :, 0:CW], ACT.Tanh, scale=0.5).then_inc(free_a, 1)
                            act.wait_ge(free_a, A + 9 + gi + 4 * i + 2)
                            act.dma_start(gd[ds(4 * i + gi, 1), :, :].rearrange("o p w -> p (o w)"), gst[:, :]).then_inc(g_stored, 16)
                        if u8 == 0:
                            act.wait_ge(s5_pe, 3 * b + 1)
                            for ri in range(2):
                                for g2 in range(2):
                                    src = PS[0][NS * g2:NS * g2 + NS, ri * P:(ri + 1) * P].rearrange(
                                        "q (p g c) -> q p g c", p=4, g=2)[:, :, g2, :]
                                    mm = act.activation(Cc[NS * g2:NS * g2 + NS, :, ri, :], src, ACT.Copy,
                                                        scale=1.0 - 2.0 * ri)
                            mm.then_inc(s5_ev, 1)
                        elif u8 == 1 and not first:
                            s5_outputs(i - 1)
                        elif u8 == 3:
                            act.wait_ge(s5_pe, 3 * b + 2)
                            for hf in range(2):
                                act.activation(Gs[0:CG, hf::2, :],
                                               PT[hf][0:CG, :].rearrange("p (a b) -> p a b", a=4), ACT.Copy)
                            act.activation(Min[:, :, :, :].rearrange("q p r w -> q (p r w)").rearrange("q (c w) -> q c w", c=2),
                                           PB[:, 0:2, :], ACT.Copy).then_inc(s5_ev, 1)
                        elif u8 == 4:
                            act.wait_ge(s5_pe, 3 * b + 3)
                            for p in (2, 3, 0, 1):
                                mm = act.activation(St[:, p, :, 1:NCH + 1], BK4[p][:, 0:2 * NCH].rearrange(
                                    "p (a b) -> p a b", a=2), ACT.Copy)
                            mm.then_inc(s5_ev, 1)
                        if kv == 0:
                            act.wait_ge(pv_done, un + 1)
                            act.activation(vst[:, :, :], Vb[:, ds(2 * i + u8 // 4, 2), :], ACT.Copy)
                        act.wait_ge(tr_done, un + 2)
                        act.activation(pt_sb[:, 0, :, :], PT[0].rearrange("p (a b) -> p a b", a=4), ACT.Copy)
                        for g in range(4):
                            mm = act.activation(ptm_sb[32 * g:32 * g + 32, g, :], PO[32 * g:32 * g + 32, 256:384], ACT.Copy)
                        mm.then_inc(pt_act, 1)

                stage(0)
                attention(0, first=True)
                with act.Fori(1, NB - 1) as i:
                    attention(i)
                attention(NB - 1, last=True)
                s5_outputs(NB - 1)

                act.wait_ge(strip_done, S + 31 + 3)
                act.wait_ge(y_out, l * 32 + 33)
                act.sem_inc(passed, 1)
                with act.Fori(0, KD) as k:
                    act.activation(HH[:, ds(k, 1), :], QY[:, ds(k, 1), :], ACT.Copy).then_inc(ys_hi, 1)
                with act.Fori(0, 4) as i:
                    for par in range(2):
                        nxt(S_OA + par, i)
                    act.wait_ge(yr_loaded, 64 * (l + 1))
                    act.activation(MT[:, 2, 0:L].rearrange("p (j t) -> p j t", t=CT),
                                   X[:, ds(i, 1), 0:L].rearrange("p o (t j) -> p (o j) t", t=CT), ACT.Square).then_inc(ge[0], 1)
                    act.wait_ge(ge[2], l * 4 + i + 1)
                    act.activation(MT[:, 3, 0:L], MT[:, 2, 0:L], ACT.Tanh, scale=0.7978845608028654).then_inc(ge[3], 1)
                    act.wait_ge(ev_f, l * EVF + i + 1)
                    act.activation(BL[:, ds(i, 1), :], X[:, ds(4 + i, 1), :], ACT.Copy, scale=0.5).then_inc(ev_hi, 1)
                with act.Fori(0, 2) as i:
                    for par in range(2):
                        nxt(S_GLU + par, i)
                        act.wait_ge(strip_done, S + S_GLU + par + 2 * i + 3)
                        act.activation(v3(MT[:, 2, :]), pset(par)[:, :, 0:CW], ACT.Tanh, scale=0.5,
                                       bias=bgluh[:, ds(l, 1), ds(2 * i + par, 1)].rearrange("p a b -> p (a b)")
                                       ).then_inc(freed(par), 1)
                        act.wait_ge(ev_f, l * EVF + 4 + 2 * i + par + 1)
                        act.activation(XR[:, ds(2 * i + par, 1), :], MT[:, 3:4, :], ACT.Copy, scale=0.25).then_inc(ev_hi, 1)
                with act.Fori(0, 4) as i:
                    for par in range(2):
                        nxt(S_OS + par, i)
                        act.wait_ge(ev_f, l * EVF + 8 + 2 * i + par + 1)
                        act.activation(BH[:, ds(2 * i + par, 1), :], MT[:, 3:4, :], ACT.Copy, scale=0.5).then_inc(ev_hi, 1)
                act.wait_ge(mg_ready, l * KD + KD)
                act.sem_inc(passed, 1)
                with act.Fori(0, 4) as i:
                    for par in range(2):
                        nxt(S_OUT + par, i)
                        act.wait_ge(strip_done, S + S_OUT + par + 2 * i + 3)
                        act.wait_ge(mix_acc, l * 16 + 2 * i + par + 1)
                        act.activation(v3(MT[:, 1, :]), pset(par)[:, :, 0:CW], ACT.Square).then_inc(mix_sq, 1)
                        act.activation(X[:, ds(2 * i + par, 1), :].rearrange("p o (c w) -> p (o c) w", c=NC3),
                                       pset(par)[:, :, 0:CW], ACT.Copy).then_inc(freed(par), 1)
                act.wait_ge(x_stored, 16 * (KD + 16 * l))
                for k in range(2):
                    old_x(k)
                rsqrt0(A_POST1)
                squares(8)
                rsqrt0(A_PRE2)
                h_high(8)

                def mlp(q, last):
                    with act.Fori(0, 4) as i:
                        for par in range(2):
                            nxt(S_FF + par, i + 8 * q)
                            act.wait_ge(strip_done, S + S_FF + par + 2 * i + 16 * q + 3)
                            act.activation(v3(MT[:, 2, :]), pset(par)[:, :, 0:CW], ACT.Relu).then_inc(freed(par), 1)
                            act.drain()
                            act.wait_ge(hid_ready, l * 32 + q * 8 + 2 * i + par + 1)
                            act.activation(MT[:, 3, :], MT[:, 2, :], ACT.Square)
                            act.drain()
                            act.activation(BH[:, ds(2 * i + par, 1), :], MT[:, 3:4, :], ACT.Copy).then_inc(ev_hi, 1)
                    with act.Fori(0, 4) as i:
                        for par in range(2):
                            nxt(S_FF + 8 + par, i + 8 * q)
                            if last:
                                t = 2 * i + par
                                if par == 0:
                                    act.wait_ge(free_a, A + a_use(S_FF + 8) + 8 * q + i + 2)
                                else:
                                    act.wait_ge(free_b, B + b_use(S_FF + 9) + 8 * q + i + 2)
                                act.wait_ge(mix_acc, l * 16 + 8 + t + 1)
                                act.activation(MT[:, 1:2, :], X[:, ds(t, 1), :], ACT.Square).then_inc(mix_sq, 1)

                with act.Fori(0, 3) as q:
                    mlp(q, False)
                mlp(3, True)
                act.wait_ge(x_stored, 16 * (2 * KD + 16 * l))
                act.wait_ge(hid_ready, l * 32 + 33)
                for k in range(2):
                    old_x(k)
                rsqrt0(A_POST2)
                for k in range(KD):
                    act.wait_ge(x_ready, l * 16 + 8 + k + 2)
                    store_x(k)

            for n in range(NBLK):
                act.wait_ge(out_tr, n + 1)
                if n >= 2:
                    act.wait_ge(out_stored[n % 2], 16 * (n // 2))
                ps, fr, u0 = (PA, free_a, DEPTH * A_PER + A_INIT) if n % 2 == 0 else (PB, free_b, DEPTH * B_PER + B_INIT)
                act.activation(OT[:, n % 2, :].rearrange("p (c w) -> p c w", c=2), ps[:, 0:2, :], ACT.Copy).then_inc(fr, 1)
                act.wait_ge(fr, u0 + n // 2 + 2)
                act.dma_start(out[n * P:(n + 1) * P, :], OT[:, n % 2, :]).then_inc(out_stored[n % 2], 16)
            for k in range(2):
                act.wait_ge(out_stored[k], 16 * (NBLK // 2))
            act.wait_ge(x_stored, 16 * (KD + 16 * DEPTH))
            act.wait_ge(g_stored, 16 * (16 * DEPTH) + 16)
            act.wait_ge(y_stored, 128 * NB * DEPTH + 128)
            for k in range(2):
                act.wait_ge(u_stored[k], 16 * 2 * DEPTH + 16)

        @block.vector
        def _(dve):
            dve.sem_inc(w_split, 2)
            dve.sem_inc(free_a, 1)
            dve.sem_inc(free_b, 1)
            dve.sem_inc(x_ready, 1)
            dve.sem_inc(rope_done, 1)
            dve.sem_inc(stt_done, 2)
            dve.sem_inc(y_out, 1)
            dve.sem_inc(hid_ready, 1)
            dve.sem_inc(pv_done, 1)

            def w_low(s, par):
                dve.wait_ge(w_hi, s + 1)
                dve.tensor_tensor(WLO[:, par, :, :], WRAW[:, par, :, :], WHI[:, par, :, :].bitcast(F32),
                                  ALU.subtract).then_inc(w_split, 1)

            def split_low(lo, src, hi, scale, done):
                dve.scalar_tensor_tensor(out=lo, in0=src, scalar=scale, in1=hi.bitcast(F32), op0=ALU.mult,
                                         op1=ALU.subtract).then_inc(done, 1)

            w_low(0, 0)
            dve.wait_ge(const_loaded, 16 * 14)
            with dve.Fori(0, DEPTH) as l:
                S = l * STRIPS
                A, B = l * A_PER + A_INIT, l * B_PER + B_INIT

                def freed(s):
                    return free_a if a_use(s) is not None else free_b

                def rsqrt(r):
                    dve.tensor_scalar(v3(nv[:, :]), PA[:, :, 0:CW], 1.0 / D, EPS, ALU.mult, ALU.add).then_inc(free_a, 1)
                    dve.wait_ge(rs0_done, l * 4 + r + 1)
                    dve.scalar_tensor_tensor(out=nt[:, :], in0=nv[:, :], scalar=-0.5, in1=ny[:, :], op0=ALU.mult, op1=ALU.mult)
                    dve.drain()
                    dve.tensor_tensor(nt[:, :], nt[:, :], ny[:, :], ALU.mult)
                    dve.drain()
                    dve.scalar_tensor_tensor(out=rstd[:, :], in0=nt[:, :], scalar=1.5, in1=ny[:, :], op0=ALU.add, op1=ALU.mult)
                    dve.drain()

                def gain(i, k):
                    return gains[:, ds(l, 1), i, k:k + 1].rearrange("p a b -> p (a b)")

                def pre_norm(q0, gi, r):
                    dve.wait_ge(sq_used, l * 16 + q0 + KD + 2)
                    rsqrt(r)
                    for k in range(KD + 1):
                        if k > 1:
                            dve.drain()
                        if k < KD:
                            dve.scalar_tensor_tensor(out=nx[:, k % 2, :], in0=X[:, k, :], scalar=gain(gi, k), in1=rstd[:, :],
                                                     op0=ALU.mult, op1=ALU.mult).then_inc(hx_ready, 1)
                        if k > 0:
                            dve.wait_ge(hx_hi, l * 16 + q0 + k)
                            split_low(HL[:, k - 1, :], nx[:, (k - 1) % 2, :], HH[:, k - 1, :], 1.0, h_ready)

                def post_norm(j, gi, r):
                    dve.wait_ge(stat_done, l * 2 + j + 1)
                    rsqrt(r)
                    for k in range(KD):
                        dve.scalar_tensor_tensor(out=nx[:, k % 2, :], in0=X[:, k, :], scalar=gain(gi, k), in1=rstd[:, :],
                                                 op0=ALU.mult, op1=ALU.mult)
                        dve.drain()
                        dve.wait_ge(xo_loaded[k % 2], 16 * (l * 8 + j * 4 + k // 2 + 1))
                        dve.tensor_tensor(X[:, k, :], nx[:, k % 2, :], MT[:, 2 + k % 2, :], ALU.add).then_inc(x_ready, 1)

                pre_norm(0, 0, 0)
                with dve.Fori(0, 2) as i:
                    for par in range(2):
                        w_low(S + S_U + par + 1 + 2 * i, (par + 1) % 2)
                dve.wait_ge(tab_loaded, 64 * (l + 1))
                dve.sem_inc(passed, 1)

                def rope(par, i, s0, tile, dst):
                    w_low(S + s0 + par + 1 + 2 * i, (par + 1) % 2)
                    dve.drain()
                    dve.wait_ge(rot_ready, 4 * (l * 10 + tile + 1))
                    dve.tensor_tensor(v3(rt1[:, :]), pset(par)[:, :, 0:CW], v3(cosb[:, :]), ALU.mult).then_inc(freed(par), 1)
                    dve.tensor_tensor(rt2[:, :], rot[:, :], sinb[:, :], ALU.mult)
                    dve.drain()
                    for o, c0, c1 in dst:
                        mm = dve.tensor_tensor(o, rt1[:, c0:c1], rt2[:, c0:c1], ALU.add)
                    mm.then_inc(rope_done, 1)

                with dve.Fori(0, 4) as i:
                    for par in range(2):
                        rope(par, i, S_Q, 2 * i + par, [(QY[:, ds(2 * i + par, 1), :].rearrange("p o w -> p (o w)"), 0, LP)])
                dve.wait_ge(x_stored, 16 * (KD + 16 * l))
                for par in range(2):
                    rope(par, 0, S_K, 8 + par, [(kbuf[:, par, 0:NMETA], 0, NMETA), (kbuf[:, par, KOFF:], NMETA, L)])
                for par in range(2):
                    w_low(S + S_V + par + 1, (par + 1) % 2)

                pflat = s_sb[0:NMETA, :, :].rearrange("p a b -> p (a b)")[:, 0:256].rearrange("p (h k) -> p h k", h=NH)
                st0 = [stat[0:NMETA, r, :] for r in range(6)]
                sk0 = sink[0:NMETA, ds(l, 1), :].rearrange("p a b -> p (a b)")
                dve.wait_ge(m0_done[0], l + 1)
                for e in range(2):
                    dve.scalar_tensor_tensor(out=pflat[:, e::2, :], in0=PS[e][0:NMETA, 0:P].rearrange("p (h k) -> p h k", h=NH // 2),
                                             scalar=SCALE, in1=mask0[0:NMETA, :].unsqueeze(1).to_broadcast([NMETA, NH // 2, NMETA]),
                                             op0=ALU.mult, op1=ALU.add)
                dve.drain()
                dve.tensor_reduce(st0[0], pflat, AX.X, ALU.max)
                dve.drain()
                dve.tensor_tensor(st0[1], st0[0], sk0, ALU.max)
                dve.drain()
                dve.tensor_tensor(pflat, pflat, st0[1].unsqueeze(2).to_broadcast([NMETA, NH, NMETA]), ALU.subtract)
                dve.tensor_tensor(st0[4], sk0, st0[1], ALU.subtract).then_inc(m0_done[1], 1)
                dve.wait_ge(m0_done[2], l + 1)
                dve.tensor_reduce(st0[3], pflat, AX.X, ALU.add)
                dve.drain()
                dve.tensor_tensor(st0[0], st0[3], st0[5], ALU.add)
                dve.drain()
                dve.reciprocal(st0[1], st0[0])
                dve.drain()
                dve.tensor_tensor(pflat, pflat, st0[1].unsqueeze(2).to_broadcast([NMETA, NH, NMETA]), ALU.mult).then_inc(m0_done[3], 1)
                dve.wait_ge(m0_done[6], l + 1)
                dve.tensor_copy(QY[:, :, 0:NMETA], PO[:, 0:P].rearrange("p (t q) -> p t q", t=KD)).then_inc(m0_done[7], 1)

                def y_store(un, kv, n):
                    dve.wait_ge(pv_done, un + 2)
                    dve.tensor_copy(QY[:, 2 * kv:2 * kv + 2, ds(NMETA + n * P, P)],
                                    PO[:, 0:256].rearrange("p (a b) -> p a b", a=2)).then_inc(y_out, 1)

                def attention(i, first=False):
                    for u8 in range(8):
                        kv = u8 % NKV
                        un = l * 32 + 8 * i + u8
                        mask = mask_cur if u8 < 4 else mask_rest
                        dve.wait_ge(tr_done, un + 1)
                        for g in range(4):
                            dve.wait_ge(scores_done, 4 * un + g + 1)
                            dve.scalar_tensor_tensor(out=s_sb[:, g, :], in0=PS[g % 2][:, 0:KEYS], scalar=SCALE,
                                                     in1=mask[:, :], op0=ALU.mult, op1=ALU.add).then_inc(stt_done, 1)
                        dve.drain()
                        dve.tensor_reduce(stat[:, 0, 0:4], s_sb[:, :, :], AX.X, ALU.max)
                        dve.drain()
                        sk = sink[:, ds(l, 1), 4 * kv:4 * kv + 4].rearrange("p a b -> p (a b)")
                        dve.tensor_tensor(stat[:, 1, 0:4], stat[:, 0, 0:4], sk, ALU.max)
                        dve.drain()
                        dve.tensor_scalar(stat[:, 2, 0:4], stat[:, 1, 0:4], -1.0, None, ALU.mult)
                        dve.tensor_tensor(stat[:, 4, 0:4], sk, stat[:, 1, 0:4], ALU.subtract).then_inc(m_ready, 1)
                        if u8 % 2 == 1:
                            gi = u8 // 2
                            w_low(S + S_G + gi + 4 * i + 1, (gi + 1) % 2)
                        if u8 == 3:
                            dve.tensor_copy(mask_cur[:, :], mask_rest[:, :])
                        dve.wait_ge(exp_done, un + 1)
                        dve.tensor_tensor(stat[:, 0, 0:4], stat[:, 3, 0:4], stat[:, 5, 0:4], ALU.add)
                        dve.drain()
                        dve.reciprocal(stat[:, 1, 0:4], stat[:, 0, 0:4])
                        dve.drain()
                        dve.tensor_tensor(pm_sb[:, :, :], s_sb[:, :, 0:32],
                                          stat[:, 1, 0:4].unsqueeze(2).to_broadcast([P, 4, 32]), ALU.mult)
                        for g in range(4):
                            mm = dve.tensor_scalar(s_sb[:, g, 32:KEYS], s_sb[:, g, 32:KEYS], stat[:, 1, g:g + 1], None, ALU.mult)
                        mm.then_inc(p_ready, 1)
                        if not (first and u8 == 0):
                            y_store(un - 1, (kv - 1) % NKV, 2 * i + (u8 - 1) // NKV)
                        dve.wait_ge(tr_done, un + 2)
                        dve.tensor_copy(pt_sb[:, 1, :, :], PT[1].rearrange("p (a b) -> p a b", a=4)).then_inc(pt_dve, 1)

                attention(0, first=True)
                with dve.Fori(1, NB) as i:
                    attention(i)
                y_store(l * 32 + 31, NKV - 1, NBLK - 1)

                with dve.Fori(0, KD) as k:
                    dve.wait_ge(ys_hi, l * KD + k + 1)
                    split_low(HL[:, ds(k, 1), :], QY[:, ds(k, 1), :], HH[:, ds(k, 1), :], 1.0, ys_ready)
                dve.memset(X[:, 4:8, L:LP], 0.0)
                with dve.Fori(0, 4) as i:
                    for par in range(2):
                        w_low(S + S_OA + par + 1 + 2 * i, (par + 1) % 2)
                        t = 2 * i + par
                        dve.wait_ge(strip_done, S + S_OA + t + 3)
                        dve.wait_ge(gate_loaded[par], 16 * (l * 8 + i + 1))
                        dve.scalar_tensor_tensor(out=QY[:, ds(t, 1), :].rearrange("p o (c w) -> p (o c) w", c=NC3),
                                                 in0=v3(MT[:, par, :]), scalar=1.0, in1=pset(par)[:, :, 0:CW],
                                                 op0=ALU.add, op1=ALU.mult).then_inc(freed(par), 1)
                    dve.wait_ge(yr_loaded, 64 * (l + 1))
                    yr = X[:, ds(i, 1), 0:L].rearrange("p o (t j) -> p (o j) t", t=CT)
                    xz = X[:, ds(4 + i, 1), 0:L].rearrange("p o (j t) -> p (o j) t", t=CT)
                    tk = lambda t: t.rearrange("p (j t) -> p j t", t=CT)
                    dve.wait_ge(ge[0], l * 4 + i + 1)
                    dve.tensor_scalar(MT[:, 2, 0:L], MT[:, 2, 0:L], 0.044715, 1.0, ALU.mult, ALU.add)
                    dve.drain()
                    dve.tensor_tensor(tk(MT[:, 2, 0:L]), tk(MT[:, 2, 0:L]), yr, ALU.mult).then_inc(ge[2], 1)
                    dve.wait_ge(ge[3], l * 4 + i + 1)
                    dve.scalar_tensor_tensor(out=xz, in0=tk(MT[:, 3, 0:L]), scalar=1.0, in1=yr,
                                             op0=ALU.add, op1=ALU.mult).then_inc(ev_f, 1)
                    dve.wait_ge(ev_hi, l * EVH + i + 1)
                    split_low(BL[:, ds(4 + i, 1), :], X[:, ds(4 + i, 1), :], BL[:, ds(i, 1), :], 0.5, z_ready)
                with dve.Fori(0, 2) as i:
                    for par in range(2):
                        k = 2 * i + par
                        w_low(S + S_GLU + par + 1 + 2 * i, (par + 1) % 2)
                        dve.drain()
                        if par == 0:
                            dve.wait_ge(free_a, A + a_use(S_GLU) + i + 2)
                        else:
                            dve.wait_ge(free_b, B + b_use(S_GLU + 1) + i + 2)
                        dve.scalar_tensor_tensor(out=MT[:, 3:4, :], in0=MT[:, 2:3, :], scalar=1.0, in1=X[:, ds(4 + k, 1), :],
                                                 op0=ALU.add, op1=ALU.mult).then_inc(ev_f, 1)
                        dve.wait_ge(ev_hi, l * EVH + 4 + k + 1)
                        split_low(XR[:, ds(4 + k, 1), :], MT[:, 3:4, :], XR[:, ds(k, 1), :], 0.25, z2_ready)
                with dve.Fori(0, 4) as i:
                    for par in range(2):
                        t = 2 * i + par
                        w_low(S + S_OS + par + 1 + 2 * i, (par + 1) % 2)
                        dve.wait_ge(strip_done, S + S_OS + t + 3)
                        dve.wait_ge(gate_loaded[par], 16 * (l * 8 + 4 + i + 1))
                        dve.scalar_tensor_tensor(out=v3(MT[:, 2, :]), in0=v3(MT[:, par, :]), scalar=1.0,
                                                 in1=pset(par)[:, :, 0:CW], op0=ALU.add, op1=ALU.mult).then_inc(freed(par), 1)
                        dve.drain()
                        dve.tensor_tensor(MT[:, 3:4, :], MT[:, 2:3, :], QY[:, ds(t, 1), :], ALU.add).then_inc(ev_f, 1)
                        dve.wait_ge(ev_hi, l * EVH + 8 + t + 1)
                        split_low(BL[:, ds(t, 1), :], MT[:, 3:4, :], BH[:, ds(t, 1), :], 0.5, mg_ready)
                with dve.Fori(0, 4) as i:
                    for par in range(2):
                        w_low(S + S_OUT + par + 1 + 2 * i, (par + 1) % 2)
                post_norm(0, 1, 1)
                pre_norm(8, 2, 2)

                with dve.Fori(0, 4) as q:
                    with dve.Fori(0, 4) as i:
                        for par in range(2):
                            t = 2 * i + par
                            w_low(S + S_FF + par + 1 + 2 * i + 16 * q, (par + 1) % 2)
                            dve.wait_ge(ev_hi, l * EVH + 16 + q * 8 + t + 1)
                            split_low(BL[:, ds(t, 1), :], MT[:, 3:4, :], BH[:, ds(t, 1), :], 1.0, hid_ready)
                    dve.wait_ge(acc_done, l + 1)
                    dve.sem_inc(passed, 1)
                    with dve.Fori(0, 4) as i:
                        for par in range(2):
                            t = 2 * i + par
                            w_low(S + S_FF + 8 + par + 1 + 2 * i + 16 * q, (par + 1) % 2)
                            dve.wait_ge(strip_done, S + S_FF + 8 + t + 16 * q + 3)
                            xt = X[:, ds(t, 1), :].rearrange("p o (c w) -> p (o c) w", c=NC3)
                            dve.tensor_tensor(xt, xt, pset(par)[:, :, 0:CW], ALU.add).then_inc(freed(par), 1)
                post_norm(1, 3, 3)

        @block.gpsimd
        def _(pool):
            def await_(s, v):
                pool.wait_ge(s, v)
                pool.sem_inc(passed, 1)

            pool.sem_inc(mix_acc, 1)
            pool.sem_inc(y_stored, 128)
            pool.memset(ones[:, :], 1.0)
            pool.memset(X[:, :, L:LP], 0.0)
            pool.drain()
            pool.sem_inc(pool_init, 1)
            def tt(o, a, b, op):
                return pool.tensor_tensor(o, a, b, op)

            def cmul(o, x, re_b, im_b, t1, t2, op=ALU.subtract):
                tt(t1, x, re_b, ALU.mult)
                tt(t2, x, im_b, ALU.mult)
                pool.drain()
                return tt(o, t1, t2[:, :, ::-1] if len(t2.shape) == 3 else t2[:, :, ::-1, :], op)

            with pool.Fori(0, DEPTH) as l:
                await_(h_ready, l * 16 + 8)
                await_(x_stored, 16 * (KD + 16 * l))
                pool.memset(kbuf[:, :, NMETA:KOFF], 0.0).then_inc(pool_init, 1)
                pool.memset(kst[:, :, :], 0.0).then_inc(pool_init, 1)
                pool.memset(Vb[:, 0, :], 0.0).then_inc(pool_init, 1)
                pool.memset(vmeta[:, :], 0.0).then_inc(pool_init, 1)
                pool.memset(ptm_sb[:, :, :], 0.0).then_inc(pool_init, 1)
                c16 = lambda t, i: t[:, 16 * i:16 * i + 16]
                are, aim, ldt, er, th, kk, u1, u2 = (c16(T1p, i) for i in range(8))
                sn, cs, mag, inv, nr, v1, v2, v3_ = (c16(T2p, i) for i in range(8))
                for t, v in ((are, a_pn[0]), (aim, a_pn[1])):
                    pool.dma_start(t, v[ds(l, 1), :, :].rearrange("o q p -> (o q) p"), allow_slow_non_contiguous=True).then_inc(s5_coef, 16)
                for g2 in range(2):
                    pool.dma_start(ldt[NS * g2:NS * g2 + NS, :], dt_v[ds(l, 1), g2, :].to_broadcast([NS, NP]), allow_slow_non_contiguous=True).then_inc(s5_coef, 16)
                await_(s5_coef, 64 * (l + 1))
                pool.memset(u1, float(np.e))
                pool.drain()
                tt(u2, u1, ldt, ALU.pow)
                pool.drain()
                tt(er, are, u2, ALU.mult)
                pool.drain()
                tt(th, aim, u2, ALU.mult)
                pool.drain()
                tt(mag, u1, er, ALU.pow)
                pool.drain()
                pool.tensor_scalar(kk, th, 1.0 / (2 * np.pi), 12582912.0, ALU.mult, ALU.add)
                pool.drain()
                pool.tensor_scalar(kk, kk, -12582912.0, None, ALU.add)
                pool.drain()
                for c in (6.28125, 0.0019340515136718750, 1.2556660464e-06):
                    pool.tensor_scalar(u2, kk, -c, None, ALU.mult)
                    pool.drain()
                    tt(th, th, u2, ALU.add)
                    pool.drain()
                pool.tensor_scalar(th, th, 3.1415925, -3.1415925, ALU.min, ALU.max)
                pool.drain()
                pool.sem_inc(s5_e[0], 1)
                await_(s5_e[1], l + 1)
                A1, A1s = PW[:, 1, :, :], PWs[:, 1, :, :]
                tt(A1[:, :, 0], mag, cs, ALU.mult)
                pool.drain()
                tt(A1[:, :, 1], mag, sn, ALU.mult)
                pool.drain()
                pool.memset(PW[:, 0, :, 0], 1.0)
                pool.drain()
                pool.memset(PW[:, 0, :, 1], 0.0)
                pool.drain()

                def partners(dst, src, lo, hi):
                    pool.tensor_scalar(dst[:, lo:hi, :, 0], src[:, lo:hi, :, 1], -1.0, 0.0, ALU.mult, ALU.add)
                    pool.drain()
                    pool.tensor_scalar(dst[:, lo:hi, :, 1], src[:, lo:hi, :, 1], 1.0, 0.0, ALU.mult, ALU.add)
                    pool.drain()

                q1 = T1p[:, 64:96].rearrange("p (a b) -> p a b", b=2)
                q2 = T1p[:, 96:128].rearrange("p (a b) -> p a b", b=2)
                partners(PWs, PW, 0, 2)
                re1 = PW[:, 1, :, 0:1].to_broadcast([P, NP, 2])
                for t in range(2, CT + 1):
                    cmul(PW[:, t, :, :], PW[:, t - 1, :, :], re1, A1s, q1, q2)
                    pool.drain()
                partners(PWs, PW, 2, CT + 1)
                tt(P8[:, 1, :, :], PW[:, CT, :, :], PW[:, 0, :, 0:1].to_broadcast([P, NP, 2]), ALU.mult)
                pool.drain()
                partners(P8s, P8, 1, 2)
                re8 = P8[:, 1, :, 0:1].to_broadcast([P, NP, 2])
                for t in range(2, RUN + 1):
                    cmul(P8[:, t, :, :], P8[:, t - 1, :, :], re8, P8s[:, 1, :, :], q1, q2)
                    pool.drain()
                partners(P8s, P8, 2, RUN + 1)
                pool.tensor_scalar(nr, A1[:, :, 0], -1.0, None, ALU.add)
                pool.drain()
                tt(v1, are, are, ALU.mult)
                pool.drain()
                tt(v2, aim, aim, ALU.mult)
                pool.drain()
                tt(v1, v1, v2, ALU.add)
                pool.drain()
                pool.memset(v2, -1.0)
                pool.drain()
                tt(inv, v1, v2, ALU.pow)
                pool.drain()
                tt(v1, nr, are, ALU.mult)
                pool.drain()
                tt(v2, A1[:, :, 1], aim, ALU.mult)
                pool.drain()
                tt(v1, v1, v2, ALU.add)
                pool.drain()
                tt(v2, nr, aim, ALU.mult)
                pool.drain()
                tt(v3_, A1[:, :, 1], are, ALU.mult)
                pool.drain()
                tt(v3_, v3_, v2, ALU.subtract)
                pool.drain()
                tt(FB[:, :, 0], v1, inv, ALU.mult)
                pool.drain()
                tt(FB[:, :, 1], v3_, inv, ALU.mult)
                pool.drain()
                pool.tensor_scalar(FBs[:, :, 0], FB[:, :, 1], -1.0, 0.0, ALU.mult, ALU.add)
                pool.drain()
                pool.tensor_scalar(FBs[:, :, 1], FB[:, :, 1], 1.0, 0.0, ALU.mult, ALU.add)
                pool.drain()
                await_(rope_done, l * 10 + 11)
                for k in range(2):
                    await_(u_stored[k], 16 * (2 * l + 2) + 16)
                pool.memset(Mtoe[:, :, :], 0.0)
                pool.memset(St[:, :, :, 0], 0.0)
                pool.drain()
                t1 = T1p[:, :].rearrange("p (a i c) -> p a i c", a=4, i=2)
                t2 = T2p[:, :].rearrange("p (a i c) -> p a i c", a=4, i=2)

                def rb(tab, n):
                    return tab[:, :, 0:1].to_broadcast([P, 4, 2]).unsqueeze(3).to_broadcast([P, 4, 2, n])

                def ib(tab, n):
                    return tab.unsqueeze(3).to_broadcast([P, 4, 2, n])

                def input_matrices(i):
                    b, pr = l * NB + i, ds(4 * i, 4)
                    await_(b_loaded, 112 * (b + 1))
                    cmul(BB[:, :, :, :], Bx[:, :, :, :], rb(FB[:, pr, :], CG), ib(FBs[:, pr, :], CG), t1, t2)
                    pool.drain()
                    for t in range(CT):
                        e = CT - 1 - t
                        cmul(MinT[:, :, :, CG * t:CG * t + CG], BB[:, :, :, :], rb(PW[:, e, pr, :], CG),
                             ib(PWs[:, e, pr, :], CG), t1, t2)
                        pool.drain()
                    pool.sem_inc(s5_min, 1)

                def batch(i):
                    b, pr = l * NB + i, ds(4 * i, 4)
                    await_(s5_ev, 3 * b + 1)
                    if not isinstance(i, int) or i > 0:
                        await_(s5_out, b)
                    for t in range(CT + 1):
                        cmul(W9[:, :, :, CG * t:CG * t + CG], Cc[:, :, :, :], rb(PW[:, t, pr, :], CG),
                             ib(PWs[:, t, pr, :], CG), t1, t2, ALU.add)
                        pool.drain()
                    pool.sem_inc(s5_w, 1)
                    await_(s5_ev, 3 * b + 2)
                    tg = T1p[0:CG, :].rearrange("p (g c) -> p g c", g=8)
                    tt(tg, dsk[0:CG, :].unsqueeze(2).to_broadcast([CG, 8, CG]),
                       ident[0:CG, 0:CG].unsqueeze(1).to_broadcast([CG, 8, CG]), ALU.mult)
                    pool.drain()
                    tt(Gs[0:CG, :, 0:CG], Gs[0:CG, :, 0:CG], tg, ALU.add).then_inc(s5_g, 1)
                    pool.drain()
                    await_(s5_ev, 3 * b + 3)
                    sv = St[:, :, :, 1:NCH + 1].rearrange("q p i (s r) -> q p i s r", s=SEG)

                    def at_r(r, s0, s1):
                        return sv[:, :, :, s0:s1, r].rearrange("q p i s o -> q p i (s o)")

                    def step(dst, src, k, n):
                        a1 = T1p[:, 0:8 * n].rearrange("p (a i c) -> p a i c", a=4, i=2)
                        a2 = T2p[:, 0:8 * n].rearrange("p (a i c) -> p a i c", a=4, i=2)
                        tab, tabs = P8[:, k, pr, :].rearrange("p o a i -> p (o a) i"), P8s[:, k, pr, :].rearrange("p o a i -> p (o a) i")
                        tt(a1, src, rb(tab, n), ALU.mult)
                        tt(a2, src, ib(tabs, n), ALU.mult)
                        pool.drain()
                        tt(a1, a1, a2[:, :, ::-1, :], ALU.subtract)
                        pool.drain()
                        tt(dst, dst, a1, ALU.add)
                        pool.drain()

                    with pool.Fori(0, (RUN - 1) // 3) as r3:
                        for k in range(1, 4):
                            step(at_r(ds(3 * r3 + k, 1), 0, SEG), at_r(ds(3 * r3 + k - 1, 1), 0, SEG), ds(1, 1), SEG)
                    with pool.Fori(0, (SEG - 1) // 3) as s3:
                        ends = sv[:, :, :, :, RUN - 1]
                        for k in range(1, 4):
                            step(ends[:, :, :, ds(3 * s3 + k, 1)], ends[:, :, :, ds(3 * s3 + k - 1, 1)], ds(RUN, 1), 1)
                    with pool.Fori(0, (RUN - 1) // 3) as r3:
                        for k in range(3):
                            step(at_r(ds(3 * r3 + k, 1), 1, SEG), at_r(ds(RUN - 1, 1), 0, SEG - 1), ds(3 * r3 + k + 1, 1), SEG - 1)
                    pool.sem_inc(s5_scan, 1)

                input_matrices(0)
                with pool.Fori(0, NB - 1) as i:
                    batch(i)
                    await_(toe_loaded, 128 * (l * NB + i + 1))
                    input_matrices(i + 1)
                batch(NB - 1)

                await_(y_stored, 128 * NB * (l + 1) + 128)
                await_(y_out, l * 32 + 33)
                for k in range(4):
                    pool.dma_start(X[:, k, 0:L], yd[k * P:(k + 1) * P, :, :].rearrange("c t j -> c (t j)")).then_inc(yr_loaded, 16)
                await_(g_stored, 16 * 16 * (l + 1) + 16)

                def gate(t, par):
                    pool.dma_start(MT[:, par:par + 1, :], gd[ds(t, 1), :, :].rearrange("o p w -> p o w")).then_inc(gate_loaded[par], 16)

                A, B = l * A_PER + A_INIT, l * B_PER + B_INIT
                for par in range(2):
                    gate(8 + par, par)
                with pool.Fori(1, 4) as i:
                    for par in range(2):
                        await_(free_a if par == 0 else free_b,
                                     (A + a_use(S_OA) if par == 0 else B + b_use(S_OA + 1)) + i + 1)
                        gate(8 + 2 * i + par, par)
                for par in range(2):
                    await_(free_a if par == 0 else free_b,
                                 (A + a_use(S_OA) if par == 0 else B + b_use(S_OA + 1)) + 4 + 1)
                    gate(par, par)
                with pool.Fori(1, 4) as i:
                    for par in range(2):
                        await_(free_a if par == 0 else free_b,
                                     (A + a_use(S_OS) if par == 0 else B + b_use(S_OS + 1)) + i + 1)
                        gate(2 * i + par, par)
                await_(mg_ready, l * KD + KD)
                for j in range(2):
                    if j == 1:
                        await_(h_ready, l * 16 + 16)
                        await_(x_stored, 16 * (2 * KD + 16 * l))
                        pool.memset(X[:, :, :], 0.0).then_inc(acc_done, 1)
                    pool.memset(MT[:, 0, :], 0.0)
                    pool.drain()
                    with pool.Fori(0, KD) as t:
                        await_(mix_sq, l * 16 + 8 * j + t + 1)
                        tt(MT[:, 0, :], MT[:, 0, :], MT[:, 1, :], ALU.add).then_inc(mix_acc, 1)
                        pool.drain()


_INS = ["x", "meta_tokens", "norm_mix_pre", "norm_mix_post", "norm_mlp_pre", "norm_mlp_post", "w_in", "ssm_a_re",
        "ssm_a_im", "ssm_log_dt", "ssm_b_re", "ssm_b_im", "ssm_c_re", "ssm_c_im", "ssm_d", "w_glu", "b_glu",
        "attn_sinks", "w_o_ssm", "w_o_attn", "w_out", "w_up", "w_down"]


def shape_constants():
    inv = (1.0 / (10000.0 ** (np.arange(0, HD, 2, dtype=np.float32) / HD))).astype(np.float32)
    ang = np.arange(L, dtype=np.float32)[None, :] * inv[:, None]
    cos, sin = np.zeros((P, LP), np.float32), np.zeros((P, LP), np.float32)
    cos[:, :L] = np.tile(np.cos(ang), (4, 1))
    sin[:, :L] = np.concatenate([-np.sin(ang), np.sin(ang)] * 2, 0)
    q, k = np.arange(P)[:, None], np.arange(P)[None, :]
    mask = np.full((2, P, KEYS), NEG, np.float32)
    mask[:, :, 0:NMETA] = 0.0
    mask[1, :, 32:160] = np.where(k > q, 0.0, NEG)
    mask[:, :, 160:288] = np.where(k <= q, 0.0, NEG)
    m0 = np.where(np.arange(NMETA)[None, :] <= np.arange(NMETA)[:, None], 0.0, NEG).astype(np.float32)
    return {"cos_t": cos, "sin_t": sin, "mask_t": mask, "mask0_t": m0, "ident_t": np.eye(P, dtype=np.float32)}


def kernel(**inputs):
    import concourse.bacc as bacc
    from concourse.bass_utils import run_bass_kernel_spmd

    nc = bacc.Bacc("TRN2", target_bir_lowering=False, num_devices=1)
    arrays, aps = {}, {}
    named = {n: np.ascontiguousarray(inputs[n]) for n in _INS}
    named["x"] = named["x"].reshape(SEQ, D)
    named.update(shape_constants())
    for n, a in named.items():
        arrays[f"in_{n}"] = a
        aps[n] = nc.dram_tensor(f"in_{n}", a.shape, mybir.dt.from_np(a.dtype), kind="ExternalInput").ap()
    out = nc.dram_tensor("out_dram", (SEQ, D), F32, kind="ExternalOutput").ap()
    g = aps
    build(nc, g["x"], g["meta_tokens"],
          [g["norm_mix_pre"], g["norm_mix_post"], g["norm_mlp_pre"], g["norm_mlp_post"]], g["w_in"], g["ssm_a_re"],
          g["ssm_a_im"], g["ssm_log_dt"], g["ssm_b_re"], g["ssm_b_im"], g["ssm_c_re"], g["ssm_c_im"], g["ssm_d"],
          g["w_glu"], g["b_glu"], g["attn_sinks"], g["w_o_ssm"], g["w_o_attn"], g["w_out"], g["w_up"], g["w_down"],
          g["cos_t"], g["sin_t"], g["mask_t"], g["mask0_t"], g["ident_t"], out)
    r = run_bass_kernel_spmd(nc, [arrays], core_ids=[0])
    return r.results[0]["out_dram"].reshape(1, SEQ, D)
```

```python
from contextlib import ExitStack

import numpy as np
import concourse.bass as bass
from concourse import mybir

P = 128
D = 1024
SEQ = 1024
NMETA = 16
DEPTH = 2
KD = D // P
L = SEQ + NMETA
NC3 = 3
CW = 348
LP = NC3 * CW
NBLK = SEQ // P
NH = 16
NKV = 4
HD = 64
G_S = 32
CG = 16
NS = 64
NP = G_S // 2
CT = 8
NCH = L // CT
SEG, RUN = 13, 10
assert SEG * RUN == NCH and (SEG - 1) % 3 == 0 and (RUN - 1) % 3 == 0
NB = 4
DFF = 4 * D
EPS = 1e-6
SCALE = HD ** -0.5
KEYS = 288
KOFF = 144
NEG = -1e30

S_U, S_Q, S_K, S_V, S_G = 0, 4, 12, 14, 16
S_OA, S_GLU, S_OS, S_OUT, S_FF = 32, 40, 44, 52, 60
STRIPS = 124
A_PER, B_PER = 75, 55
A_INIT, B_INIT = 4, 4

F32 = mybir.dt.float32
F32R = mybir.dt.float32r
ALU = mybir.AluOpType
ACT = mybir.ActivationFunctionType
AX = mybir.AxisListType
ds = bass.ds


def a_use(s):
    if s < 16:
        return 1 + s // 2 if s % 2 == 0 else None
    if s < 32:
        return 11 + s - 16
    if s < 60:
        return 27 + (s - 32) // 2 if s % 2 == 0 else None
    return 42 + (s - 60) // 2 if s % 2 == 0 else None


def b_use(s):
    if s < 16:
        return (s - 1) // 2
    if s < 60:
        return 8 + (s - 33) // 2
    return 23 + (s - 61) // 2


EVF, EVH = 16, 48
A_PRE1, A_VT, A_POST1, B_PRE2, A_POST2 = 0, 9, 41, 22, 74


def build(nc, x, meta, norms, w_in, a_re, a_im, log_dt, b_re, b_im, c_re, c_im, d_skip, w_glu, b_glu, sinks,
          w_o_ssm, w_o_attn, w_out, w_up, w_down, cos_t, sin_t, mask_t, mask0_t, ident_t, out):
    with ExitStack() as ctx:
        base = (nc.sbuf_base + 31) // 32 * 32

        def at(name, shape, off, dt=F32):
            return nc.alloc_sbuf_tensor_at(name, shape, dt, offset=base + 4 * off, align_bytes=4)

        TL = KD * LP
        HH, HL = at("h_hi", [P, KD, LP], 0, F32R), at("h_lo", [P, KD, LP], TL, F32R)
        XO = at("x_old", [P, KD, LP], TL)
        BH, BL = at("b_hi", [P, KD, LP], 2 * TL, F32R), at("b_lo", [P, KD, LP], 3 * TL, F32R)
        X, XR = at("x_res", [P, KD, LP], 4 * TL), at("z2_split", [P, KD, LP], 4 * TL, F32R)
        WRAW = at("w_raw", [P, 2, KD, P], 5 * TL)
        WHI, WLO = at("w_hi", [P, 2, KD, P], 5 * TL + 2048, F32R), at("w_lo", [P, 2, KD, P], 5 * TL + 4096, F32R)
        M0 = 5 * TL + 6144
        ident = at("ident", [P, P], M0)
        ones = at("ones", [P, P], M0 + 128)
        gains = at("gains", [P, DEPTH, 4, KD], M0 + 256)
        bglu = at("bglu", [P, DEPTH, 4], M0 + 320)
        sink = at("sink", [P, DEPTH, NH], M0 + 328)
        mask0 = at("mask0", [P, NMETA], M0 + 360)
        bgluh = at("bgluh", [P, DEPTH, 4], M0 + 376)
        stat = at("att_stat", [P, 6, NH], M0 + 384)
        M1 = M0 + 480
        MT = at("m_tiles", [P, 4, LP], M1)
        s_sb = at("s_sb", [P, 4, KEYS], M1)
        mask_cur = at("mask_cur", [P, KEYS], M1 + 1152)
        mask_rest = at("mask_rest", [P, KEYS], M1 + 1440)
        pt_sb = at("pt_sb", [P, 2, 4, P], M1 + 1728)
        PW = at("pw", [P, CT + 1, NP, 2], M1 + 2752)
        PWs = at("pw_s", [P, CT + 1, NP, 2], M1 + 3040)
        P8 = at("p8", [P, RUN + 1, NP, 2], M1 + 3328)
        P8s = at("p8_s", [P, RUN + 1, NP, 2], M1 + 3776)
        FB = at("f_b", [P, NP, 2], M1 + 4224)
        FBs = at("f_bs", [P, NP, 2], M1 + 4256)
        BB = at("b_bar", [P, 4, 2, CG], M1 + 4288)
        T1p = at("pool_t1", [P, P], M1 + 4416)
        T2p = at("pool_t2", [P, P], M1 + 4544)
        pm_sb = at("pm_sb", [P, 4, 32], M1 + 4672)
        assert M0 + 480 + 4800 <= (nc.sbuf_usable_end - base) // 4 - 8, (M1 + 4672, nc.sbuf_usable_end - base)
        QY = at("qy", [P, KD, LP], 2 * TL)
        R1 = 3 * TL
        cosb, sinb = at("cosb", [P, LP], R1), at("sinb", [P, LP], R1 + LP)
        rot = at("rot", [P, LP], R1 + 2 * LP)
        rt1, rt2 = at("rt1", [P, LP], R1 + 3 * LP), at("rt2", [P, LP], R1 + 4 * LP)
        ut = at("u_tok", [P, LP], R1 + 5 * LP)
        ust = at("u_stage", [P, 2, CT, NCH], R1 + 6 * LP)
        Uch = at("u_chunk", [P, 8, NCH], R1)
        St = at("s5_state", [P, 4, 2, NCH + 1], R1 + 1040)
        MinT = at("m_in_t", [P, 4, 2, CT * CG], R1 + 2088)
        Min = at("m_in", [P, 4, 2, P], R1 + 3112)
        Mtoe = at("m_toe", [P, 8, P], R1 + 4136)
        W9 = at("w9", [P, 4, 2, (CT + 1) * CG], R1 + 5160)
        dsk = at("d_skip", [P, 8], R1 + 6312)
        Gs = at("g_small", [P, 8, P], R1 + 2088)
        nv, ny, nt, rstd = (at(f"n_{k}", [P, LP], 2 * TL + i * LP) for i, k in enumerate(("v", "y", "t", "rstd")))
        sqr = at("sq_ring", [P, 2, LP], 2 * TL + 4 * LP)
        nx = at("n_x", [P, 2, LP], 2 * TL + 6 * LP)
        R2 = 4 * TL
        kbuf = at("kbuf", [P, 2, KOFF + SEQ], R2)
        Vb = at("vb", [P, NBLK + 1, 256], R2 + 2336)
        vmeta = at("vmeta", [P, 256], R2 + 4640)
        kst = at("kst", [P, NKV, KEYS], R2 + 4896)
        qst = at("qst", [P, KD, P], R2 + 6048)
        vst = at("vst", [P, 2, 256], R2 + 7072)
        ptm_sb = at("ptm_sb", [P, 4, P], R2 + 7584)
        Bx = at("b_raw", [P, 4, 2, CG], R2 + 8096)
        Cc = at("c_conj", [P, 4, 2, CG], R2 + 8224)
        gst = at("gate_stage", [P, LP], R1 + 6320)
        Craw = at("c_raw", [P, 2, P], R1 + 7364)
        vt = [at("v_feat0", [P, LP], R1 + 6320), at("v_feat1", [P, LP], M1)]
        XT = at("x_tok", [P, NBLK + 1, D], 0)
        OT = at("o_tok", [P, 2, D], 0)

        PA = ctx.enter_context(nc.psum_tensor("ps_a", [P, 3, 512], F32))
        PB = ctx.enter_context(nc.psum_tensor("ps_b", [P, 3, 512], F32))
        PC = ctx.enter_context(nc.psum_tensor("ps_c", [P, 2, 512], F32))
        PS = [PB[:, 0, :], PB[:, 1, :]]
        PT = [PB[:, 2, :], PC[:, 0, :]]
        PO = PC[:, 1, :]
        BK4 = [PB[:, 0, :], PB[:, 1, :], PB[:, 2, :], PC[:, 0, :]]

        def dram(name, shape):
            return nc.dram_tensor(name, shape, F32, kind="Internal").ap()

        xd = dram("x_spill", (KD, P, LP))
        gd = dram("gate_spill", (16, P, LP))
        ud = dram("u_spill", (512, CT, NCH))
        yd = dram("y_spill", (512, CT, NCH))

        def sem(name):
            return ctx.enter_context(nc.semaphore(name))

        const_loaded = sem("const_loaded")
        xtok_loaded = sem("xtok_loaded")
        w_loaded = [sem("w_loaded0"), sem("w_loaded1")]
        w_hi = sem("w_hi")
        w_split = sem("w_split")
        strip_done = sem("strip_done")
        free_a = sem("free_a")
        free_b = sem("free_b")
        init_tr = sem("init_tr")
        x_ready = sem("x_ready")
        sq_ready = sem("sq_ready")
        sq_used = sem("sq_used")
        stat_done = sem("stat_done")
        var_done = sem("var_done")
        ln_done = sem("ln_done")
        rs0_done = sem("rs0_done")
        hx_ready = sem("hx_ready")
        hx_hi = sem("hx_hi")
        h_ready = sem("h_ready")
        mix_sq = sem("mix_sq")
        mix_acc = sem("mix_acc")
        xo_loaded = sem("xo_loaded")
        post_scaled = sem("post_scaled")
        x_stored = sem("x_stored")
        tab_loaded = sem("tab_loaded")
        u_copied = sem("u_copied")
        u_stored = [sem("u_stored0"), sem("u_stored1")]
        rot_ready = sem("rot_ready")
        rope_done = sem("rope_done")
        pool_init = sem("pool_init")
        v_tr = sem("v_tr")
        stage_qk = sem("stage_qk")
        scores_done = sem("scores_done")
        stt_done = sem("stt_done")
        m_ready = sem("m_ready")
        exp_done = sem("exp_done")
        p_ready = sem("p_ready")
        tr_done = sem("tr_done")
        pt_act = sem("pt_act")
        pt_dve = sem("pt_dve")
        pv_done = sem("pv_done")
        y_out = sem("y_out")
        m0_done = [sem(f"meta_{k}") for k in ("scores", "max", "exp", "p", "tr", "pt", "pv", "y")]
        g_stored = sem("g_stored")
        s5_coef = sem("s5_coef")
        s5_e = [sem(f"s5_e{i}") for i in range(6)]
        b_loaded = sem("b_loaded")
        s5_min = sem("s5_min")
        s5_w = sem("s5_w")
        s5_cc = sem("s5_cc")
        s5_pe = sem("s5_pe")
        s5_ev = sem("s5_ev")
        s5_out = sem("s5_out")
        s5_out_ev = sem("s5_out_ev")
        s5_g = sem("s5_g")
        toe_loaded = sem("toe_loaded")
        u_loaded = sem("u_loaded")
        s5_scan = sem("s5_scan")
        y_stored = sem("y_stored")
        yr_loaded = sem("yr_loaded")
        ys_hi = sem("ys_hi")
        ys_ready = sem("ys_ready")
        ge = [sem(f"gelu_{i}") for i in range(4)]
        z_ready = sem("z_ready")
        gate_loaded = [sem("gate_loaded0"), sem("gate_loaded1")]
        gate_used = sem("gate_used")
        ev_t = sem("ev_t")
        ev_f = sem("ev_f")
        ev_hi = sem("ev_hi")
        z2_ready = sem("z2_ready")
        mg_ready = sem("mg_ready")
        hid_ready = sem("hid_ready")
        relu_done = sem("relu_done")
        acc_done = sem("acc_done")
        passed = sem("passed")
        out_tr = sem("out_tr")
        out_ev = sem("out_ev")
        out_stored = [sem("out_stored0"), sem("out_stored1")]

        block = ctx.enter_context(nc.Block())
        W = dict(
            w_in=w_in.rearrange("l r c -> (l r) c"), w_oa=w_o_attn.rearrange("l r c -> (l r) c"),
            w_os=w_o_ssm.rearrange("l r c -> (l r) c"), w_glu=w_glu.rearrange("l r c -> (l r) c"),
            w_out=w_out.rearrange("l r c -> (l r) c"), w_up=w_up.rearrange("l r c -> (l r) c"),
            w_down=w_down.rearrange("l r c -> (l r) c"))

        a_pn = [a.rearrange("l (p g) n -> l (g n) p", g=2) for a in (a_re, a_im)]
        dt_v = log_dt.rearrange("l (p g) -> l g p", g=2)
        b_v = [t.rearrange("l (k p g) n c -> (l k) (g n) p c", k=NB, g=2) for t in (b_re, b_im)]
        c_v = [t.rearrange("l (k g) c n -> (l k) (g c) n", k=NB) for t in (c_re, c_im)]
        d_v = d_skip.rearrange("l (k g) c -> (l k) c g", k=NB)

        def v3(t):
            return t.rearrange("p (c w) -> p c w", c=NC3)

        def pset(s):
            return PA if a_use(s) is not None else PB

        @block.sync
        def _(sp):
            sp.dma_start(ident[:, :], ident_t).then_inc(const_loaded, 16)
            sp.dma_start(XT[0:NMETA, 0, :], meta).then_inc(xtok_loaded, 16)
            for n in range(NBLK):
                sp.dma_start(XT[:, n + 1, :], x[n * P:(n + 1) * P, :]).then_inc(xtok_loaded, 16)
            for l in range(DEPTH):
                for i in range(4):
                    sp.dma_start(gains[:, l, i, :], norms[i][l].rearrange("(k p) -> p k", p=P), allow_slow_non_contiguous=True).then_inc(const_loaded, 16)
                sp.dma_start(bglu[:, l, :], b_glu[l].rearrange("(k p) -> p k", p=P), allow_slow_non_contiguous=True).then_inc(const_loaded, 16)
                sp.dma_start(sink[:, l, :], sinks[l].partition_broadcast(P)).then_inc(const_loaded, 16)
            sp.dma_start(mask0[0:NMETA, :], mask0_t).then_inc(const_loaded, 16)

            sp.wait_ge(w_split, 1)
            sp.dma_start(WRAW[:, 0, :, :], W["w_in"][0:D, 0:P].rearrange("(k p) c -> p k c", p=P)).then_inc(w_loaded[0], 16)
            with sp.Fori(0, DEPTH) as l:
                S = l * STRIPS

                def strip(s, par, rows, row0, col0, ks):
                    sp.wait_ge(w_split, s + 1)
                    sp.sem_inc(passed, 1)
                    sp.dma_start(WRAW[:, par, 0:ks, :],
                                 rows[ds(row0, ks * P), ds(col0, P)].rearrange("(k p) c -> p k c", p=P)
                                 ).then_inc(w_loaded[par], 16)

                def tables():
                    sp.wait_ge(h_ready, l * 16 + 8)
                    sp.dma_start(cosb[:, :], cos_t).then_inc(tab_loaded, 16)
                    sp.dma_start(sinb[:, :], sin_t).then_inc(tab_loaded, 16)
                    sp.dma_start(mask_cur[:, :], mask_t[0]).then_inc(tab_loaded, 16)
                    sp.dma_start(mask_rest[:, :], mask_t[1]).then_inc(tab_loaded, 16)

                strip(S + 1, 1, W["w_in"], l * D, P, KD)
                tables()
                with sp.Fori(1, 8) as i:
                    for par in range(2):
                        strip(S + 2 * i + par, par, W["w_in"], l * D, (2 * i + par) * P, KD)

                def coef_loads(b):
                    one = lambda v: v[ds(b, 1), :, :].rearrange("o q n -> (o q) n")
                    for ri in range(2):
                        sp.dma_start(Bx[:, :, ri, :], b_v[ri][ds(b, 1), :, :, :].rearrange("o q p c -> (o q) p c")).then_inc(b_loaded, 16)
                        for dup in range(2):
                            sp.dma_start(Craw[:, ri, NS * dup:NS * dup + NS], one(c_v[ri])).then_inc(b_loaded, 16)
                    sp.dma_start(dsk[0:CG, :], one(d_v), allow_slow_non_contiguous=True).then_inc(b_loaded, 16)

                def gate_strips(i, lo, hi):
                    for j in range(lo, hi):
                        strip(S + S_G + 4 * i + j, j % 2, W["w_in"], l * D, (S_G + 4 * i + j) * P, KD)

                sp.wait_ge(x_stored, 16 * (KD + 16 * l))
                for k in range(2):
                    sp.wait_ge(u_stored[k], 16 * (2 * l + 2) + 16)
                sp.sem_inc(passed, 1)
                coef_loads(l * NB)

                def attention_loads(i, last=False):
                    b = l * NB + i
                    gate_strips(i, 0, 3)
                    sp.wait_ge(rope_done, l * 10 + 11)
                    sp.wait_ge(y_stored, 128 * b + 128)
                    sp.sem_inc(passed, 1)
                    for t in range(CT):
                        sp.dma_start(Uch[CG * t:CG * t + CG, :, :],
                                     ud[ds(i * P, P), t, :].rearrange("(g c) j -> c g j", g=8)).then_inc(u_loaded, 16)
                    gate_strips(i, 3, 4)
                    sp.wait_ge(s5_g, b + 1)
                    sp.sem_inc(passed, 1)
                    for t in range(CT):
                        sp.dma_start(Mtoe[CG * t:CG * t + CG, :, CG * t:P], Gs[0:CG, :, 0:P - CG * t]).then_inc(toe_loaded, 16)
                    if not last:
                        coef_loads(b + 1)

                with sp.Fori(0, NB - 1) as i:
                    attention_loads(i)
                attention_loads(NB - 1, last=True)
                with sp.Fori(0, 4) as i:
                    for par in range(2):
                        strip(S + S_OA + 2 * i + par, par, W["w_oa"], l * D, (2 * i + par) * P, KD)
                with sp.Fori(0, 2) as i:
                    for par in range(2):
                        strip(S + S_GLU + 2 * i + par, par, W["w_glu"], l * 512, (2 * i + par) * P, 4)
                with sp.Fori(0, 4) as i:
                    for par in range(2):
                        strip(S + S_OS + 2 * i + par, par, W["w_os"], l * 512, (2 * i + par) * P, 4)
                def x_old(t, strips_done, j):
                    sp.wait_ge(strip_done, S + strips_done + 2)
                    sp.wait_ge(x_stored, 16 * ((1 + j) * KD + 16 * l))
                    sp.sem_inc(passed, 1)
                    sp.dma_start(XO[:, ds(t, 1), :], xd[ds(t, 1), :, :].rearrange("o p w -> p o w")).then_inc(xo_loaded, 16)

                with sp.Fori(0, 4) as i:
                    for par in range(2):
                        strip(S + S_OUT + 2 * i + par, par, W["w_out"], l * D, (2 * i + par) * P, KD)
                        x_old(2 * i + par, S_OA + 8, 0)

                def mlp_loads(q, last=False):
                    with sp.Fori(0, 4) as i:
                        for par in range(2):
                            strip(S + S_FF + 16 * q + 2 * i + par, par, W["w_up"], l * D,
                                  q * D + (2 * i + par) * P, KD)
                    with sp.Fori(0, 4) as i:
                        for par in range(2):
                            strip(S + S_FF + 16 * q + 8 + 2 * i + par, par, W["w_down"], l * DFF + q * D,
                                  (2 * i + par) * P, KD)
                            if last:
                                x_old(2 * i + par, S_FF + 56, 1)

                with sp.Fori(0, 3) as q:
                    mlp_loads(q)
                mlp_loads(3, last=True)
                strip(S + STRIPS, 0, W["w_in"], (1 - l) * D, 0, KD)

        @block.tensor
        def _(pe):
            pe.sem_inc(strip_done, 2)
            pe.sem_inc(sq_used, 2)
            pe.sem_inc(tr_done, 1)
            pe.wait_ge(const_loaded, 16 * 14)
            pe.wait_ge(xtok_loaded, 16 * (NBLK + 1))
            for k in range(KD):
                ps, fr = (PA, free_a) if k % 2 == 0 else (PB, free_b)
                pe.wait_ge(fr, k // 2 + 1)
                for n in range(NBLK):
                    pe.transpose(ps[:, n // 4, (n % 4) * P:(n % 4 + 1) * P], XT[:, n + 1, k * P:(k + 1) * P], ident[:, :])
                pe.transpose(ps[:, 2, 0:NMETA], XT[0:NMETA, 0, k * P:(k + 1) * P],
                             ident[0:NMETA, 0:NMETA]).then_inc(init_tr, 1)

            def pre_stats(q0):
                for k in range(KD):
                    pe.wait_ge(sq_ready, q0 + k + 1)
                    for c in range(NC3):
                        mm = pe.matmul(PA[:, c, 0:CW], ones[:, :], sqr[:, k % 2, c * CW:(c + 1) * CW],
                                       start=(k == 0), stop=(k == KD - 1))
                    mm.then_inc(sq_used, 1)

            pe.wait_ge(free_a, A_INIT + 1)
            pre_stats(0)
            with pe.Fori(0, DEPTH) as l:
                S, A, B = l * STRIPS, l * A_PER + A_INIT, l * B_PER + B_INIT

                def post_stats(a, n):
                    pe.wait_ge(free_a, A + a + 1)
                    pe.wait_ge(mix_acc, l * 16 + n + 1)
                    for c in range(NC3):
                        mm = pe.matmul(PA[:, c, 0:CW], ones[:, :], MT[:, 0, c * CW:(c + 1) * CW], start=True, stop=True)
                    mm.then_inc(stat_done, 1)

                def ksteps(ps, par, ks, rh, rl, k0, total, waits=None):
                    for k in ks:
                        if waits:
                            waits(k)
                        for t, (w, r) in enumerate(((WHI, rh), (WHI, rl), (WLO, rh))):
                            for c in range(NC3):
                                mm = pe.matmul(ps[:, c, 0:CW], w[:, par, k, :], r[:, k0 + k, c * CW:(c + 1) * CW],
                                               start=(k == 0 and t == 0), stop=(k == total - 1 and t == 2))
                    return mm

                def take(s_static, s, i2):
                    pe.wait_ge(w_split, S + s + 3)
                    if a_use(s_static) is not None:
                        pe.wait_ge(free_a, A + a_use(s_static) + i2 + 1)
                    else:
                        pe.wait_ge(free_b, B + b_use(s_static) + i2 + 1)

                def strips(s0, n, total, rh, rl, extra=0, waits=None):
                    with pe.Fori(0, n // 2) as i:
                        for par in range(2):
                            take(s0 + par, extra * 16 + s0 + 2 * i + par, i + extra * 8)
                            ksteps(pset(s0 + par), par, range(total), rh, rl, 0, total, waits).then_inc(strip_done, 1)

                strips(S_U, 14, KD, HH, HL, waits=lambda k: pe.wait_ge(h_ready, l * 16 + k + 1))
                for par in range(2):
                    take(S_V + par, S_V + par, 0)
                    ksteps(pset(S_V + par), par, range(KD), HH, HL, 0, KD).then_inc(strip_done, 1)

                def v_tokens(par):
                    pe.wait_ge(free_a, A + A_VT + par + 1)
                    for n in range(NBLK):
                        pe.transpose(PA[:, n // 4, (n % 4) * P:(n % 4 + 1) * P],
                                     vt[par][:, NMETA + n * P:NMETA + (n + 1) * P], ident[:, :])
                    pe.transpose(PA[0:NMETA, 2, 0:P], vt[par][:, 0:NMETA], ident[:, :]).then_inc(v_tr, 1)

                v_tokens(0)

                pe.wait_ge(stage_qk, l * 9 + 1)
                pe.wait_ge(free_b, B + 8 + 1)
                pe.sem_inc(passed, 1)
                for h in range(NH):
                    kv, hb = h // 4, HD * (h % 2)
                    mm = pe.matmul(PS[h % 2][0:NMETA, (h // 2) * 16:(h // 2 + 1) * 16], QY[hb:hb + HD, h // 2, 0:NMETA],
                                   kst[hb:hb + HD, kv, 0:NMETA], start=True, stop=True)
                mm.then_inc(m0_done[0], 1)
                v_tokens(1)
                pe.wait_ge(m0_done[3], l + 1)
                pe.sem_inc(passed, 1)
                pflat = s_sb[:, :, :].rearrange("p a b -> p (a b)")
                for h in range(NH):
                    mm = pe.transpose(PT[0][0:NMETA, h * 16:(h + 1) * 16], pflat[0:NMETA, h * 16:(h + 1) * 16],
                                      ident[0:NMETA, 0:NMETA])
                mm.then_inc(m0_done[4], 1)
                pe.wait_ge(m0_done[5], l + 1)
                pe.sem_inc(passed, 1)
                ptm = pt_sb[:, 0, 0:2, :].rearrange("p a b -> p (a b)").rearrange("p (v j g q) -> p v g j q", v=4, j=2, g=2)
                for kv in range(NKV):
                    for g in range(2):
                        mm = pe.matmul(PO[HD * g:HD * g + HD, kv * 32:kv * 32 + 32], vmeta[0:NMETA, kv * HD:(kv + 1) * HD],
                                       ptm[0:NMETA, kv, g, :, :], start=True, stop=True)
                mm.then_inc(m0_done[6], 1)

                def scores(un, kv, n, ev=None):
                    if kv == 0:
                        pe.wait_ge(stage_qk, l * 9 + 2 + n)
                    if ev is not None:
                        pe.wait_ge(*ev)
                    for g in range(4):
                        hb = HD * (g % 2)
                        pe.wait_ge(stt_done, 4 * un + g + 1)
                        pe.matmul(PS[g % 2][:, 0:KEYS], qst[hb:hb + HD, 2 * kv + g // 2, :], kst[hb:hb + HD, kv, :],
                                  start=True, stop=True).then_inc(scores_done, 1)

                def transposes(un, ev=None):
                    pe.wait_ge(p_ready, un + 1)
                    if ev is not None:
                        pe.wait_ge(*ev)
                    for g in range(4):
                        pe.transpose(PT[0][:, g * P:(g + 1) * P], s_sb[:, g, 32:160], ident[:, :])
                        pe.transpose(PT[1][:, g * P:(g + 1) * P], s_sb[:, g, 160:288], ident[:, :])
                    pe.wait_ge(y_out, un + 1)
                    pe.transpose(PO[:, 256:384], pm_sb[:, :, :].rearrange("p a b -> p (a b)"), ident[:, :]).then_inc(tr_done, 1)

                def pv(un, kv):
                    pe.wait_ge(pt_act, un + 1)
                    pe.wait_ge(pt_dve, un + 1)
                    vc = slice(kv * HD, kv * HD + HD)
                    for hf in range(2):
                        o = PO[HD * hf:HD * hf + HD, 0:256]
                        for j in range(2):
                            pe.matmul(o, vst[:, j, vc], pt_sb[:, j, hf::2, :], start=(j == 0), stop=False)
                        mm = pe.matmul(o, vmeta[:, vc], ptm_sb[:, hf::2, :], start=False, stop=True)
                    mm.then_inc(pv_done, 1)

                def banks_free(un):
                    pe.wait_ge(stt_done, 4 * un + 6)
                    pe.wait_ge(pt_act, un)
                    pe.wait_ge(pt_dve, un)
                    pe.sem_inc(passed, 1)

                def s5_a0(b, un):
                    pe.wait_ge(b_loaded, 112 * (b + 1))
                    pe.wait_ge(stt_done, 4 * un + 6)
                    for ri in range(2):
                        mm = pe.transpose(PS[0][:, ri * P:(ri + 1) * P], Craw[:, ri, :], ident[:, :])
                    mm.then_inc(s5_pe, 1)

                def s5_a(b, un):
                    pe.wait_ge(s5_min, b + 1)
                    pe.wait_ge(s5_w, b + 1)
                    banks_free(un)
                    for p in range(4):
                        for ri in range(2):
                            i = 2 * p + ri
                            pe.transpose(PS[i // 4][:, (i % 4) * P:(i % 4 + 1) * P], MinT[:, p, ri, :], ident[:, :])
                    for g in range(8):
                        gb, p = NS * (g % 2), g // 2
                        for ri in range(2):
                            mm = pe.matmul(PT[g % 2][0:CG, p * P:(p + 1) * P], BB[gb:gb + NS, p, ri, :],
                                           W9[gb:gb + NS, p, ri, 0:P], start=(ri == 0), stop=(ri == 1))
                    mm.then_inc(s5_pe, 1)

                def s5_b(b, un):
                    pe.wait_ge(s5_ev, 3 * b + 2)
                    pe.wait_ge(u_loaded, 128 * (b + 1))
                    banks_free(un)
                    for p in range(4):
                        for g2 in range(2):
                            for ri in range(2):
                                mm = pe.matmul(BK4[p][NS * g2:NS * g2 + NS, ri * NCH:(ri + 1) * NCH],
                                               Min[:, p, ri, NS * g2:NS * g2 + NS], Uch[:, 2 * p + g2, :],
                                               start=True, stop=True)
                    mm.then_inc(s5_pe, 1)

                def s5_c(b):
                    pe.wait_ge(s5_scan, b + 1)
                    pe.wait_ge(toe_loaded, 128 * (b + 1))
                    pe.sem_inc(passed, 1)
                    for g in range(8):
                        p, gb = g // 2, NS * (g % 2)
                        o = BK4[2 * (g % 2) + p // 2][:, (p % 2) * NCH:(p % 2 + 1) * NCH]
                        pe.matmul(o, Mtoe[:, g, :], Uch[:, g, :], start=True, stop=False)
                        for ri in range(2):
                            mm = pe.matmul(o, W9[gb:gb + NS, p, ri, CG:CG + P], St[gb:gb + NS, p, ri, 0:NCH],
                                           start=False, stop=(ri == 1))
                    mm.then_inc(s5_out, 1)

                pe.wait_ge(m0_done[7], l + 1)
                pe.sem_inc(passed, 1)
                def attention(i, first=False):
                    b = l * NB + i
                    for u8 in range(8):
                        kv = u8 % NKV
                        un = l * 32 + 8 * i + u8
                        ev = {0: (s5_ev, 3 * b + 1), 3: (s5_ev, 3 * b + 2), 4: (s5_ev, 3 * b + 3)}
                        if not first:
                            ev[1] = (s5_out_ev, b)
                        scores(un, kv, 2 * i + u8 // NKV, ev.get(u8 - 1))
                        gi = u8 // 2
                        if u8 % 2 == 0:
                            pe.wait_ge(w_split, S + S_G + gi + 4 * i + 3)
                            pe.wait_ge(free_a, A + a_use(S_G) + gi + 4 * i + 1)
                            ksteps(PA, gi % 2, range(0, 4), HH, HL, 0, KD)
                        else:
                            ksteps(PA, gi % 2, range(4, 8), HH, HL, 0, KD).then_inc(strip_done, 1)
                        if u8 == 0:
                            s5_a0(b, un)
                        elif u8 == 1 and not first:
                            banks_free(un)
                            s5_c(b - 1)
                        elif u8 == 3:
                            s5_a(b, un)
                        elif u8 == 4:
                            s5_b(b, un)
                        if not (first and u8 == 0):
                            pv(un - 1, (kv - 1) % NKV)
                        transposes(un, ev.get(u8) if u8 else None)

                attention(0, first=True)
                with pe.Fori(1, NB) as i:
                    attention(i)
                pv(l * 32 + 31, NKV - 1)
                strips(S_OA, 2, KD, HH, HL, waits=lambda k: pe.wait_ge(ys_ready, l * KD + k + 1))
                pe.wait_ge(free_b, B + b_use(S_OA + 1) + 2)
                pe.wait_ge(pt_act, l * 32 + 32)
                pe.wait_ge(pt_dve, l * 32 + 32)
                s5_c(l * NB + NB - 1)
                take(S_OA + 2, S_OA + 2, 0)
                ksteps(PA, 0, range(KD), HH, HL, 0, KD).then_inc(strip_done, 1)
                pe.wait_ge(s5_out_ev, NB * (l + 1))
                take(S_OA + 3, S_OA + 3, 0)
                ksteps(PB, 1, range(KD), HH, HL, 0, KD).then_inc(strip_done, 1)
                strips(S_OA + 4, 4, KD, HH, HL)
                zl = BL[:, 4:8, :]
                strips(S_GLU, 4, 4, BL, zl, waits=lambda k: pe.wait_ge(z_ready, l * 4 + k + 1))
                strips(S_OS, 8, 4, XR, XR[:, 4:8, :], waits=lambda k: pe.wait_ge(z2_ready, l * 4 + k + 1))
                strips(S_OUT, 8, KD, BH, BL, waits=lambda k: pe.wait_ge(mg_ready, l * KD + k + 1))
                post_stats(A_POST1, 8)
                take(S_FF, S_FF, 0)
                pe.wait_ge(free_b, B + B_PRE2 + 1)
                for k in range(KD):
                    pe.wait_ge(h_ready, l * 16 + 8 + k + 1)
                    mm = ksteps(PA, 0, [k], HH, HL, 0, KD)
                    if k == KD - 1:
                        mm.then_inc(strip_done, 1)
                    pe.wait_ge(sq_ready, l * 16 + 8 + k + 1)
                    for c in range(NC3):
                        mm = pe.matmul(PB[:, c, 0:CW], ones[:, :], sqr[:, k % 2, c * CW:(c + 1) * CW],
                                       start=(k == 0), stop=(k == KD - 1))
                    mm.then_inc(sq_used, 1)

                def quarter(q, first=False):
                    if first:
                        take(S_FF + 1, S_FF + 1, 0)
                        ksteps(PB, 1, range(KD), HH, HL, 0, KD).then_inc(strip_done, 1)
                        strips(S_FF + 2, 6, KD, HH, HL)
                    else:
                        strips(S_FF, 8, KD, HH, HL, extra=q)
                    strips(S_FF + 8, 8, KD, BH, BL, extra=q,
                           waits=lambda k: pe.wait_ge(hid_ready, l * 32 + q * 8 + k + 2))

                quarter(0, first=True)
                with pe.Fori(1, 4) as q:
                    quarter(q)
                post_stats(A_POST2, 16)
                pe.wait_ge(free_a, A + A_PER + 1)
                pre_stats(l * 16 + 16)

            A, B = DEPTH * A_PER + A_INIT, DEPTH * B_PER + B_INIT
            pe.wait_ge(x_ready, 16 * DEPTH + 1)
            for n in range(NBLK):
                ps, fr, u0 = (PA, free_a, A) if n % 2 == 0 else (PB, free_b, B)
                pe.wait_ge(fr, u0 + n // 2 + 1)
                for k in range(KD):
                    mm = pe.transpose(ps[:, k // 4, (k % 4) * P:(k % 4 + 1) * P],
                                      X[:, k, NMETA + n * P:NMETA + (n + 1) * P], ident[:, :])
                mm.then_inc(out_tr, 1)

        @block.scalar
        def _(act):
            for k in range(2):
                act.sem_inc(u_stored[k], 16)
            act.sem_inc(g_stored, 16)

            def w_high(s, par, ks=KD):
                s2 = s[1]
                act.wait_ge(w_loaded[par], 16 * (s2 + 1))
                act.wait_ge(strip_done, s[0] + 1)
                act.activation(WHI[:, par, 0:ks, :], WRAW[:, par, 0:ks, :], ACT.Copy).then_inc(w_hi, 1)

            w_high((0, 0), 0)
            act.wait_ge(const_loaded, 16 * 14)
            act.activation(bgluh[:, :, :], bglu[:, :, :], ACT.Copy, scale=0.5)
            act.wait_ge(pool_init, 1)
            for k in range(KD):
                ps, fr = (PA, free_a) if k % 2 == 0 else (PB, free_b)
                act.wait_ge(init_tr, k + 1)
                act.activation(X[:, k, NMETA:L].rearrange("p (c w) -> p c w", c=2), ps[:, 0:2, :], ACT.Copy)
                act.activation(X[:, k, 0:NMETA], ps[:, 2, 0:NMETA], ACT.Copy).then_inc(fr, 1)
                act.wait_ge(fr, k // 2 + 2)
                act.drain()
                act.dma_start(xd[k], X[:, k, :]).then_inc(x_stored, 16)

            def square(k, q0):
                act.wait_ge(sq_used, q0 + k + 1)
                act.activation(sqr[:, k % 2, :], X[:, k, :], ACT.Square).then_inc(sq_ready, 1)

            for k in range(KD):
                square(k, 0)
            with act.Fori(0, DEPTH) as l:
                S, S2 = l * STRIPS, l * (STRIPS // 2)
                A, B = l * A_PER + A_INIT, l * B_PER + B_INIT

                def nxt(s, i, ks=KD):
                    w_high((S + s + 1 + 2 * i, S2 + (s + 1) // 2 + i), (s + 1) % 2, ks)

                def freed(s):
                    return free_a if a_use(s) is not None else free_b

                def rsqrt0(sums, n, ps):
                    act.wait_ge(sums, n)
                    act.activation(v3(ny[:, :]), ps[:, :, 0:CW], ACT.Ln, scale=1.0 / D, bias=EPS).then_inc(ln_done, 1)
                    act.drain()
                    act.activation(ny[:, :], ny[:, :], ACT.Exp, scale=-0.5).then_inc(rs0_done, 1)

                rsqrt0(sq_used, l * 16 + KD + 2, PA)
                for k in range(KD):
                    act.wait_ge(hx_ready, l * 8 + k + 1)
                    act.activation(HH[:, k, :], nx[:, k % 2, :], ACT.Copy).then_inc(hx_hi, 1)
                with act.Fori(0, 2) as i:
                    for par in range(2):
                        nxt(S_U + par, i)
                        act.wait_ge(strip_done, S + S_U + par + 2 * i + 3)
                        act.activation(v3(ut[:, :]), pset(par)[:, :, 0:CW], ACT.Copy).then_inc(freed(par), 1)
                        act.drain()
                        act.wait_ge(u_stored[par], 16 * (2 * l + i) + 16)
                        act.activation(ust[:, par, :, :], ut[:, 0:L].rearrange("p (j t) -> p t j", t=CT),
                                       ACT.Copy).then_inc(u_copied, 1)
                        act.wait_ge(u_copied, l * 4 + 2 * i + par + 1)
                        act.dma_start(ud[ds((2 * i + par) * P, P), :, :], ust[:, par, :, :]).then_inc(u_stored[par], 16)
                act.wait_ge(s5_e[0], l + 1)
                act.activation(T2p[:, 0:16], T1p[:, 64:80], ACT.Sin)
                act.activation(T1p[:, 112:128], T1p[:, 64:80], ACT.Abs)
                act.drain()
                act.activation(T2p[:, 16:32], T1p[:, 112:128], ACT.Sin, scale=-1.0, bias=float(np.pi / 2)).then_inc(s5_e[1], 1)
                with act.Fori(0, 5) as i:
                    for par in range(2):
                        nxt(S_Q + par, i)
                        act.wait_ge(strip_done, S + S_Q + par + 2 * i + 3)
                        act.wait_ge(rope_done, l * 10 + 2 * i + par + 1)
                        for qd in range(4):
                            o, r = 32 * qd, 32 * (qd ^ 1)
                            act.activation(v3(rot[o:o + 32, :]), pset(par)[r:r + 32, :, 0:CW], ACT.Copy).then_inc(rot_ready, 1)
                act.wait_ge(pool_init, l * 5 + 6)
                act.wait_ge(rope_done, l * 10 + 11)
                for sh in range(2):
                    for dh in range(2):
                        mm = act.activation(kst[HD * dh:HD * dh + HD, sh::2, 0:NMETA],
                                            kbuf[HD * sh:HD * sh + HD, :, 0:NMETA], ACT.Copy)
                mm.then_inc(stage_qk, 1)

                def stage(n):
                    act.activation(qst[:, :, :], QY[:, :, ds(NMETA + n * P, P)], ACT.Copy)
                    for sh in range(2):
                        for dh in range(2):
                            mm = act.activation(kst[HD * dh:HD * dh + HD, sh::2, 32:KEYS],
                                                kbuf[HD * sh:HD * sh + HD, :, ds(NMETA + n * P, 2 * P)], ACT.Copy)
                    mm.then_inc(stage_qk, 1)

                for k in range(2):
                    act.wait_ge(u_stored[k], 16 * (2 * l + 2) + 16)
                for par in range(2):
                    nxt(S_V + par, 0)
                    act.wait_ge(strip_done, S + S_V + par + 3)
                    act.activation(v3(vt[par][:, :]), pset(par)[:, :, 0:CW], ACT.Copy).then_inc(freed(par), 1)
                    if par == 0:
                        stage(0)
                for par in range(2):
                    act.wait_ge(v_tr, l * 2 + par + 1)
                    act.activation(Vb[:, 1:NBLK + 1, par * P:(par + 1) * P],
                                   PA[:, 0:2, :].rearrange("p c (n w) -> p (c n) w", n=4), ACT.Copy)
                    for g in range(4):
                        mm = act.activation(vmeta[32 * g:32 * g + NMETA, par * P:(par + 1) * P], PA[0:NMETA, 2, 0:P], ACT.Copy)
                    mm.then_inc(free_a, 1)

                pflat = s_sb[:, :, :].rearrange("p a b -> p (a b)")
                act.wait_ge(m0_done[1], l + 1)
                act.activation(pflat[0:NMETA, 0:256], pflat[0:NMETA, 0:256], ACT.Exp)
                act.activation(stat[0:NMETA, 5, :], stat[0:NMETA, 4, :], ACT.Exp).then_inc(m0_done[2], 1)
                act.wait_ge(m0_done[4], l + 1)
                act.activation(pt_sb[0:NMETA, 0, 0:2, :], PT[0][0:NMETA, 0:256].rearrange("p (a b) -> p a b", a=2),
                               ACT.Copy).then_inc(m0_done[5], 1)
                act.wait_ge(m0_done[6], l + 1)

                def s5_outputs(i):
                    b = l * NB + i
                    act.wait_ge(s5_out, b + 1)
                    for p in (2, 3, 0, 1):
                        g0 = 4 * (p % 2) + p // 2
                        mm = act.activation(Uch[:, g0:g0 + 3:2, :], BK4[p][:, 0:2 * NCH].rearrange(
                            "p (a b) -> p a b", a=2), ACT.Copy)
                    mm.then_inc(s5_out_ev, 1)
                    act.wait_ge(s5_out_ev, b + 1)
                    for t in range(CT):
                        act.dma_start(yd[ds(i * P, P), t, :].rearrange("(g c) j -> c g j", g=8),
                                      Uch[CG * t:CG * t + CG, :, :]).then_inc(y_stored, 16)

                def attention(i, first=False, last=False):
                    b = l * NB + i
                    for u8 in range(8):
                        kv = u8 % NKV
                        un = l * 32 + 8 * i + u8
                        act.wait_ge(m_ready, un + 1)
                        for g in range(4):
                            act.activation(s_sb[:, g, :], s_sb[:, g, :], ACT.Exp, bias=stat[:, 2, g:g + 1],
                                           accum_out=stat[:, 3, g:g + 1])
                        act.activation(stat[:, 5, 0:4], stat[:, 4, 0:4], ACT.Exp).then_inc(exp_done, 1)
                        if kv == NKV - 1 and not (last and u8 == 7):
                            act.wait_ge(scores_done, 4 * un + 4)
                            stage(2 * i + (u8 + 1) // NKV)
                        gi = u8 // 2
                        if u8 % 2 == 0:
                            w_high((S + S_G + gi + 4 * i + 1, S2 + S_G // 2 + (gi + 1) // 2 + 2 * i), (gi + 1) % 2)
                        else:
                            act.wait_ge(strip_done, S + S_G + gi + 4 * i + 3)
                            act.wait_ge(g_stored, 16 * (l * 16 + 4 * i + gi) + 16)
                            act.activation(v3(gst[:, :]), PA[:, :, 0:CW], ACT.Tanh, scale=0.5).then_inc(free_a, 1)
                            act.wait_ge(free_a, A + a_use(S_G) + gi + 4 * i + 2)
                            act.dma_start(gd[ds(4 * i + gi, 1), :, :].rearrange("o p w -> p (o w)"), gst[:, :]).then_inc(g_stored, 16)
                        if u8 == 0:
                            act.wait_ge(s5_pe, 3 * b + 1)
                            for ri in range(2):
                                for g2 in range(2):
                                    src = PS[0][NS * g2:NS * g2 + NS, ri * P:(ri + 1) * P].rearrange(
                                        "q (p g c) -> q p g c", p=4, g=2)[:, :, g2, :]
                                    mm = act.activation(Cc[NS * g2:NS * g2 + NS, :, ri, :], src, ACT.Copy,
                                                        scale=1.0 - 2.0 * ri)
                            mm.then_inc(s5_ev, 1)
                        elif u8 == 1 and not first:
                            s5_outputs(i - 1)
                        elif u8 == 3:
                            act.wait_ge(s5_pe, 3 * b + 2)
                            for hf in range(2):
                                act.activation(Gs[0:CG, hf::2, :],
                                               PT[hf][0:CG, :].rearrange("p (a b) -> p a b", a=4), ACT.Copy)
                            act.activation(Min[:, :, :, :].rearrange("q p r w -> q (p r w)").rearrange("q (c w) -> q c w", c=2),
                                           PB[:, 0:2, :], ACT.Copy).then_inc(s5_ev, 1)
                        elif u8 == 4:
                            act.wait_ge(s5_pe, 3 * b + 3)
                            for p in (2, 3, 0, 1):
                                mm = act.activation(St[:, p, :, 1:NCH + 1], BK4[p][:, 0:2 * NCH].rearrange(
                                    "p (a b) -> p a b", a=2), ACT.Copy)
                            mm.then_inc(s5_ev, 1)
                        if kv == 0:
                            act.wait_ge(pv_done, un + 1)
                            act.activation(vst[:, :, :], Vb[:, ds(2 * i + u8 // 4, 2), :], ACT.Copy)
                        act.wait_ge(tr_done, un + 2)
                        act.activation(pt_sb[:, 0, :, :], PT[0].rearrange("p (a b) -> p a b", a=4), ACT.Copy)
                        for g in range(4):
                            mm = act.activation(ptm_sb[32 * g:32 * g + 32, g, :], PO[32 * g:32 * g + 32, 256:384], ACT.Copy)
                        mm.then_inc(pt_act, 1)

                attention(0, first=True)
                with act.Fori(1, NB - 1) as i:
                    attention(i)
                attention(NB - 1, last=True)

                act.wait_ge(strip_done, S + 31 + 3)
                for k in range(KD):
                    act.wait_ge(y_out, l * 32 + 30 + k // 2)
                    act.activation(HH[:, k, :], QY[:, k, :], ACT.Copy).then_inc(ys_hi, 1)
                for par in range(2):
                    nxt(S_OA + par, 0)
                s5_outputs(NB - 1)

                def gelu(i):
                    act.wait_ge(yr_loaded, 64 * (l + 1))
                    act.activation(MT[:, 2, 0:L].rearrange("p (j t) -> p j t", t=CT),
                                   X[:, ds(i, 1), 0:L].rearrange("p o (t j) -> p (o j) t", t=CT), ACT.Square).then_inc(ge[0], 1)
                    act.wait_ge(ge[2], l * 4 + i + 1)
                    act.activation(MT[:, 3, 0:L], MT[:, 2, 0:L], ACT.Tanh, scale=0.7978845608028654).then_inc(ge[3], 1)
                    act.wait_ge(ev_f, l * EVF + i + 1)
                    act.activation(BL[:, ds(i, 1), :], X[:, ds(4 + i, 1), :], ACT.Copy, scale=0.5).then_inc(ev_hi, 1)

                with act.Fori(1, 4) as i:
                    for par in range(2):
                        nxt(S_OA + par, i)
                    gelu(i - 1)
                gelu(3)
                with act.Fori(0, 2) as i:
                    for par in range(2):
                        nxt(S_GLU + par, i, 4)
                        act.wait_ge(strip_done, S + S_GLU + par + 2 * i + 3)
                        act.activation(v3(MT[:, 2, :]), pset(par)[:, :, 0:CW], ACT.Tanh, scale=0.5,
                                       bias=bgluh[:, ds(l, 1), ds(2 * i + par, 1)].rearrange("p a b -> p (a b)")
                                       ).then_inc(freed(par), 1)
                        act.wait_ge(ev_f, l * EVF + 4 + 2 * i + par + 1)
                        act.activation(XR[:, ds(2 * i + par, 1), :], MT[:, 3:4, :], ACT.Copy, scale=0.25).then_inc(ev_hi, 1)
                with act.Fori(0, 4) as i:
                    for par in range(2):
                        nxt(S_OS + par, i, KD if par else 4)
                        act.wait_ge(ev_f, l * EVF + 8 + 2 * i + par + 1)
                        act.activation(BH[:, ds(2 * i + par, 1), :], MT[:, 3:4, :], ACT.Copy, scale=0.5).then_inc(ev_hi, 1)
                act.wait_ge(mg_ready, l * KD + KD)
                act.sem_inc(passed, 1)
                with act.Fori(0, 4) as i:
                    for par in range(2):
                        nxt(S_OUT + par, i)
                        act.wait_ge(strip_done, S + S_OUT + par + 2 * i + 3)
                        act.wait_ge(mix_acc, l * 16 + 2 * i + par + 1)
                        act.activation(v3(MT[:, 1, :]), pset(par)[:, :, 0:CW], ACT.Square).then_inc(mix_sq, 1)
                        act.activation(X[:, ds(2 * i + par, 1), :].rearrange("p o (c w) -> p (o c) w", c=NC3),
                                       pset(par)[:, :, 0:CW], ACT.Copy).then_inc(freed(par), 1)
                nxt(S_FF, 0)
                rsqrt0(stat_done, l * 2 + 1, PA)
                for k in range(KD):
                    act.wait_ge(x_ready, l * 16 + k + 2)
                    act.activation(HH[:, k, :], X[:, k, :], ACT.Identity,
                                   scale=gains[:, ds(l, 1), 2, k:k + 1].rearrange("p a b -> p (a b)")).then_inc(hx_hi, 1)
                    square(k, l * 16 + 8)
                    act.dma_start(xd[k], X[:, k, :]).then_inc(x_stored, 16)
                rsqrt0(sq_used, l * 16 + 8 + KD + 2, PB)

                def up_strip(q, par, i):
                    act.wait_ge(relu_done, l * 32 + q * 8 + 2 * i + par + 1)
                    act.wait_ge(hid_ready, l * 32 + q * 8 + 2 * i + par + 1)
                    act.activation(MT[:, 3, :], MT[:, 2, :], ACT.Square)
                    act.drain()
                    act.activation(BH[:, ds(2 * i + par, 1), :], MT[:, 3:4, :], ACT.Copy).then_inc(ev_hi, 1)

                def mlp(q, first=False, last=False):
                    if first:
                        up_strip(0, 0, 0)
                        nxt(S_FF + 1, 0)
                        up_strip(0, 1, 0)
                    with act.Fori(int(first), 4) as i:
                        for par in range(2):
                            nxt(S_FF + par, i + 8 * q)
                            up_strip(q, par, i)
                    with act.Fori(0, 4) as i:
                        for par in range(2):
                            nxt(S_FF + 8 + par, i + 8 * q)
                            if last:
                                t = 2 * i + par
                                if par == 0:
                                    act.wait_ge(free_a, A + a_use(S_FF + 8) + 8 * q + i + 2)
                                else:
                                    act.wait_ge(free_b, B + b_use(S_FF + 9) + 8 * q + i + 2)
                                act.wait_ge(mix_acc, l * 16 + 8 + t + 1)
                                act.activation(MT[:, 1:2, :], X[:, ds(t, 1), :], ACT.Square).then_inc(mix_sq, 1)

                mlp(0, first=True)
                with act.Fori(1, 3) as q:
                    mlp(q)
                mlp(3, last=True)
                rsqrt0(stat_done, l * 2 + 2, PA)
                for k in range(KD):
                    act.wait_ge(x_ready, l * 16 + 8 + k + 2)
                    square(k, l * 16 + 16)
                    act.dma_start(xd[k], X[:, k, :]).then_inc(x_stored, 16)

            for n in range(NBLK):
                act.wait_ge(out_tr, n + 1)
                if n >= 2:
                    act.wait_ge(out_stored[n % 2], 16 * (n // 2))
                ps, fr, u0 = (PA, free_a, DEPTH * A_PER + A_INIT) if n % 2 == 0 else (PB, free_b, DEPTH * B_PER + B_INIT)
                act.activation(OT[:, n % 2, :].rearrange("p (c w) -> p c w", c=2), ps[:, 0:2, :], ACT.Copy).then_inc(fr, 1)
                act.wait_ge(fr, u0 + n // 2 + 2)
                act.dma_start(out[n * P:(n + 1) * P, :], OT[:, n % 2, :]).then_inc(out_stored[n % 2], 16)
            for k in range(2):
                act.wait_ge(out_stored[k], 16 * (NBLK // 2))
            act.wait_ge(x_stored, 16 * (KD + 16 * DEPTH))
            act.wait_ge(g_stored, 16 * (16 * DEPTH) + 16)
            act.wait_ge(y_stored, 128 * NB * DEPTH + 128)
            for k in range(2):
                act.wait_ge(u_stored[k], 16 * 2 * DEPTH + 16)

        @block.vector
        def _(dve):
            dve.sem_inc(w_split, 2)
            dve.sem_inc(free_a, 1)
            dve.sem_inc(free_b, 1)
            dve.sem_inc(rope_done, 1)
            dve.sem_inc(stt_done, 2)
            dve.sem_inc(y_out, 1)
            dve.sem_inc(hid_ready, 1)
            dve.sem_inc(pv_done, 1)

            def w_low(s, par, ks=KD):
                dve.wait_ge(w_hi, s + 1)
                dve.tensor_tensor(WLO[:, par, 0:ks, :], WRAW[:, par, 0:ks, :], WHI[:, par, 0:ks, :].bitcast(F32),
                                  ALU.subtract).then_inc(w_split, 1)

            def split_low(lo, src, hi, scale, done):
                dve.scalar_tensor_tensor(out=lo, in0=src, scalar=scale, in1=hi.bitcast(F32), op0=ALU.mult,
                                         op1=ALU.subtract).then_inc(done, 1)

            w_low(0, 0)
            dve.wait_ge(const_loaded, 16 * 14)
            with dve.Fori(0, DEPTH) as l:
                S = l * STRIPS
                A, B = l * A_PER + A_INIT, l * B_PER + B_INIT

                def freed(s):
                    return free_a if a_use(s) is not None else free_b

                def rsqrt(ps, freed, r, rstd):
                    dve.wait_ge(ln_done, l * 4 + r + 1)
                    dve.tensor_scalar(v3(nv[:, :]), ps[:, :, 0:CW], 1.0 / D, EPS, ALU.mult, ALU.add).then_inc(freed, 1)
                    dve.drain()
                    dve.wait_ge(rs0_done, l * 4 + r + 1)
                    dve.scalar_tensor_tensor(out=nt[:, :], in0=nv[:, :], scalar=-0.5, in1=ny[:, :], op0=ALU.mult, op1=ALU.mult)
                    dve.drain()
                    dve.tensor_tensor(nt[:, :], nt[:, :], ny[:, :], ALU.mult)
                    dve.drain()
                    dve.scalar_tensor_tensor(out=rstd, in0=nt[:, :], scalar=1.5, in1=ny[:, :], op0=ALU.add, op1=ALU.mult)
                    dve.drain()

                def gain(i, k):
                    return gains[:, ds(l, 1), i, k:k + 1].rearrange("p a b -> p (a b)")

                def post_norm(j, gi, r, pre=None):
                    rsqrt(PA, free_a, r, rstd[:, :])
                    lag = 3
                    for k in range(KD + (lag if pre is not None else 0)):
                        if k < KD:
                            dve.scalar_tensor_tensor(out=X[:, k, :], in0=X[:, k, :], scalar=gain(gi, k), in1=rstd[:, :],
                                                     op0=ALU.mult, op1=ALU.mult).then_inc(post_scaled, 1)
                        if pre is not None and k >= lag:
                            t = k - lag
                            dve.wait_ge(hx_hi, l * 16 + 8 + t + 1)
                            split_low(HL[:, t, :], X[:, t, :], HH[:, t, :], gain(pre, t), h_ready)

                rsqrt(PA, free_a, 0, rstd[:, :])
                for k in range(KD + 1):
                    if k > 1:
                        dve.drain()
                    if k < KD:
                        dve.scalar_tensor_tensor(out=nx[:, k % 2, :], in0=X[:, k, :], scalar=gain(0, k), in1=rstd[:, :],
                                                 op0=ALU.mult, op1=ALU.mult).then_inc(hx_ready, 1)
                    if k > 0:
                        dve.wait_ge(hx_hi, l * 16 + k)
                        split_low(HL[:, k - 1, :], nx[:, (k - 1) % 2, :], HH[:, k - 1, :], 1.0, h_ready)
                with dve.Fori(0, 2) as i:
                    for par in range(2):
                        w_low(S + S_U + par + 1 + 2 * i, (par + 1) % 2)
                dve.wait_ge(tab_loaded, 64 * (l + 1))
                dve.sem_inc(passed, 1)

                def rope(par, i, s0, tile, dst):
                    w_low(S + s0 + par + 1 + 2 * i, (par + 1) % 2)
                    dve.drain()
                    dve.wait_ge(rot_ready, 4 * (l * 10 + tile + 1))
                    dve.tensor_tensor(v3(rt1[:, :]), pset(par)[:, :, 0:CW], v3(cosb[:, :]), ALU.mult).then_inc(freed(par), 1)
                    dve.tensor_tensor(rt2[:, :], rot[:, :], sinb[:, :], ALU.mult)
                    dve.drain()
                    for o, c0, c1 in dst:
                        mm = dve.tensor_tensor(o, rt1[:, c0:c1], rt2[:, c0:c1], ALU.add)
                    mm.then_inc(rope_done, 1)

                with dve.Fori(0, 4) as i:
                    for par in range(2):
                        rope(par, i, S_Q, 2 * i + par, [(QY[:, ds(2 * i + par, 1), :].rearrange("p o w -> p (o w)"), 0, LP)])
                dve.wait_ge(x_stored, 16 * (KD + 16 * l))
                for par in range(2):
                    rope(par, 0, S_K, 8 + par, [(kbuf[:, par, 0:NMETA], 0, NMETA), (kbuf[:, par, KOFF:], NMETA, L)])
                for par in range(2):
                    w_low(S + S_V + par + 1, (par + 1) % 2)

                pflat = s_sb[0:NMETA, :, :].rearrange("p a b -> p (a b)")[:, 0:256].rearrange("p (h k) -> p h k", h=NH)
                st0 = [stat[0:NMETA, r, :] for r in range(6)]
                sk0 = sink[0:NMETA, ds(l, 1), :].rearrange("p a b -> p (a b)")
                dve.wait_ge(m0_done[0], l + 1)
                dve.wait_ge(v_tr, 2 * l + 2)
                for e in range(2):
                    dve.scalar_tensor_tensor(out=pflat[:, e::2, :], in0=PS[e][0:NMETA, 0:P].rearrange("p (h k) -> p h k", h=NH // 2),
                                             scalar=SCALE, in1=mask0[0:NMETA, :].unsqueeze(1).to_broadcast([NMETA, NH // 2, NMETA]),
                                             op0=ALU.mult, op1=ALU.add)
                dve.drain()
                dve.tensor_reduce(st0[0], pflat, AX.X, ALU.max)
                dve.drain()
                dve.tensor_tensor(st0[1], st0[0], sk0, ALU.max)
                dve.drain()
                dve.tensor_tensor(pflat, pflat, st0[1].unsqueeze(2).to_broadcast([NMETA, NH, NMETA]), ALU.subtract)
                dve.tensor_tensor(st0[4], sk0, st0[1], ALU.subtract).then_inc(m0_done[1], 1)
                dve.wait_ge(m0_done[2], l + 1)
                dve.tensor_reduce(st0[3], pflat, AX.X, ALU.add)
                dve.drain()
                dve.tensor_tensor(st0[0], st0[3], st0[5], ALU.add)
                dve.drain()
                dve.reciprocal(st0[1], st0[0])
                dve.drain()
                dve.tensor_tensor(pflat, pflat, st0[1].unsqueeze(2).to_broadcast([NMETA, NH, NMETA]), ALU.mult).then_inc(m0_done[3], 1)
                dve.wait_ge(m0_done[6], l + 1)
                dve.tensor_copy(QY[:, :, 0:NMETA], PO[:, 0:P].rearrange("p (t q) -> p t q", t=KD)).then_inc(m0_done[7], 1)

                def y_store(un, kv, n):
                    dve.wait_ge(pv_done, un + 2)
                    dve.tensor_copy(QY[:, 2 * kv:2 * kv + 2, ds(NMETA + n * P, P)],
                                    PO[:, 0:256].rearrange("p (a b) -> p a b", a=2)).then_inc(y_out, 1)

                def attention(i, first=False):
                    for u8 in range(8):
                        kv = u8 % NKV
                        un = l * 32 + 8 * i + u8
                        mask = mask_cur if u8 < 4 else mask_rest
                        dve.wait_ge(tr_done, un + 1)
                        for g in range(4):
                            dve.wait_ge(scores_done, 4 * un + g + 1)
                            dve.scalar_tensor_tensor(out=s_sb[:, g, :], in0=PS[g % 2][:, 0:KEYS], scalar=SCALE,
                                                     in1=mask[:, :], op0=ALU.mult, op1=ALU.add).then_inc(stt_done, 1)
                        dve.drain()
                        dve.tensor_reduce(stat[:, 0, 0:4], s_sb[:, :, :], AX.X, ALU.max)
                        dve.drain()
                        sk = sink[:, ds(l, 1), 4 * kv:4 * kv + 4].rearrange("p a b -> p (a b)")
                        dve.tensor_tensor(stat[:, 1, 0:4], stat[:, 0, 0:4], sk, ALU.max)
                        dve.drain()
                        dve.tensor_scalar(stat[:, 2, 0:4], stat[:, 1, 0:4], -1.0, None, ALU.mult)
                        dve.tensor_tensor(stat[:, 4, 0:4], sk, stat[:, 1, 0:4], ALU.subtract).then_inc(m_ready, 1)
                        if u8 % 2 == 1:
                            gi = u8 // 2
                            w_low(S + S_G + gi + 4 * i + 1, (gi + 1) % 2)
                        if u8 == 3:
                            dve.tensor_copy(mask_cur[:, :], mask_rest[:, :])
                        dve.wait_ge(exp_done, un + 1)
                        dve.tensor_tensor(stat[:, 0, 0:4], stat[:, 3, 0:4], stat[:, 5, 0:4], ALU.add)
                        dve.drain()
                        dve.reciprocal(stat[:, 1, 0:4], stat[:, 0, 0:4])
                        dve.drain()
                        dve.tensor_tensor(pm_sb[:, :, :], s_sb[:, :, 0:32],
                                          stat[:, 1, 0:4].unsqueeze(2).to_broadcast([P, 4, 32]), ALU.mult)
                        for g in range(4):
                            mm = dve.tensor_scalar(s_sb[:, g, 32:KEYS], s_sb[:, g, 32:KEYS], stat[:, 1, g:g + 1], None, ALU.mult)
                        mm.then_inc(p_ready, 1)
                        if not (first and u8 == 0):
                            y_store(un - 1, (kv - 1) % NKV, 2 * i + (u8 - 1) // NKV)
                        dve.wait_ge(tr_done, un + 2)
                        dve.tensor_copy(pt_sb[:, 1, :, :], PT[1].rearrange("p (a b) -> p a b", a=4)).then_inc(pt_dve, 1)

                attention(0, first=True)
                with dve.Fori(1, NB) as i:
                    attention(i)
                y_store(l * 32 + 31, NKV - 1, NBLK - 1)

                with dve.Fori(0, KD) as k:
                    dve.wait_ge(ys_hi, l * KD + k + 1)
                    split_low(HL[:, ds(k, 1), :], QY[:, ds(k, 1), :], HH[:, ds(k, 1), :], 1.0, ys_ready)
                def m1(i):
                    for par in range(2):
                        w_low(S + S_OA + par + 1 + 2 * i, (par + 1) % 2)
                        t = 2 * i + par
                        dve.wait_ge(strip_done, S + S_OA + t + 3)
                        dve.wait_ge(gate_loaded[par], 16 * (l * 8 + i + 1))
                        dve.scalar_tensor_tensor(out=QY[:, ds(t, 1), :].rearrange("p o (c w) -> p (o c) w", c=NC3),
                                                 in0=v3(MT[:, par, :]), scalar=1.0, in1=pset(par)[:, :, 0:CW],
                                                 op0=ALU.add, op1=ALU.mult).then_inc(freed(par), 1)

                def gelu(i):
                    yr = X[:, ds(i, 1), 0:L].rearrange("p o (t j) -> p (o j) t", t=CT)
                    xz = X[:, ds(4 + i, 1), 0:L].rearrange("p o (j t) -> p (o j) t", t=CT)
                    tk = lambda t: t.rearrange("p (j t) -> p j t", t=CT)
                    dve.wait_ge(ge[0], l * 4 + i + 1)
                    dve.tensor_scalar(MT[:, 2, 0:L], MT[:, 2, 0:L], 0.044715, 1.0, ALU.mult, ALU.add)
                    dve.drain()
                    dve.tensor_tensor(tk(MT[:, 2, 0:L]), tk(MT[:, 2, 0:L]), yr, ALU.mult).then_inc(ge[2], 1)
                    dve.wait_ge(ge[3], l * 4 + i + 1)
                    dve.scalar_tensor_tensor(out=xz, in0=tk(MT[:, 3, 0:L]), scalar=1.0, in1=yr,
                                             op0=ALU.add, op1=ALU.mult).then_inc(ev_f, 1)
                    dve.wait_ge(ev_hi, l * EVH + i + 1)
                    split_low(BL[:, ds(4 + i, 1), :], X[:, ds(4 + i, 1), :], BL[:, ds(i, 1), :], 0.5, z_ready)

                m1(0)
                dve.memset(X[:, 4:8, L:LP], 0.0)
                with dve.Fori(1, 4) as i:
                    m1(i)
                    gelu(i - 1)
                gelu(3)
                with dve.Fori(0, 2) as i:
                    for par in range(2):
                        k = 2 * i + par
                        w_low(S + S_GLU + par + 1 + 2 * i, (par + 1) % 2, 4)
                        dve.drain()
                        if par == 0:
                            dve.wait_ge(free_a, A + a_use(S_GLU) + i + 2)
                        else:
                            dve.wait_ge(free_b, B + b_use(S_GLU + 1) + i + 2)
                        dve.scalar_tensor_tensor(out=MT[:, 3:4, :], in0=MT[:, 2:3, :], scalar=1.0, in1=X[:, ds(4 + k, 1), :],
                                                 op0=ALU.add, op1=ALU.mult).then_inc(ev_f, 1)
                        dve.wait_ge(ev_hi, l * EVH + 4 + k + 1)
                        split_low(XR[:, ds(4 + k, 1), :], MT[:, 3:4, :], XR[:, ds(k, 1), :], 0.25, z2_ready)
                with dve.Fori(0, 4) as i:
                    for par in range(2):
                        t = 2 * i + par
                        w_low(S + S_OS + par + 1 + 2 * i, (par + 1) % 2, KD if par else 4)
                        dve.wait_ge(strip_done, S + S_OS + t + 3)
                        dve.wait_ge(gate_loaded[par], 16 * (l * 8 + 4 + i + 1))
                        dve.scalar_tensor_tensor(out=v3(MT[:, 2, :]), in0=v3(MT[:, par, :]), scalar=1.0,
                                                 in1=pset(par)[:, :, 0:CW], op0=ALU.add, op1=ALU.mult).then_inc(freed(par), 1)
                        dve.drain()
                        dve.tensor_tensor(MT[:, 3:4, :], MT[:, 2:3, :], QY[:, ds(t, 1), :], ALU.add).then_inc(ev_f, 1)
                        dve.wait_ge(ev_hi, l * EVH + 8 + t + 1)
                        split_low(BL[:, ds(t, 1), :], MT[:, 3:4, :], BH[:, ds(t, 1), :], 0.5, mg_ready)
                with dve.Fori(0, 4) as i:
                    for par in range(2):
                        w_low(S + S_OUT + par + 1 + 2 * i, (par + 1) % 2)
                w_low(S + S_FF + 1, 1)
                post_norm(0, 1, 1, pre=2)
                rsqrt(PB, free_b, 2, MT[:, 0, :])

                def up_strip(q, par, i):
                    t = 2 * i + par
                    dve.wait_ge(strip_done, S + S_FF + t + 16 * q + 3)
                    dve.scalar_tensor_tensor(out=v3(MT[:, 2, :]), in0=pset(par)[:, :, 0:CW], scalar=0.0,
                                             in1=v3(MT[:, 0, :]), op0=ALU.max, op1=ALU.mult).then_inc(relu_done, 1)
                    dve.drain()
                    dve.sem_inc(freed(par), 1)
                    dve.wait_ge(ev_hi, l * EVH + 16 + q * 8 + t + 1)
                    split_low(BL[:, ds(t, 1), :], MT[:, 3:4, :], BH[:, ds(t, 1), :], 1.0, hid_ready)

                def mlp(q, first=False):
                    if first:
                        up_strip(0, 0, 0)
                        w_low(S + S_FF + 2, 0)
                        up_strip(0, 1, 0)
                    with dve.Fori(int(first), 4) as i:
                        for par in range(2):
                            w_low(S + S_FF + par + 1 + 2 * i + 16 * q, (par + 1) % 2)
                            up_strip(q, par, i)
                    dve.wait_ge(acc_done, l + 1)
                    dve.sem_inc(passed, 1)
                    with dve.Fori(0, 4) as i:
                        for par in range(2):
                            t = 2 * i + par
                            w_low(S + S_FF + 8 + par + 1 + 2 * i + 16 * q, (par + 1) % 2)
                            dve.wait_ge(strip_done, S + S_FF + 8 + t + 16 * q + 3)
                            xt = X[:, ds(t, 1), :].rearrange("p o (c w) -> p (o c) w", c=NC3)
                            dve.tensor_tensor(xt, xt, pset(par)[:, :, 0:CW], ALU.add).then_inc(freed(par), 1)

                mlp(0, first=True)
                with dve.Fori(1, 4) as q:
                    mlp(q)
                post_norm(1, 3, 3)

        @block.gpsimd
        def _(pool):
            def await_(s, v):
                pool.wait_ge(s, v)
                pool.sem_inc(passed, 1)

            pool.sem_inc(mix_acc, 1)
            pool.sem_inc(x_ready, 1)
            pool.sem_inc(y_stored, 128)
            pool.memset(ones[:, :], 1.0)
            pool.memset(X[:, :, L:LP], 0.0)
            pool.drain()
            pool.sem_inc(pool_init, 1)
            def tt(o, a, b, op):
                return pool.tensor_tensor(o, a, b, op)

            def cmul(o, x, re_b, im_b, t1, t2, op=ALU.subtract):
                tt(t1, x, re_b, ALU.mult)
                tt(t2, x, im_b, ALU.mult)
                pool.drain()
                return tt(o, t1, t2[:, :, ::-1] if len(t2.shape) == 3 else t2[:, :, ::-1, :], op)

            with pool.Fori(0, DEPTH) as l:
                await_(h_ready, l * 16 + 8)
                await_(x_stored, 16 * (KD + 16 * l))
                pool.memset(kbuf[:, :, NMETA:KOFF], 0.0).then_inc(pool_init, 1)
                pool.memset(kst[:, :, :], 0.0).then_inc(pool_init, 1)
                pool.memset(Vb[:, 0, :], 0.0).then_inc(pool_init, 1)
                pool.memset(vmeta[:, :], 0.0).then_inc(pool_init, 1)
                pool.memset(ptm_sb[:, :, :], 0.0).then_inc(pool_init, 1)
                c16 = lambda t, i: t[:, 16 * i:16 * i + 16]
                are, aim, ldt, er, th, kk, u1, u2 = (c16(T1p, i) for i in range(8))
                sn, cs, mag, inv, nr, v1, v2, v3_ = (c16(T2p, i) for i in range(8))
                for t, v in ((are, a_pn[0]), (aim, a_pn[1])):
                    pool.dma_start(t, v[ds(l, 1), :, :].rearrange("o q p -> (o q) p"), allow_slow_non_contiguous=True).then_inc(s5_coef, 16)
                for g2 in range(2):
                    pool.dma_start(ldt[NS * g2:NS * g2 + NS, :], dt_v[ds(l, 1), g2, :].to_broadcast([NS, NP]), allow_slow_non_contiguous=True).then_inc(s5_coef, 16)
                await_(s5_coef, 64 * (l + 1))
                pool.memset(u1, float(np.e))
                pool.drain()
                tt(u2, u1, ldt, ALU.pow)
                pool.drain()
                tt(er, are, u2, ALU.mult)
                pool.drain()
                tt(th, aim, u2, ALU.mult)
                pool.drain()
                tt(mag, u1, er, ALU.pow)
                pool.drain()
                pool.tensor_scalar(kk, th, 1.0 / (2 * np.pi), 12582912.0, ALU.mult, ALU.add)
                pool.drain()
                pool.tensor_scalar(kk, kk, -12582912.0, None, ALU.add)
                pool.drain()
                for c in (6.28125, 0.0019340515136718750, 1.2556660464e-06):
                    pool.tensor_scalar(u2, kk, -c, None, ALU.mult)
                    pool.drain()
                    tt(th, th, u2, ALU.add)
                    pool.drain()
                pool.tensor_scalar(th, th, 3.1415925, -3.1415925, ALU.min, ALU.max)
                pool.drain()
                pool.sem_inc(s5_e[0], 1)
                await_(s5_e[1], l + 1)
                A1, A1s = PW[:, 1, :, :], PWs[:, 1, :, :]
                tt(A1[:, :, 0], mag, cs, ALU.mult)
                pool.drain()
                tt(A1[:, :, 1], mag, sn, ALU.mult)
                pool.drain()
                pool.memset(PW[:, 0, :, 0], 1.0)
                pool.drain()
                pool.memset(PW[:, 0, :, 1], 0.0)
                pool.drain()

                def partners(dst, src, lo, hi):
                    pool.tensor_scalar(dst[:, lo:hi, :, 0], src[:, lo:hi, :, 1], -1.0, 0.0, ALU.mult, ALU.add)
                    pool.drain()
                    pool.tensor_scalar(dst[:, lo:hi, :, 1], src[:, lo:hi, :, 1], 1.0, 0.0, ALU.mult, ALU.add)
                    pool.drain()

                q1 = T1p[:, 64:96].rearrange("p (a b) -> p a b", b=2)
                q2 = T1p[:, 96:128].rearrange("p (a b) -> p a b", b=2)
                partners(PWs, PW, 0, 2)
                re1 = PW[:, 1, :, 0:1].to_broadcast([P, NP, 2])
                for t in range(2, CT + 1):
                    cmul(PW[:, t, :, :], PW[:, t - 1, :, :], re1, A1s, q1, q2)
                    pool.drain()
                partners(PWs, PW, 2, CT + 1)
                tt(P8[:, 1, :, :], PW[:, CT, :, :], PW[:, 0, :, 0:1].to_broadcast([P, NP, 2]), ALU.mult)
                pool.drain()
                partners(P8s, P8, 1, 2)
                re8 = P8[:, 1, :, 0:1].to_broadcast([P, NP, 2])
                for t in range(2, RUN + 1):
                    cmul(P8[:, t, :, :], P8[:, t - 1, :, :], re8, P8s[:, 1, :, :], q1, q2)
                    pool.drain()
                partners(P8s, P8, 2, RUN + 1)
                pool.tensor_scalar(nr, A1[:, :, 0], -1.0, None, ALU.add)
                pool.drain()
                tt(v1, are, are, ALU.mult)
                pool.drain()
                tt(v2, aim, aim, ALU.mult)
                pool.drain()
                tt(v1, v1, v2, ALU.add)
                pool.drain()
                pool.memset(v2, -1.0)
                pool.drain()
                tt(inv, v1, v2, ALU.pow)
                pool.drain()
                tt(v1, nr, are, ALU.mult)
                pool.drain()
                tt(v2, A1[:, :, 1], aim, ALU.mult)
                pool.drain()
                tt(v1, v1, v2, ALU.add)
                pool.drain()
                tt(v2, nr, aim, ALU.mult)
                pool.drain()
                tt(v3_, A1[:, :, 1], are, ALU.mult)
                pool.drain()
                tt(v3_, v3_, v2, ALU.subtract)
                pool.drain()
                tt(FB[:, :, 0], v1, inv, ALU.mult)
                pool.drain()
                tt(FB[:, :, 1], v3_, inv, ALU.mult)
                pool.drain()
                pool.tensor_scalar(FBs[:, :, 0], FB[:, :, 1], -1.0, 0.0, ALU.mult, ALU.add)
                pool.drain()
                pool.tensor_scalar(FBs[:, :, 1], FB[:, :, 1], 1.0, 0.0, ALU.mult, ALU.add)
                pool.drain()
                await_(rope_done, l * 10 + 11)
                for k in range(2):
                    await_(u_stored[k], 16 * (2 * l + 2) + 16)
                pool.memset(Mtoe[:, :, :], 0.0)
                pool.memset(St[:, :, :, 0], 0.0)
                pool.drain()
                t1 = T1p[:, :].rearrange("p (a i c) -> p a i c", a=4, i=2)
                t2 = T2p[:, :].rearrange("p (a i c) -> p a i c", a=4, i=2)

                def rb(tab, n):
                    return tab[:, :, 0:1].to_broadcast([P, 4, 2]).unsqueeze(3).to_broadcast([P, 4, 2, n])

                def ib(tab, n):
                    return tab.unsqueeze(3).to_broadcast([P, 4, 2, n])

                def input_matrices(i):
                    b, pr = l * NB + i, ds(4 * i, 4)
                    await_(b_loaded, 112 * (b + 1))
                    cmul(BB[:, :, :, :], Bx[:, :, :, :], rb(FB[:, pr, :], CG), ib(FBs[:, pr, :], CG), t1, t2)
                    pool.drain()
                    for t in range(CT):
                        e = CT - 1 - t
                        cmul(MinT[:, :, :, CG * t:CG * t + CG], BB[:, :, :, :], rb(PW[:, e, pr, :], CG),
                             ib(PWs[:, e, pr, :], CG), t1, t2)
                        pool.drain()
                    pool.sem_inc(s5_min, 1)

                def batch(i):
                    b, pr = l * NB + i, ds(4 * i, 4)
                    await_(s5_ev, 3 * b + 1)
                    if not isinstance(i, int) or i > 0:
                        await_(s5_out, b)
                    for t in range(CT + 1):
                        cmul(W9[:, :, :, CG * t:CG * t + CG], Cc[:, :, :, :], rb(PW[:, t, pr, :], CG),
                             ib(PWs[:, t, pr, :], CG), t1, t2, ALU.add)
                        pool.drain()
                    pool.sem_inc(s5_w, 1)
                    await_(s5_ev, 3 * b + 2)
                    tg = T1p[0:CG, :].rearrange("p (g c) -> p g c", g=8)
                    tt(tg, dsk[0:CG, :].unsqueeze(2).to_broadcast([CG, 8, CG]),
                       ident[0:CG, 0:CG].unsqueeze(1).to_broadcast([CG, 8, CG]), ALU.mult)
                    pool.drain()
                    tt(Gs[0:CG, :, 0:CG], Gs[0:CG, :, 0:CG], tg, ALU.add).then_inc(s5_g, 1)
                    pool.drain()
                    await_(s5_ev, 3 * b + 3)
                    sv = St[:, :, :, 1:NCH + 1].rearrange("q p i (s r) -> q p i s r", s=SEG)

                    def at_r(r, s0, s1):
                        return sv[:, :, :, s0:s1, r].rearrange("q p i s o -> q p i (s o)")

                    def step(dst, src, k, n):
                        a1 = T1p[:, 0:8 * n].rearrange("p (a i c) -> p a i c", a=4, i=2)
                        a2 = T2p[:, 0:8 * n].rearrange("p (a i c) -> p a i c", a=4, i=2)
                        tab, tabs = P8[:, k, pr, :].rearrange("p o a i -> p (o a) i"), P8s[:, k, pr, :].rearrange("p o a i -> p (o a) i")
                        tt(a1, src, rb(tab, n), ALU.mult)
                        tt(a2, src, ib(tabs, n), ALU.mult)
                        pool.drain()
                        tt(a1, a1, a2[:, :, ::-1, :], ALU.subtract)
                        pool.drain()
                        tt(dst, dst, a1, ALU.add)
                        pool.drain()

                    with pool.Fori(0, (RUN - 1) // 3) as r3:
                        for k in range(1, 4):
                            step(at_r(ds(3 * r3 + k, 1), 0, SEG), at_r(ds(3 * r3 + k - 1, 1), 0, SEG), ds(1, 1), SEG)
                    with pool.Fori(0, (SEG - 1) // 3) as s3:
                        ends = sv[:, :, :, :, RUN - 1]
                        for k in range(1, 4):
                            step(ends[:, :, :, ds(3 * s3 + k, 1)], ends[:, :, :, ds(3 * s3 + k - 1, 1)], ds(RUN, 1), 1)
                    with pool.Fori(0, (RUN - 1) // 3) as r3:
                        for k in range(3):
                            step(at_r(ds(3 * r3 + k, 1), 1, SEG), at_r(ds(RUN - 1, 1), 0, SEG - 1), ds(3 * r3 + k + 1, 1), SEG - 1)
                    pool.sem_inc(s5_scan, 1)

                input_matrices(0)
                with pool.Fori(0, NB - 1) as i:
                    batch(i)
                    await_(toe_loaded, 128 * (l * NB + i + 1))
                    input_matrices(i + 1)
                batch(NB - 1)

                def gate(t, par):
                    pool.dma_start(MT[:, par:par + 1, :], gd[ds(t, 1), :, :].rearrange("o p w -> p o w")).then_inc(gate_loaded[par], 16)

                A, B = l * A_PER + A_INIT, l * B_PER + B_INIT
                await_(y_out, l * 32 + 33)
                await_(g_stored, 16 * 16 * (l + 1) + 16)
                for par in range(2):
                    gate(8 + par, par)
                await_(y_stored, 128 * NB * (l + 1) + 128)
                for k in range(4):
                    pool.dma_start(X[:, k, 0:L], yd[k * P:(k + 1) * P, :, :].rearrange("c t j -> c (t j)")).then_inc(yr_loaded, 16)
                with pool.Fori(1, 4) as i:
                    for par in range(2):
                        await_(free_a if par == 0 else free_b,
                                     (A + a_use(S_OA) if par == 0 else B + b_use(S_OA + 1)) + i + 1)
                        gate(8 + 2 * i + par, par)
                for par in range(2):
                    await_(free_a if par == 0 else free_b,
                                 (A + a_use(S_OA) if par == 0 else B + b_use(S_OA + 1)) + 4 + 1)
                    gate(par, par)
                with pool.Fori(1, 4) as i:
                    for par in range(2):
                        await_(free_a if par == 0 else free_b,
                                     (A + a_use(S_OS) if par == 0 else B + b_use(S_OS + 1)) + i + 1)
                        gate(2 * i + par, par)
                await_(mg_ready, l * KD + KD)
                for j in range(2):
                    if j == 1:
                        await_(h_ready, l * 16 + 16)
                        await_(sq_ready, l * 16 + 16)
                        await_(x_stored, 16 * (2 * KD + 16 * l))
                        pool.memset(X[:, :, :], 0.0).then_inc(acc_done, 1)
                        await_(relu_done, l * 32 + 32)
                    pool.memset(MT[:, 0, :], 0.0)
                    pool.drain()
                    with pool.Fori(0, KD) as t:
                        await_(mix_sq, l * 16 + 8 * j + t + 1)
                        tt(MT[:, 0, :], MT[:, 0, :], MT[:, 1, :], ALU.add).then_inc(mix_acc, 1)
                        pool.drain()
                    for k in range(KD):
                        await_(xo_loaded, 16 * (l * 16 + j * 8 + k + 1))
                        await_(post_scaled, l * 16 + j * 8 + k + 1)
                        tt(X[:, k, :], X[:, k, :], XO[:, k, :], ALU.add).then_inc(x_ready, 1)


_INS = ["x", "meta_tokens", "norm_mix_pre", "norm_mix_post", "norm_mlp_pre", "norm_mlp_post", "w_in", "ssm_a_re",
        "ssm_a_im", "ssm_log_dt", "ssm_b_re", "ssm_b_im", "ssm_c_re", "ssm_c_im", "ssm_d", "w_glu", "b_glu",
        "attn_sinks", "w_o_ssm", "w_o_attn", "w_out", "w_up", "w_down"]


def shape_constants():
    inv = (1.0 / (10000.0 ** (np.arange(0, HD, 2, dtype=np.float32) / HD))).astype(np.float32)
    ang = np.arange(L, dtype=np.float32)[None, :] * inv[:, None]
    cos, sin = np.zeros((P, LP), np.float32), np.zeros((P, LP), np.float32)
    cos[:, :L] = np.tile(np.cos(ang), (4, 1))
    sin[:, :L] = np.concatenate([-np.sin(ang), np.sin(ang)] * 2, 0)
    q, k = np.arange(P)[:, None], np.arange(P)[None, :]
    mask = np.full((2, P, KEYS), NEG, np.float32)
    mask[:, :, 0:NMETA] = 0.0
    mask[1, :, 32:160] = np.where(k > q, 0.0, NEG)
    mask[:, :, 160:288] = np.where(k <= q, 0.0, NEG)
    m0 = np.where(np.arange(NMETA)[None, :] <= np.arange(NMETA)[:, None], 0.0, NEG).astype(np.float32)
    return {"cos_t": cos, "sin_t": sin, "mask_t": mask, "mask0_t": m0, "ident_t": np.eye(P, dtype=np.float32)}


def kernel(**inputs):
    import concourse.bacc as bacc
    from concourse.bass_utils import run_bass_kernel_spmd

    nc = bacc.Bacc("TRN2", target_bir_lowering=False, num_devices=1)
    arrays, aps = {}, {}
    named = {n: np.ascontiguousarray(inputs[n]) for n in _INS}
    named["x"] = named["x"].reshape(SEQ, D)
    named.update(shape_constants())
    for n, a in named.items():
        arrays[f"in_{n}"] = a
        aps[n] = nc.dram_tensor(f"in_{n}", a.shape, mybir.dt.from_np(a.dtype), kind="ExternalInput").ap()
    out = nc.dram_tensor("out_dram", (SEQ, D), F32, kind="ExternalOutput").ap()
    g = aps
    build(nc, g["x"], g["meta_tokens"],
          [g["norm_mix_pre"], g["norm_mix_post"], g["norm_mlp_pre"], g["norm_mlp_post"]], g["w_in"], g["ssm_a_re"],
          g["ssm_a_im"], g["ssm_log_dt"], g["ssm_b_re"], g["ssm_b_im"], g["ssm_c_re"], g["ssm_c_im"], g["ssm_d"],
          g["w_glu"], g["b_glu"], g["attn_sinks"], g["w_o_ssm"], g["w_o_attn"], g["w_out"], g["w_up"], g["w_down"],
          g["cos_t"], g["sin_t"], g["mask_t"], g["mask0_t"], g["ident_t"], out)
    r = run_bass_kernel_spmd(nc, [arrays], core_ids=[0])
    return r.results[0]["out_dram"].reshape(1, SEQ, D)
```

```python
from contextlib import ExitStack

import numpy as np
import concourse.bass as bass
from concourse import mybir

P = 128
D = 1024
SEQ = 1024
NMETA = 16
DEPTH = 2
KD = D // P
L = SEQ + NMETA
NC3 = 3
CW = 348
LP = NC3 * CW
NBLK = SEQ // P
NH = 16
NKV = 4
HD = 64
G_S = 32
CG = 16
NS = 64
NP = G_S // 2
CT = 8
NCH = L // CT
SEG, RUN = 13, 10
assert SEG * RUN == NCH and (SEG - 1) % 3 == 0 and (RUN - 1) % 3 == 0
NB = 4
DFF = 4 * D
EPS = 1e-6
SCALE = HD ** -0.5
KEYS = 288
KOFF = 144
NEG = -1e30

S_U, S_Q, S_K, S_V, S_G = 0, 4, 12, 14, 16
S_OA, S_GLU, S_OS, S_OUT, S_FF = 32, 40, 44, 52, 60
STRIPS = 124
A_PER, B_PER = 75, 55
A_INIT, B_INIT = 4, 4

F32 = mybir.dt.float32
F32R = mybir.dt.float32r
ALU = mybir.AluOpType
ACT = mybir.ActivationFunctionType
AX = mybir.AxisListType
ds = bass.ds


def a_use(s):
    if s < 16:
        return 1 + s // 2 if s % 2 == 0 else None
    if s < 32:
        return 11 + s - 16
    if s < 60:
        return 27 + (s - 32) // 2 if s % 2 == 0 else None
    return 42 + (s - 60) // 2 if s % 2 == 0 else None


def b_use(s):
    if s < 16:
        return (s - 1) // 2
    if s < 60:
        return 8 + (s - 33) // 2
    return 23 + (s - 61) // 2


BY_DVE, BY_POOL = (3, 5, 7), (0, 1, 2, 4, 6)
EVF, EVH = 16, 48
A_PRE1, A_VT, A_POST1, B_PRE2, A_POST2 = 0, 9, 41, 22, 74


def build(nc, x, meta, norms, w_in, a_re, a_im, log_dt, b_re, b_im, c_re, c_im, d_skip, w_glu, b_glu, sinks,
          w_o_ssm, w_o_attn, w_out, w_up, w_down, cos_t, sin_t, mask_t, mask0_t, ident_t, out):
    with ExitStack() as ctx:
        base = (nc.sbuf_base + 31) // 32 * 32

        def at(name, shape, off, dt=F32):
            return nc.alloc_sbuf_tensor_at(name, shape, dt, offset=base + 4 * off, align_bytes=4)

        TL = KD * LP
        HH, HL = at("h_hi", [P, KD, LP], 0, F32R), at("h_lo", [P, KD, LP], TL, F32R)
        XO = at("x_old", [P, KD, LP], TL)
        BH, BL = at("b_hi", [P, KD, LP], 2 * TL, F32R), at("b_lo", [P, KD, LP], 3 * TL, F32R)
        X, XR = at("x_res", [P, KD, LP], 4 * TL), at("z2_split", [P, KD, LP], 4 * TL, F32R)
        WRAW = at("w_raw", [P, 2, KD, P], 5 * TL)
        WHI, WLO = at("w_hi", [P, 2, KD, P], 5 * TL + 2048, F32R), at("w_lo", [P, 2, KD, P], 5 * TL + 4096, F32R)
        M0 = 5 * TL + 6144
        ident = at("ident", [P, P], M0)
        ones = at("ones", [P, P], M0 + 128)
        gains = at("gains", [P, DEPTH, 4, KD], M0 + 256)
        bglu = at("bglu", [P, DEPTH, 4], M0 + 320)
        sink = at("sink", [P, DEPTH, NH], M0 + 328)
        mask0 = at("mask0", [P, NMETA], M0 + 360)
        bgluh = at("bgluh", [P, DEPTH, 4], M0 + 376)
        stat = at("att_stat", [P, 6, NH], M0 + 384)
        M1 = M0 + 480
        MT = at("m_tiles", [P, 4, LP], M1)
        s_sb = at("s_sb", [P, 4, KEYS], M1)
        mask_cur = at("mask_cur", [P, KEYS], M1 + 1152)
        mask_rest = at("mask_rest", [P, KEYS], M1 + 1440)
        pt_sb = at("pt_sb", [P, 2, 4, P], M1 + 1728)
        m0p = pt_sb[:, 1, 0:2, :].rearrange("p a b -> p (a b)")
        nsink = at("neg_sink", [P, NH], M1 + 3680)
        PW = at("pw", [P, CT + 1, NP, 2], M1 + 2752)
        PWs = at("pw_s", [P, CT + 1, NP, 2], M1 + 3040)
        P8 = at("p8", [P, RUN + 1, NP, 2], M1 + 3328)
        P8s = at("p8_s", [P, RUN + 1, NP, 2], M1 + 3776)
        FB = at("f_b", [P, NP, 2], M1 + 4224)
        FBs = at("f_bs", [P, NP, 2], M1 + 4256)
        BB = at("b_bar", [P, 4, 2, CG], M1 + 4288)
        T1p = at("pool_t1", [P, P], M1 + 4416)
        T2p = at("pool_t2", [P, P], M1 + 4544)
        pm_sb = at("pm_sb", [P, 4, 32], M1 + 4672)
        assert M0 + 480 + 4800 <= (nc.sbuf_usable_end - base) // 4 - 8, (M1 + 4672, nc.sbuf_usable_end - base)
        QY = at("qy", [P, KD, LP], 2 * TL)
        R1 = 3 * TL
        cosb, sinb = at("cosb", [P, LP], R1), at("sinb", [P, LP], R1 + LP)
        rot = at("rot", [P, LP], R1 + 2 * LP)
        rt1, rt2 = at("rt1", [P, LP], R1 + 3 * LP), at("rt2", [P, LP], R1 + 4 * LP)
        ut = at("u_tok", [P, LP], R1 + 5 * LP)
        ust = at("u_stage", [P, 2, CT, NCH], R1 + 6 * LP)
        Uch = at("u_chunk", [P, 8, NCH], R1)
        St = at("s5_state", [P, 4, 2, NCH + 1], R1 + 1040)
        MinT = at("m_in_t", [P, 4, 2, CT * CG], R1 + 2088)
        Min = at("m_in", [P, 4, 2, P], R1 + 3112)
        Mtoe = at("m_toe", [P, 8, P], R1 + 4136)
        W9 = at("w9", [P, 4, 2, (CT + 1) * CG], R1 + 5160)
        dsk = at("d_skip", [P, 8], R1 + 6312)
        Gs = at("g_small", [P, 8, P], R1 + 2088)
        nv, ny, nt, rstd = (at(f"n_{k}", [P, LP], 2 * TL + i * LP) for i, k in enumerate(("v", "y", "t", "rstd")))
        sqr = at("sq_ring", [P, 2, LP], 2 * TL + 4 * LP)
        nx = at("n_x", [P, 2, LP], 2 * TL + 6 * LP)
        R2 = 4 * TL
        kbuf = at("kbuf", [P, 2, KOFF + SEQ], R2)
        Vb = at("vb", [P, NBLK + 1, 256], R2 + 2336)
        vmeta = at("vmeta", [P, 256], R2 + 4640)
        kst = at("kst", [P, NKV, KEYS], R2 + 4896)
        qst = at("qst", [P, KD, P], R2 + 6048)
        vst = at("vst", [P, 2, 256], R2 + 7072)
        ptm_sb = at("ptm_sb", [P, 4, P], R2 + 7584)
        Bx = at("b_raw", [P, 4, 2, CG], R2 + 8096)
        Cc = at("c_conj", [P, 4, 2, CG], R2 + 8224)
        gst = at("gate_stage", [P, LP], R1 + 6320)
        Craw = at("c_raw", [P, 2, P], R1 + 7364)
        vt = [at("v_feat0", [P, LP], R1 + 6320), at("v_feat1", [P, LP], M1)]
        XT = at("x_tok", [P, NBLK + 1, D], 0)
        rowsq = at("row_squares", [P, NBLK + 1], M0 + 384)
        diag = at("row_diag", [P, NBLK + 1, P], 3 * TL)
        junk = at("squares_unused", [P, D], 3 * TL + 1152)
        OT = at("o_tok", [P, NBLK, D], 0)

        PA = ctx.enter_context(nc.psum_tensor("ps_a", [P, 3, 512], F32))
        PB = ctx.enter_context(nc.psum_tensor("ps_b", [P, 3, 512], F32))
        PC = ctx.enter_context(nc.psum_tensor("ps_c", [P, 2, 512], F32))
        PS = [PB[:, 0, :], PB[:, 1, :]]
        PT = [PB[:, 2, :], PC[:, 0, :]]
        PO = PC[:, 1, :]
        BK4 = [PB[:, 0, :], PB[:, 1, :], PB[:, 2, :], PC[:, 0, :]]

        def dram(name, shape):
            return nc.dram_tensor(name, shape, F32, kind="Internal").ap()

        xd = dram("x_spill", (KD, P, LP))
        gd = dram("gate_spill", (16, P, LP))
        ud = dram("u_spill", (512, CT, NCH))
        yd = dram("y_spill", (512, CT, NCH))

        def sem(name):
            return ctx.enter_context(nc.semaphore(name))

        const_loaded = sem("const_loaded")
        ident_loaded = sem("ident_loaded")
        xtok_loaded = [sem(f"xtok_loaded{n}") for n in range(NBLK + 1)]
        w_loaded = [sem("w_loaded0"), sem("w_loaded1")]
        w_hi = sem("w_hi")
        w_split = sem("w_split")
        strip_done = sem("strip_done")
        free_a = sem("free_a")
        free_b = sem("free_b")
        init_tr = sem("init_tr")
        rows_sq = sem("rows_sq")
        diag_ready = sem("diag_ready")
        x_ready = sem("x_ready")
        x_ready_v = sem("x_ready_v")
        sq_ready = sem("sq_ready")
        sq_used = sem("sq_used")
        stat_done = sem("stat_done")
        var_done = sem("var_done")
        ln_done = sem("ln_done")
        rs0_done = sem("rs0_done")
        hx_ready = sem("hx_ready")
        hx_hi = sem("hx_hi")
        h_ready = sem("h_ready")
        mix_sq = sem("mix_sq")
        mix_acc = sem("mix_acc")
        xo_loaded = sem("xo_loaded")
        post_scaled = sem("post_scaled")
        x_stored = sem("x_stored")
        tab_loaded = sem("tab_loaded")
        u_copied = sem("u_copied")
        u_stored = [sem("u_stored0"), sem("u_stored1")]
        rot_ready = sem("rot_ready")
        rope_done = sem("rope_done")
        pool_init = sem("pool_init")
        v_tr = sem("v_tr")
        stage_qk = sem("stage_qk")
        scores_done = sem("scores_done")
        stt_done = sem("stt_done")
        m_ready = sem("m_ready")
        sink_ready = sem("sink_ready")
        exp_done = sem("exp_done")
        p_ready = sem("p_ready")
        tr_done = sem("tr_done")
        pt_act = sem("pt_act")
        pt_dve = sem("pt_dve")
        pv_done = sem("pv_done")
        y_out = sem("y_out")
        m0_done = [sem(f"meta_{k}") for k in ("scores", "max", "exp", "p", "tr", "pt", "pv", "y")]
        g_stored = sem("g_stored")
        s5_coef = sem("s5_coef")
        s5_e = [sem(f"s5_e{i}") for i in range(6)]
        b_loaded = sem("b_loaded")
        s5_min = sem("s5_min")
        s5_w = sem("s5_w")
        s5_cc = sem("s5_cc")
        s5_pe = sem("s5_pe")
        s5_ev = sem("s5_ev")
        s5_out = sem("s5_out")
        s5_out_ev = sem("s5_out_ev")
        s5_g = sem("s5_g")
        toe_loaded = sem("toe_loaded")
        u_loaded = sem("u_loaded")
        s5_scan = sem("s5_scan")
        y_stored = sem("y_stored")
        yr_loaded = sem("yr_loaded")
        ys_hi = sem("ys_hi")
        ys_ready = sem("ys_ready")
        ge = [sem(f"gelu_{i}") for i in range(3)]
        z_ready = sem("z_ready")
        gate_loaded = [sem("gate_loaded0"), sem("gate_loaded1")]
        gate_used = sem("gate_used")
        ev_t = sem("ev_t")
        ev_f = sem("ev_f")
        ev_hi = sem("ev_hi")
        z2_ready = sem("z2_ready")
        mg_ready = sem("mg_ready")
        hid_ready = sem("hid_ready")
        relu_done = sem("relu_done")
        acc_done = sem("acc_done")
        passed = sem("passed")
        out_tr = sem("out_tr")
        out_stored = [sem("out_stored0"), sem("out_stored1")]

        block = ctx.enter_context(nc.Block())
        W = dict(
            w_in=w_in.rearrange("l r c -> (l r) c"), w_oa=w_o_attn.rearrange("l r c -> (l r) c"),
            w_os=w_o_ssm.rearrange("l r c -> (l r) c"), w_glu=w_glu.rearrange("l r c -> (l r) c"),
            w_out=w_out.rearrange("l r c -> (l r) c"), w_up=w_up.rearrange("l r c -> (l r) c"),
            w_down=w_down.rearrange("l r c -> (l r) c"))

        a_pn = [a.rearrange("l (p g) n -> l (g n) p", g=2) for a in (a_re, a_im)]
        dt_v = log_dt.rearrange("l (p g) -> l g p", g=2)
        b_v = [t.rearrange("l (k p g) n c -> (l k) (g n) p c", k=NB, g=2) for t in (b_re, b_im)]
        c_v = [t.rearrange("l (k g) c n -> (l k) (g c) n", k=NB) for t in (c_re, c_im)]
        d_v = d_skip.rearrange("l (k g) c -> (l k) c g", k=NB)

        def v3(t):
            return t.rearrange("p (c w) -> p c w", c=NC3)

        def pset(s):
            return PA if a_use(s) is not None else PB

        @block.sync
        def _(sp):
            sp.dma_start(ident[:, :], ident_t).then_inc(ident_loaded, 16)
            sp.dma_start(XT[0:NMETA, 0, :], meta).then_inc(xtok_loaded[0], 16)
            for n in range(NBLK):
                sp.dma_start(XT[:, n + 1, :], x[n * P:(n + 1) * P, :]).then_inc(xtok_loaded[n + 1], 16)
            for l in range(DEPTH):
                for i in range(4):
                    sp.dma_start(gains[:, l, i, :], norms[i][l].rearrange("(k p) -> p k", p=P), allow_slow_non_contiguous=True).then_inc(const_loaded, 16)
                sp.dma_start(bglu[:, l, :], b_glu[l].rearrange("(k p) -> p k", p=P), allow_slow_non_contiguous=True).then_inc(const_loaded, 16)
                sp.dma_start(sink[:, l, :], sinks[l].partition_broadcast(P)).then_inc(const_loaded, 16)
            sp.dma_start(mask0[0:NMETA, :], mask0_t).then_inc(const_loaded, 16)

            sp.wait_ge(w_split, 1)
            sp.dma_start(WRAW[:, 0, :, :], W["w_in"][0:D, 0:P].rearrange("(k p) c -> p k c", p=P)).then_inc(w_loaded[0], 16)
            with sp.Fori(0, DEPTH) as l:
                S = l * STRIPS

                def strip(s, par, rows, row0, col0, ks):
                    sp.wait_ge(w_split, s + 1)
                    sp.sem_inc(passed, 1)
                    sp.dma_start(WRAW[:, par, 0:ks, :],
                                 rows[ds(row0, ks * P), ds(col0, P)].rearrange("(k p) c -> p k c", p=P)
                                 ).then_inc(w_loaded[par], 16)

                def tables():
                    sp.wait_ge(h_ready, l * 16 + 8)
                    sp.dma_start(cosb[:, :], cos_t).then_inc(tab_loaded, 16)
                    sp.dma_start(sinb[:, :], sin_t).then_inc(tab_loaded, 16)
                    sp.dma_start(mask_cur[:, :], mask_t[0]).then_inc(tab_loaded, 16)
                    sp.dma_start(mask_rest[:, :], mask_t[1]).then_inc(tab_loaded, 16)

                strip(S + 1, 1, W["w_in"], l * D, P, KD)
                tables()
                with sp.Fori(1, 8) as i:
                    for par in range(2):
                        strip(S + 2 * i + par, par, W["w_in"], l * D, (2 * i + par) * P, KD)

                def coef_loads(b):
                    one = lambda v: v[ds(b, 1), :, :].rearrange("o q n -> (o q) n")
                    for ri in range(2):
                        sp.dma_start(Bx[:, :, ri, :], b_v[ri][ds(b, 1), :, :, :].rearrange("o q p c -> (o q) p c")).then_inc(b_loaded, 16)
                        for dup in range(2):
                            sp.dma_start(Craw[:, ri, NS * dup:NS * dup + NS], one(c_v[ri])).then_inc(b_loaded, 16)
                    sp.dma_start(dsk[0:CG, :], one(d_v), allow_slow_non_contiguous=True).then_inc(b_loaded, 16)

                def gate_strips(i, lo, hi):
                    for j in range(lo, hi):
                        strip(S + S_G + 4 * i + j, j % 2, W["w_in"], l * D, (S_G + 4 * i + j) * P, KD)

                sp.wait_ge(x_stored, 16 * (KD + 16 * l))
                for k in range(2):
                    sp.wait_ge(u_stored[k], 16 * (2 * l + 2) + 16)
                sp.sem_inc(passed, 1)
                coef_loads(l * NB)

                def attention_loads(i, last=False):
                    b = l * NB + i
                    gate_strips(i, 0, 3)
                    sp.wait_ge(rope_done, l * 10 + 11)
                    sp.wait_ge(y_stored, 128 * b + 128)
                    sp.sem_inc(passed, 1)
                    for t in range(CT):
                        sp.dma_start(Uch[CG * t:CG * t + CG, :, :],
                                     ud[ds(i * P, P), t, :].rearrange("(g c) j -> c g j", g=8)).then_inc(u_loaded, 16)
                    gate_strips(i, 3, 4)
                    sp.wait_ge(s5_g, b + 1)
                    sp.sem_inc(passed, 1)
                    for t in range(CT):
                        sp.dma_start(Mtoe[CG * t:CG * t + CG, :, CG * t:P], Gs[0:CG, :, 0:P - CG * t]).then_inc(toe_loaded, 16)
                    if not last:
                        coef_loads(b + 1)

                with sp.Fori(0, NB - 1) as i:
                    attention_loads(i)
                attention_loads(NB - 1, last=True)
                with sp.Fori(0, 4) as i:
                    for par in range(2):
                        strip(S + S_OA + 2 * i + par, par, W["w_oa"], l * D, (2 * i + par) * P, KD)
                with sp.Fori(0, 2) as i:
                    for par in range(2):
                        strip(S + S_GLU + 2 * i + par, par, W["w_glu"], l * 512, (2 * i + par) * P, 4)
                with sp.Fori(0, 4) as i:
                    for par in range(2):
                        strip(S + S_OS + 2 * i + par, par, W["w_os"], l * 512, (2 * i + par) * P, 4)
                def x_old(t, strips_done, j):
                    sp.wait_ge(strip_done, S + strips_done + 2)
                    sp.wait_ge(x_stored, 16 * ((1 + j) * KD + 16 * l))
                    sp.sem_inc(passed, 1)
                    sp.dma_start(XO[:, ds(t, 1), :], xd[ds(t, 1), :, :].rearrange("o p w -> p o w")).then_inc(xo_loaded, 16)

                with sp.Fori(0, 4) as i:
                    for par in range(2):
                        strip(S + S_OUT + 2 * i + par, par, W["w_out"], l * D, (2 * i + par) * P, KD)
                        x_old(2 * i + par, S_OA + 8, 0)

                def mlp_loads(q, last=False):
                    with sp.Fori(0, 4) as i:
                        for par in range(2):
                            strip(S + S_FF + 16 * q + 2 * i + par, par, W["w_up"], l * D,
                                  q * D + (2 * i + par) * P, KD)
                    with sp.Fori(0, 4) as i:
                        for par in range(2):
                            strip(S + S_FF + 16 * q + 8 + 2 * i + par, par, W["w_down"], l * DFF + q * D,
                                  (2 * i + par) * P, KD)
                            if last:
                                x_old(2 * i + par, S_FF + 56, 1)

                with sp.Fori(0, 3) as q:
                    mlp_loads(q)
                mlp_loads(3, last=True)
                strip(S + STRIPS, 0, W["w_in"], (1 - l) * D, 0, KD)

            for n in range(1, NBLK, 2):
                sp.wait_ge(free_b, DEPTH * B_PER + B_INIT + n // 2 + 2)
                sp.dma_start(out[n * P:(n + 1) * P, :], OT[:, n, :]).then_inc(out_stored[1], 16)
            sp.wait_ge(out_stored[1], 16 * (NBLK // 2))

        @block.tensor
        def _(pe):
            pe.sem_inc(strip_done, 2)
            pe.sem_inc(sq_used, 2)
            pe.sem_inc(tr_done, 1)
            pe.wait_ge(ident_loaded, 16)
            for n in range(NBLK):
                ps, fr = (PA, free_a) if n % 2 == 0 else (PB, free_b)
                pe.wait_ge(fr, n // 2 + 1)
                if n == 0:
                    pe.wait_ge(xtok_loaded[0], 16)
                    for k in range(KD):
                        pe.transpose(ps[:, 2, k * NMETA:(k + 1) * NMETA], XT[0:NMETA, 0, k * P:(k + 1) * P],
                                     ident[0:NMETA, 0:NMETA])
                pe.wait_ge(xtok_loaded[n + 1], 16)
                for k in range(KD):
                    mm = pe.transpose(ps[:, k // 4, (k % 4) * P:(k % 4 + 1) * P], XT[:, n + 1, k * P:(k + 1) * P], ident[:, :])
                mm.then_inc(init_tr, 1)

            def pre_stats(q0):
                for k in range(KD):
                    pe.wait_ge(sq_ready, q0 + k + 1)
                    for c in range(NC3):
                        mm = pe.matmul(PA[:, c, 0:CW], ones[:, :], sqr[:, k % 2, c * CW:(c + 1) * CW],
                                       start=(k == 0), stop=(k == KD - 1))
                    mm.then_inc(sq_used, 1)

            pe.wait_ge(free_a, A_INIT + 1)
            for n in range(NBLK + 1):
                pe.wait_ge(diag_ready, n + 1)
                rows, t0 = (NMETA, 0) if n == 0 else (P, NMETA + (n - 1) * P)
                for c in range(NC3):
                    lo, hi = max(t0, c * CW), min(t0 + rows, (c + 1) * CW)
                    if lo < hi:
                        pe.matmul(PA[:, c, lo - c * CW:hi - c * CW], ones[0:rows, :], diag[0:rows, n, lo - t0:hi - t0],
                                  start=True, stop=True)
            pe.matmul(PA[:, NC3 - 1, CW - (LP - L):CW], ones[:, :], ones[:, 0:LP - L], start=True, stop=True).then_inc(sq_used, KD)
            with pe.Fori(0, DEPTH) as l:
                S, A, B = l * STRIPS, l * A_PER + A_INIT, l * B_PER + B_INIT

                def post_stats(a, j):
                    pe.wait_ge(free_a, A + a + 1)
                    pe.wait_ge(mix_acc, l * 14 + 7 * j + 8)
                    for c in range(NC3):
                        pe.matmul(PA[:, c, 0:CW], ones[:, :], MT[:, 0, c * CW:(c + 1) * CW], start=True, stop=False)
                    pe.wait_ge(mix_sq, l * 16 + 8 * j + 8)
                    for c in range(NC3):
                        mm = pe.matmul(PA[:, c, 0:CW], ones[:, :], MT[:, 1, c * CW:(c + 1) * CW], start=False, stop=True)
                    mm.then_inc(stat_done, 1)

                def ksteps(ps, par, ks, rh, rl, k0, total, waits=None):
                    for k in ks:
                        if waits:
                            waits(k)
                        for t, (w, r) in enumerate(((WHI, rh), (WHI, rl), (WLO, rh))):
                            for c in range(NC3):
                                mm = pe.matmul(ps[:, c, 0:CW], w[:, par, k, :], r[:, k0 + k, c * CW:(c + 1) * CW],
                                               start=(k == 0 and t == 0), stop=(k == total - 1 and t == 2))
                    return mm

                def take(s_static, s, i2):
                    pe.wait_ge(w_split, S + s + 3)
                    if a_use(s_static) is not None:
                        pe.wait_ge(free_a, A + a_use(s_static) + i2 + 1)
                    else:
                        pe.wait_ge(free_b, B + b_use(s_static) + i2 + 1)

                def strips(s0, n, total, rh, rl, extra=0, waits=None):
                    def strip(par, i, waits=None):
                        take(s0 + par, extra * 16 + s0 + 2 * i + par, i + extra * 8)
                        ksteps(pset(s0 + par), par, range(total), rh, rl, 0, total, waits).then_inc(strip_done, 1)

                    if waits is not None:
                        strip(0, 0, waits)
                        strip(1, 0)
                    with pe.Fori(0 if waits is None else 1, n // 2) as i:
                        for par in range(2):
                            strip(par, i)

                strips(S_U, 14, KD, HH, HL, waits=lambda k: pe.wait_ge(h_ready, l * 16 + k + 1))
                take(S_V, S_V, 0)
                ksteps(pset(S_V), 0, range(KD), HH, HL, 0, KD).then_inc(strip_done, 1)
                pe.wait_ge(stage_qk, l * 9 + 1)
                pe.sem_inc(passed, 1)
                for h in range(NH):
                    kv, hb = h // 4, HD * (h % 2)
                    mm = pe.matmul(PC[0:NMETA, h % 2, (h // 2) * 16:(h // 2 + 1) * 16], QY[hb:hb + HD, h // 2, 0:NMETA],
                                   kst[hb:hb + HD, kv, 0:NMETA], start=True, stop=True)
                mm.then_inc(m0_done[0], 1)
                take(S_V + 1, S_V + 1, 0)
                ksteps(pset(S_V + 1), 1, range(KD), HH, HL, 0, KD).then_inc(strip_done, 1)

                def v_tokens(par):
                    pe.wait_ge(free_a, A + A_VT + par + 1)
                    for n in range(NBLK):
                        pe.transpose(PA[:, n // 4, (n % 4) * P:(n % 4 + 1) * P],
                                     vt[par][:, NMETA + n * P:NMETA + (n + 1) * P], ident[:, :])
                    pe.transpose(PA[0:NMETA, 2, 0:P], vt[par][:, 0:NMETA], ident[:, :]).then_inc(v_tr, 1)

                v_tokens(0)
                pe.wait_ge(m0_done[3], l + 1)
                pe.sem_inc(passed, 1)
                for h in range(NH):
                    mm = pe.transpose(PC[0:NMETA, 0, h * 16:(h + 1) * 16], m0p[0:NMETA, h * 16:(h + 1) * 16],
                                      ident[0:NMETA, 0:NMETA])
                mm.then_inc(m0_done[4], 1)
                pe.wait_ge(free_b, B + 8 + 1)
                v_tokens(1)
                pe.wait_ge(free_a, A + A_VT + 2 + 1)
                pe.wait_ge(m0_done[5], l + 1)
                pe.sem_inc(passed, 1)
                ptm = pt_sb[:, 0, 0:2, :].rearrange("p a b -> p (a b)").rearrange("p (v j g q) -> p v g j q", v=4, j=2, g=2)
                for kv in range(NKV):
                    for g in range(2):
                        mm = pe.matmul(PO[HD * g:HD * g + HD, kv * 32:kv * 32 + 32], vmeta[0:NMETA, kv * HD:(kv + 1) * HD],
                                       ptm[0:NMETA, kv, g, :, :], start=True, stop=True)
                mm.then_inc(m0_done[6], 1)

                def scores(un, kv):
                    for g in range(4):
                        hb = HD * (g % 2)
                        pe.wait_ge(stt_done, 4 * un + g + 1)
                        pe.matmul(PS[g % 2][:, 0:KEYS], qst[hb:hb + HD, 2 * kv + g // 2, :], kst[hb:hb + HD, kv, :],
                                  start=True, stop=True).then_inc(scores_done, 1)

                def transposes(un, ev=None):
                    pe.wait_ge(p_ready, un + 1)
                    if ev is not None:
                        pe.wait_ge(*ev)
                    for g in range(4):
                        pe.transpose(PT[0][:, g * P:(g + 1) * P], s_sb[:, g, 32:160], ident[:, :])
                        pe.transpose(PT[1][:, g * P:(g + 1) * P], s_sb[:, g, 160:288], ident[:, :])
                    pe.wait_ge(y_out, un + 1)
                    pe.transpose(PO[:, 256:384], pm_sb[:, :, :].rearrange("p a b -> p (a b)"), ident[:, :]).then_inc(tr_done, 1)

                def pv(un, kv):
                    pe.wait_ge(pt_act, un + 1)
                    pe.wait_ge(pt_dve, un + 1)
                    vc = slice(kv * HD, kv * HD + HD)
                    for hf in range(2):
                        o = PO[HD * hf:HD * hf + HD, 0:256]
                        for j in range(2):
                            pe.matmul(o, vst[:, j, vc], pt_sb[:, j, hf::2, :], start=(j == 0), stop=False)
                        mm = pe.matmul(o, vmeta[:, vc], ptm_sb[:, hf::2, :], start=False, stop=True)
                    mm.then_inc(pv_done, 1)

                def banks_free(un):
                    pe.wait_ge(stt_done, 4 * un + 6)
                    pe.wait_ge(pt_act, un)
                    pe.wait_ge(pt_dve, un)
                    pe.sem_inc(passed, 1)

                def s5_a0(b, un):
                    pe.wait_ge(b_loaded, 112 * (b + 1))
                    pe.wait_ge(stt_done, 4 * un + 6)
                    for ri in range(2):
                        mm = pe.transpose(PS[0][:, ri * P:(ri + 1) * P], Craw[:, ri, :], ident[:, :])
                    mm.then_inc(s5_pe, 1)

                def s5_a(b, un):
                    pe.wait_ge(s5_min, b + 1)
                    pe.wait_ge(s5_w, b + 1)
                    banks_free(un)
                    for p in range(4):
                        for ri in range(2):
                            i = 2 * p + ri
                            pe.transpose(PS[i // 4][:, (i % 4) * P:(i % 4 + 1) * P], MinT[:, p, ri, :], ident[:, :])
                    for g in range(8):
                        gb, p = NS * (g % 2), g // 2
                        for ri in range(2):
                            mm = pe.matmul(PT[g % 2][0:CG, p * P:(p + 1) * P], BB[gb:gb + NS, p, ri, :],
                                           W9[gb:gb + NS, p, ri, 0:P], start=(ri == 0), stop=(ri == 1))
                    mm.then_inc(s5_pe, 1)

                def s5_b(b, un):
                    pe.wait_ge(s5_ev, 3 * b + 2)
                    pe.wait_ge(u_loaded, 128 * (b + 1))
                    banks_free(un)
                    for p in range(4):
                        for g2 in range(2):
                            for ri in range(2):
                                mm = pe.matmul(BK4[p][NS * g2:NS * g2 + NS, ri * NCH:(ri + 1) * NCH],
                                               Min[:, p, ri, NS * g2:NS * g2 + NS], Uch[:, 2 * p + g2, :],
                                               start=True, stop=True)
                    mm.then_inc(s5_pe, 1)

                def s5_c(b):
                    pe.wait_ge(s5_scan, b + 1)
                    pe.wait_ge(toe_loaded, 128 * (b + 1))
                    pe.sem_inc(passed, 1)
                    for g in range(8):
                        p, gb = g // 2, NS * (g % 2)
                        o = BK4[2 * (g % 2) + p // 2][:, (p % 2) * NCH:(p % 2 + 1) * NCH]
                        pe.matmul(o, Mtoe[:, g, :], Uch[:, g, :], start=True, stop=False)
                        for ri in range(2):
                            mm = pe.matmul(o, W9[gb:gb + NS, p, ri, CG:CG + P], St[gb:gb + NS, p, ri, 0:NCH],
                                           start=False, stop=(ri == 1))
                    mm.then_inc(s5_out, 1)

                def attention(i, first=False):
                    b = l * NB + i
                    for u8 in range(8):
                        kv = u8 % NKV
                        un = l * 32 + 8 * i + u8
                        ev = {0: (s5_ev, 3 * b + 1), 3: (s5_ev, 3 * b + 2), 4: (s5_ev, 3 * b + 3)}
                        if not first:
                            ev[1] = (s5_out_ev, b)
                        if kv == 0:
                            pe.wait_ge(stage_qk, l * 9 + 2 + 2 * i + u8 // NKV)
                        if u8 - 1 in ev:
                            pe.wait_ge(*ev[u8 - 1])
                        scores(un, kv)
                        gi, k0 = u8 // 2, 4 * (u8 % 2)
                        if u8 % 2 == 0:
                            pe.wait_ge(w_split, S + S_G + gi + 4 * i + 3)
                            pe.wait_ge(free_a, A + a_use(S_G) + gi + 4 * i + 1)
                        ksteps(PA, gi % 2, range(k0, k0 + 2), HH, HL, 0, KD)
                        if u8 == 4:
                            s5_b(b, un)
                        mm = ksteps(PA, gi % 2, range(k0 + 2, k0 + 4), HH, HL, 0, KD)
                        if u8 % 2 == 1:
                            mm.then_inc(strip_done, 1)
                        if u8 == 0:
                            s5_a0(b, un)
                        elif u8 == 1 and not first:
                            banks_free(un)
                            s5_c(b - 1)
                        elif u8 == 3:
                            s5_a(b, un)
                        if not (first and u8 == 0):
                            pv(un - 1, (kv - 1) % NKV)
                        if first and u8 == 0:
                            pe.wait_ge(m0_done[7], l + 1)
                        transposes(un, ev.get(u8) if u8 else None)

                attention(0, first=True)
                with pe.Fori(1, NB) as i:
                    attention(i)
                pv(l * 32 + 31, NKV - 1)
                for par in range(2):
                    take(S_OA + par, S_OA + par, 0)
                    ksteps(pset(S_OA + par), par, range(KD), HH, HL, 0, KD,
                           waits=(lambda k: pe.wait_ge(ys_ready, l * KD + k + 1)) if par == 0 else None).then_inc(strip_done, 1)
                pe.wait_ge(free_b, B + b_use(S_OA + 1) + 2)
                pe.wait_ge(pt_act, l * 32 + 32)
                pe.wait_ge(pt_dve, l * 32 + 32)
                s5_c(l * NB + NB - 1)
                take(S_OA + 2, S_OA + 2, 0)
                ksteps(PA, 0, range(KD), HH, HL, 0, KD).then_inc(strip_done, 1)
                pe.wait_ge(s5_out_ev, NB * (l + 1))
                take(S_OA + 3, S_OA + 3, 0)
                ksteps(PB, 1, range(KD), HH, HL, 0, KD).then_inc(strip_done, 1)
                strips(S_OA + 4, 4, KD, HH, HL)
                zl = BL[:, 4:8, :]
                strips(S_GLU, 4, 4, BL, zl, waits=lambda k: pe.wait_ge(z_ready, l * 4 + k + 1))
                strips(S_OS, 8, 4, XR, XR[:, 4:8, :], waits=lambda k: pe.wait_ge(z2_ready, l * 4 + k + 1))
                strips(S_OUT, 8, KD, BH, BL, waits=lambda k: pe.wait_ge(mg_ready, l * KD + k + 1))
                post_stats(A_POST1, 0)
                take(S_FF, S_FF, 0)
                pe.wait_ge(free_b, B + B_PRE2 + 1)
                for k in range(KD):
                    pe.wait_ge(h_ready, l * 16 + 8 + k + 1)
                    mm = ksteps(PA, 0, [k], HH, HL, 0, KD)
                    if k == KD - 1:
                        mm.then_inc(strip_done, 1)
                    pe.wait_ge(sq_ready, l * 16 + 8 + k + 1)
                    for c in range(NC3):
                        mm = pe.matmul(PB[:, c, 0:CW], ones[:, :], sqr[:, k % 2, c * CW:(c + 1) * CW],
                                       start=(k == 0), stop=(k == KD - 1))
                    mm.then_inc(sq_used, 1)

                def quarter(q, first=False):
                    if first:
                        take(S_FF + 1, S_FF + 1, 0)
                        ksteps(PB, 1, range(KD), HH, HL, 0, KD).then_inc(strip_done, 1)
                        strips(S_FF + 2, 6, KD, HH, HL)
                    else:
                        strips(S_FF, 8, KD, HH, HL, extra=q)
                    strips(S_FF + 8, 8, KD, BH, BL, extra=q,
                           waits=lambda k: pe.wait_ge(hid_ready, l * 32 + q * 8 + k + 2))

                quarter(0, first=True)
                with pe.Fori(1, 4) as q:
                    quarter(q)
                post_stats(A_POST2, 1)
                pe.wait_ge(free_a, A + A_PER + 1)
                pre_stats(l * 16 + 16)

            A, B = DEPTH * A_PER + A_INIT, DEPTH * B_PER + B_INIT
            pe.wait_ge(x_ready, 13 * DEPTH + 1)
            pe.wait_ge(x_ready_v, 3 * DEPTH)
            for n in range(NBLK):
                ps, fr, u0 = (PA, free_a, A) if n % 2 == 0 else (PB, free_b, B)
                pe.wait_ge(fr, u0 + n // 2 + 1)
                for k in range(KD):
                    mm = pe.transpose(ps[:, k // 4, (k % 4) * P:(k % 4 + 1) * P],
                                      X[:, k, NMETA + n * P:NMETA + (n + 1) * P], ident[:, :])
                mm.then_inc(out_tr, 1)

        @block.scalar
        def _(act):
            for k in range(2):
                act.sem_inc(u_stored[k], 16)
            act.sem_inc(g_stored, 16)

            def w_high(s, par, ks=KD):
                s2 = s[1]
                act.wait_ge(w_loaded[par], 16 * (s2 + 1))
                act.wait_ge(strip_done, s[0] + 1)
                act.activation(WHI[:, par, 0:ks, :], WRAW[:, par, 0:ks, :], ACT.Copy).then_inc(w_hi, 1)

            act.wait_ge(pool_init, 1)
            for n in range(NBLK):
                if n == 0:
                    act.wait_ge(xtok_loaded[0], 16)
                    act.activation(junk[0:NMETA, :], XT[0:NMETA, 0, :], ACT.Square, accum_out=rowsq[0:NMETA, 0:1]).then_inc(rows_sq, 1)
                act.wait_ge(xtok_loaded[n + 1], 16)
                act.drain()
                act.activation(junk[:, :], XT[:, n + 1, :], ACT.Square, accum_out=rowsq[:, n + 1:n + 2]).then_inc(rows_sq, 1)
                ps, fr = (PA, free_a) if n % 2 == 0 else (PB, free_b)
                act.wait_ge(init_tr, n + 1)
                if n == 0:
                    act.activation(X[:, :, 0:NMETA], ps[:, 2, 0:P].rearrange("p (k w) -> p k w", k=KD), ACT.Copy)
                act.activation(X[:, :, NMETA + n * P:NMETA + (n + 1) * P],
                               ps[:, 0:2, :].rearrange("p c (k w) -> p (c k) w", w=P), ACT.Copy).then_inc(fr, 1)
            act.drain()
            act.wait_ge(free_b, B_INIT + 1)
            for k in range(KD):
                act.dma_start(xd[k], X[:, k, :]).then_inc(x_stored, 16)

            def square(k, q0):
                act.wait_ge(sq_used, q0 + k + 1)
                act.activation(sqr[:, k % 2, :], X[:, k, :], ACT.Square).then_inc(sq_ready, 1)

            act.sem_inc(sq_ready, KD)
            w_high((0, 0), 0)
            with act.Fori(0, DEPTH) as l:
                S, S2 = l * STRIPS, l * (STRIPS // 2)
                A, B = l * A_PER + A_INIT, l * B_PER + B_INIT

                def nxt(s, i, ks=KD):
                    w_high((S + s + 1 + 2 * i, S2 + (s + 1) // 2 + i), (s + 1) % 2, ks)

                def freed(s):
                    return free_a if a_use(s) is not None else free_b

                def rsqrt0(sums, n, ps):
                    act.wait_ge(sums, n)
                    act.activation(v3(ny[:, :]), ps[:, :, 0:CW], ACT.Ln, scale=1.0 / D, bias=EPS).then_inc(ln_done, 1)
                    act.drain()
                    act.activation(ny[:, :], ny[:, :], ACT.Exp, scale=-0.5).then_inc(rs0_done, 1)

                rsqrt0(sq_used, l * 16 + KD + 2, PA)
                for k in range(KD):
                    act.wait_ge(hx_ready, l * 8 + k + 1)
                    act.activation(HH[:, k, :], nx[:, k % 2, :], ACT.Copy).then_inc(hx_hi, 1)
                with act.Fori(0, 2) as i:
                    for par in range(2):
                        nxt(S_U + par, i)
                        act.wait_ge(strip_done, S + S_U + par + 2 * i + 3)
                        act.activation(v3(ut[:, :]), pset(par)[:, :, 0:CW], ACT.Copy).then_inc(freed(par), 1)
                        act.drain()
                        act.wait_ge(u_stored[par], 16 * (2 * l + i) + 16)
                        act.activation(ust[:, par, :, :], ut[:, 0:L].rearrange("p (j t) -> p t j", t=CT),
                                       ACT.Copy).then_inc(u_copied, 1)
                        act.wait_ge(u_copied, l * 4 + 2 * i + par + 1)
                        act.dma_start(ud[ds((2 * i + par) * P, P), :, :], ust[:, par, :, :]).then_inc(u_stored[par], 16)
                act.wait_ge(s5_e[0], l + 1)
                act.activation(T2p[:, 0:16], T1p[:, 64:80], ACT.Sin)
                act.activation(T1p[:, 112:128], T1p[:, 64:80], ACT.Abs)
                act.drain()
                act.activation(T2p[:, 16:32], T1p[:, 112:128], ACT.Sin, scale=-1.0, bias=float(np.pi / 2)).then_inc(s5_e[1], 1)
                with act.Fori(0, 5) as i:
                    for par in range(2):
                        nxt(S_Q + par, i)
                        act.wait_ge(strip_done, S + S_Q + par + 2 * i + 3)
                        act.wait_ge(rope_done, l * 10 + 2 * i + par + 1)
                        for qd in range(4):
                            o, r = 32 * qd, 32 * (qd ^ 1)
                            act.activation(v3(rot[o:o + 32, :]), pset(par)[r:r + 32, :, 0:CW], ACT.Copy).then_inc(rot_ready, 1)
                act.wait_ge(pool_init, l * 5 + 6)
                act.wait_ge(rope_done, l * 10 + 11)
                for sh in range(2):
                    for dh in range(2):
                        mm = act.activation(kst[HD * dh:HD * dh + HD, sh::2, 0:NMETA],
                                            kbuf[HD * sh:HD * sh + HD, :, 0:NMETA], ACT.Copy)
                mm.then_inc(stage_qk, 1)

                def stage(n):
                    act.activation(qst[:, :, :], QY[:, :, ds(NMETA + n * P, P)], ACT.Copy)
                    for sh in range(2):
                        for dh in range(2):
                            mm = act.activation(kst[HD * dh:HD * dh + HD, sh::2, 32:KEYS],
                                                kbuf[HD * sh:HD * sh + HD, :, ds(NMETA + n * P, 2 * P)], ACT.Copy)
                    mm.then_inc(stage_qk, 1)

                for k in range(2):
                    act.wait_ge(u_stored[k], 16 * (2 * l + 2) + 16)
                nxt(S_V, 0)
                act.wait_ge(strip_done, S + S_V + 3)
                act.activation(v3(vt[0][:, :]), PA[:, :, 0:CW], ACT.Copy).then_inc(free_a, 1)
                nxt(S_V + 1, 0)
                act.wait_ge(m0_done[1], l + 1)
                act.activation(m0p[0:NMETA, :], m0p[0:NMETA, :], ACT.Exp)
                act.activation(stat[0:NMETA, 5, :], stat[0:NMETA, 4, :], ACT.Exp).then_inc(m0_done[2], 1)
                stage(0)
                act.wait_ge(strip_done, S + S_V + 4)
                act.activation(v3(vt[1][:, :]), PB[:, :, 0:CW], ACT.Copy).then_inc(free_b, 1)

                def v_rows(par):
                    act.wait_ge(v_tr, l * 2 + par + 1)
                    act.activation(Vb[:, 1:NBLK + 1, par * P:(par + 1) * P],
                                   PA[:, 0:2, :].rearrange("p c (n w) -> p (c n) w", n=4), ACT.Copy)
                    for g in range(4):
                        mm = act.activation(vmeta[32 * g:32 * g + NMETA, par * P:(par + 1) * P], PA[0:NMETA, 2, 0:P], ACT.Copy)
                    mm.then_inc(free_a, 1)

                v_rows(0)
                act.wait_ge(m0_done[4], l + 1)
                act.activation(pt_sb[0:NMETA, 0, 0:2, :], PC[0:NMETA, 0, 0:256].rearrange("p (a b) -> p a b", a=2),
                               ACT.Copy).then_inc(m0_done[5], 1)
                v_rows(1)
                act.wait_ge(m0_done[6], l + 1)

                def s5_outputs(i):
                    b = l * NB + i
                    act.wait_ge(s5_out, b + 1)
                    for p in (2, 3, 0, 1):
                        g0 = 4 * (p % 2) + p // 2
                        mm = act.activation(Uch[:, g0:g0 + 3:2, :], BK4[p][:, 0:2 * NCH].rearrange(
                            "p (a b) -> p a b", a=2), ACT.Copy)
                    mm.then_inc(s5_out_ev, 1)
                    act.wait_ge(s5_out_ev, b + 1)
                    for t in range(CT):
                        act.dma_start(yd[ds(i * P, P), t, :].rearrange("(g c) j -> c g j", g=8),
                                      Uch[CG * t:CG * t + CG, :, :]).then_inc(y_stored, 16)

                def attention(i, first=False, last=False):
                    b = l * NB + i
                    for u8 in range(8):
                        kv = u8 % NKV
                        un = l * 32 + 8 * i + u8
                        for g in range(4):
                            if g % 2 == 0:
                                act.wait_ge(m_ready, 2 * un + 1 + g // 2)
                            act.activation(s_sb[:, g, :], s_sb[:, g, :], ACT.Exp, bias=stat[:, 2, g:g + 1],
                                           accum_out=stat[:, 3, g:g + 1])
                        act.wait_ge(sink_ready, un + 1)
                        act.activation(stat[:, 5, 0:4], stat[:, 4, 0:4], ACT.Exp).then_inc(exp_done, 1)
                        if kv == NKV - 1 and not (last and u8 == 7):
                            act.wait_ge(scores_done, 4 * un + 4)
                            stage(2 * i + (u8 + 1) // NKV)
                        gi = u8 // 2
                        if u8 % 2 == 0:
                            w_high((S + S_G + gi + 4 * i + 1, S2 + S_G // 2 + (gi + 1) // 2 + 2 * i), (gi + 1) % 2)
                        else:
                            act.wait_ge(strip_done, S + S_G + gi + 4 * i + 3)
                            act.wait_ge(g_stored, 16 * (l * 16 + 4 * i + gi) + 16)
                            act.activation(v3(gst[:, :]), PA[:, :, 0:CW], ACT.Tanh, scale=0.5).then_inc(free_a, 1)
                            act.wait_ge(free_a, A + a_use(S_G) + gi + 4 * i + 2)
                            act.dma_start(gd[ds(4 * i + gi, 1), :, :].rearrange("o p w -> p (o w)"), gst[:, :]).then_inc(g_stored, 16)
                        if u8 == 0:
                            act.wait_ge(s5_pe, 3 * b + 1)
                            for ri in range(2):
                                for g2 in range(2):
                                    src = PS[0][NS * g2:NS * g2 + NS, ri * P:(ri + 1) * P].rearrange(
                                        "q (p g c) -> q p g c", p=4, g=2)[:, :, g2, :]
                                    mm = act.activation(Cc[NS * g2:NS * g2 + NS, :, ri, :], src, ACT.Copy,
                                                        scale=1.0 - 2.0 * ri)
                            mm.then_inc(s5_ev, 1)
                        elif u8 == 1 and not first:
                            s5_outputs(i - 1)
                        elif u8 == 3:
                            act.wait_ge(s5_pe, 3 * b + 2)
                            for hf in range(2):
                                act.activation(Gs[0:CG, hf::2, :],
                                               PT[hf][0:CG, :].rearrange("p (a b) -> p a b", a=4), ACT.Copy)
                            act.activation(Min[:, :, :, :].rearrange("q p r w -> q (p r w)").rearrange("q (c w) -> q c w", c=2),
                                           PB[:, 0:2, :], ACT.Copy).then_inc(s5_ev, 1)
                        elif u8 == 4:
                            act.wait_ge(s5_pe, 3 * b + 3)
                            for p in (2, 3, 0, 1):
                                mm = act.activation(St[:, p, :, 1:NCH + 1], BK4[p][:, 0:2 * NCH].rearrange(
                                    "p (a b) -> p a b", a=2), ACT.Copy)
                            mm.then_inc(s5_ev, 1)
                        if kv == 0:
                            act.wait_ge(pv_done, un + 1)
                            act.activation(vst[:, :, :], Vb[:, ds(2 * i + u8 // 4, 2), :], ACT.Copy)
                        act.wait_ge(tr_done, un + 2)
                        act.activation(pt_sb[:, 0, :, :], PT[0].rearrange("p (a b) -> p a b", a=4), ACT.Copy)
                        for g in range(4):
                            mm = act.activation(ptm_sb[32 * g:32 * g + 32, g, :], PO[32 * g:32 * g + 32, 256:384], ACT.Copy)
                        mm.then_inc(pt_act, 1)

                attention(0, first=True)
                with act.Fori(1, NB - 1) as i:
                    attention(i)
                attention(NB - 1, last=True)

                act.wait_ge(strip_done, S + 31 + 3)
                for k in range(KD):
                    act.wait_ge(y_out, l * 32 + 30 + k // 2)
                    act.activation(HH[:, k, :], QY[:, k, :], ACT.Copy).then_inc(ys_hi, 1)
                for par in range(2):
                    nxt(S_OA + par, 0)
                s5_outputs(NB - 1)

                def gelu(i):
                    act.wait_ge(yr_loaded, 64 * (l + 1))
                    act.activation(MT[:, 2, 0:L].rearrange("p (j t) -> p j t", t=CT),
                                   X[:, ds(i, 1), 0:L].rearrange("p o (t j) -> p (o j) t", t=CT), ACT.Square).then_inc(ge[0], 1)
                    act.wait_ge(ge[1], l * 4 + i + 1)
                    act.activation(MT[:, 3, 0:L], MT[:, 2, 0:L], ACT.Tanh, scale=0.7978845608028654).then_inc(ge[2], 1)
                    act.wait_ge(ev_f, l * EVF + i + 1)
                    act.activation(BL[:, ds(i, 1), :], X[:, ds(4 + i, 1), :], ACT.Copy, scale=0.5).then_inc(ev_hi, 1)

                nxt(S_OA, 1)
                for i in range(4):
                    nxt(S_OA + 3 + i, 0)
                    gelu(i)
                nxt(S_OA + 7, 0)
                nxt(S_GLU, 0, 4)
                with act.Fori(0, 2) as i:
                    for par in range(2):
                        act.wait_ge(strip_done, S + S_GLU + par + 2 * i + 3)
                        act.activation(v3(MT[:, 2, :]), pset(par)[:, :, 0:CW], ACT.Tanh, scale=0.5,
                                       bias=bgluh[:, ds(l, 1), ds(2 * i + par, 1)].rearrange("p a b -> p (a b)")
                                       ).then_inc(freed(par), 1)
                        nxt(S_GLU + par + 1, i, 4)
                        act.wait_ge(ev_f, l * EVF + 4 + 2 * i + par + 1)
                        act.activation(XR[:, ds(2 * i + par, 1), :], MT[:, 3:4, :], ACT.Copy, scale=0.25).then_inc(ev_hi, 1)
                def merge(i, ks):
                    for par in range(2):
                        nxt(S_OS + par + 1, i, ks)
                        act.wait_ge(ev_f, l * EVF + 8 + 2 * i + par + 1)
                        act.activation(BH[:, ds(2 * i + par, 1), :], MT[:, 3:4, :], ACT.Copy, scale=0.5).then_inc(ev_hi, 1)

                with act.Fori(0, 3) as i:
                    merge(i, 4)
                merge(3, KD)
                act.wait_ge(mg_ready, l * KD + KD)
                act.sem_inc(passed, 1)
                with act.Fori(0, 4) as i:
                    for par in range(2):
                        act.wait_ge(strip_done, S + S_OUT + par + 2 * i + 3)
                        act.wait_ge(mix_acc, l * 14 + 2 * i + par + 1)
                        act.activation(v3(MT[:, 1, :]), pset(par)[:, :, 0:CW], ACT.Square).then_inc(mix_sq, 1)
                        act.activation(X[:, ds(2 * i + par, 1), :].rearrange("p o (c w) -> p (o c) w", c=NC3),
                                       pset(par)[:, :, 0:CW], ACT.Copy).then_inc(freed(par), 1)
                        nxt(S_OUT + par + 1, i)
                rsqrt0(stat_done, l * 2 + 1, PA)
                for k in range(KD):
                    act.wait_ge(x_ready, l * 13 + k + 2)
                    act.activation(HH[:, k, :], X[:, k, :], ACT.Identity,
                                   scale=gains[:, ds(l, 1), 2, k:k + 1].rearrange("p a b -> p (a b)")).then_inc(hx_hi, 1)
                    square(k, l * 16 + 8)
                    act.dma_start(xd[k], X[:, k, :]).then_inc(x_stored, 16)
                rsqrt0(sq_used, l * 16 + 8 + KD + 2, PB)

                def up_strip(q, par, i):
                    act.wait_ge(relu_done, l * 32 + q * 8 + 2 * i + par + 1)
                    act.wait_ge(hid_ready, l * 32 + q * 8 + 2 * i + par + 1)
                    act.activation(MT[:, 3, :], MT[:, 2, :], ACT.Square)
                    act.drain()
                    act.activation(BH[:, ds(2 * i + par, 1), :], MT[:, 3:4, :], ACT.Copy).then_inc(ev_hi, 1)

                def mlp(q, first=False, last=False):
                    if first:
                        up_strip(0, 0, 0)
                        nxt(S_FF + 1, 0)
                        up_strip(0, 1, 0)
                    with act.Fori(int(first), 4) as i:
                        for par in range(2):
                            nxt(S_FF + par, i + 8 * q)
                            up_strip(q, par, i)
                    with act.Fori(0, 4) as i:
                        for par in range(2):
                            nxt(S_FF + 8 + par, i + 8 * q)
                            if last:
                                t = 2 * i + par
                                if par == 0:
                                    act.wait_ge(free_a, A + a_use(S_FF + 8) + 8 * q + i + 2)
                                else:
                                    act.wait_ge(free_b, B + b_use(S_FF + 9) + 8 * q + i + 2)
                                act.wait_ge(mix_acc, l * 14 + 7 + t + 1)
                                act.activation(MT[:, 1:2, :], X[:, ds(t, 1), :], ACT.Square).then_inc(mix_sq, 1)

                mlp(0, first=True)
                with act.Fori(1, 3) as q:
                    mlp(q)
                mlp(3, last=True)
                rsqrt0(stat_done, l * 2 + 2, PA)
                for k in range(KD):
                    if k in BY_DVE:
                        act.wait_ge(x_ready_v, l * 3 + BY_DVE.index(k) + 1)
                    else:
                        act.wait_ge(x_ready, l * 13 + 8 + BY_POOL.index(k) + 2)
                    square(k, l * 16 + 16)
                    act.dma_start(xd[k], X[:, k, :]).then_inc(x_stored, 16)

            for n in range(0, NBLK, 2):
                act.wait_ge(out_tr, n + 1)
                act.activation(OT[:, n, :].rearrange("p (c w) -> p c w", c=2), PA[:, 0:2, :], ACT.Copy).then_inc(free_a, 1)
                act.wait_ge(free_a, DEPTH * A_PER + A_INIT + n // 2 + 2)
                act.dma_start(out[n * P:(n + 1) * P, :], OT[:, n, :]).then_inc(out_stored[0], 16)
            act.wait_ge(out_stored[0], 16 * (NBLK // 2))
            act.wait_ge(x_stored, 16 * (KD + 16 * DEPTH))
            act.wait_ge(g_stored, 16 * (16 * DEPTH) + 16)
            act.wait_ge(y_stored, 128 * NB * DEPTH + 128)
            for k in range(2):
                act.wait_ge(u_stored[k], 16 * 2 * DEPTH + 16)

        @block.vector
        def _(dve):
            dve.sem_inc(w_split, 2)
            dve.sem_inc(free_a, 1)
            dve.sem_inc(free_b, 1)
            dve.sem_inc(rope_done, 1)
            dve.sem_inc(stt_done, 2)
            dve.sem_inc(y_out, 1)
            dve.sem_inc(hid_ready, 1)
            dve.sem_inc(pv_done, 1)

            def w_low(s, par, ks=KD):
                dve.wait_ge(w_hi, s + 1)
                dve.tensor_tensor(WLO[:, par, 0:ks, :], WRAW[:, par, 0:ks, :], WHI[:, par, 0:ks, :].bitcast(F32),
                                  ALU.subtract).then_inc(w_split, 1)

            def split_low(lo, src, hi, scale, done):
                dve.scalar_tensor_tensor(out=lo, in0=src, scalar=scale, in1=hi.bitcast(F32), op0=ALU.mult,
                                         op1=ALU.subtract).then_inc(done, 1)

            dve.wait_ge(ident_loaded, 16)
            for n in range(NBLK + 1):
                rows = NMETA if n == 0 else P
                dve.wait_ge(rows_sq, n + 1)
                dve.tensor_scalar(diag[0:rows, n, 0:rows], ident[0:rows, 0:rows], rowsq[0:rows, n:n + 1], None,
                                  ALU.mult).then_inc(diag_ready, 1)
            w_low(0, 0)
            dve.wait_ge(const_loaded, 16 * 13)
            with dve.Fori(0, DEPTH) as l:
                S = l * STRIPS
                A, B = l * A_PER + A_INIT, l * B_PER + B_INIT

                def freed(s):
                    return free_a if a_use(s) is not None else free_b

                def rsqrt(ps, freed, r, rstd):
                    dve.wait_ge(ln_done, l * 4 + r + 1)
                    dve.tensor_scalar(v3(nv[:, :]), ps[:, :, 0:CW], 1.0 / D, EPS, ALU.mult, ALU.add).then_inc(freed, 1)
                    dve.drain()
                    dve.wait_ge(rs0_done, l * 4 + r + 1)
                    dve.scalar_tensor_tensor(out=nt[:, :], in0=nv[:, :], scalar=-0.5, in1=ny[:, :], op0=ALU.mult, op1=ALU.mult)
                    dve.drain()
                    dve.tensor_tensor(nt[:, :], nt[:, :], ny[:, :], ALU.mult)
                    dve.drain()
                    dve.scalar_tensor_tensor(out=rstd, in0=nt[:, :], scalar=1.5, in1=ny[:, :], op0=ALU.add, op1=ALU.mult)
                    dve.drain()

                def gain(i, k):
                    return gains[:, ds(l, 1), i, k:k + 1].rearrange("p a b -> p (a b)")

                def post_norm(j, gi, r, pre=None):
                    rsqrt(PA, free_a, r, rstd[:, :])
                    lag = 3
                    for k in range(KD + (lag if pre is not None else 0)):
                        if k < KD:
                            dve.scalar_tensor_tensor(out=X[:, k, :], in0=X[:, k, :], scalar=gain(gi, k), in1=rstd[:, :],
                                                     op0=ALU.mult, op1=ALU.mult).then_inc(post_scaled, 1)
                        if pre is None and k in BY_DVE:
                            dve.drain()
                            dve.wait_ge(xo_loaded, 16 * (l * 16 + 16))
                            dve.tensor_tensor(X[:, k, :], X[:, k, :], XO[:, k, :], ALU.add).then_inc(x_ready_v, 1)
                        if pre is not None and k >= lag:
                            t = k - lag
                            dve.wait_ge(hx_hi, l * 16 + 8 + t + 1)
                            split_low(HL[:, t, :], X[:, t, :], HH[:, t, :], gain(pre, t), h_ready)

                rsqrt(PA, free_a, 0, rstd[:, :])
                for k in range(KD + 1):
                    if k > 1:
                        dve.drain()
                    if k < KD:
                        dve.scalar_tensor_tensor(out=nx[:, k % 2, :], in0=X[:, k, :], scalar=gain(0, k), in1=rstd[:, :],
                                                 op0=ALU.mult, op1=ALU.mult).then_inc(hx_ready, 1)
                    if k > 0:
                        dve.wait_ge(hx_hi, l * 16 + k)
                        split_low(HL[:, k - 1, :], nx[:, (k - 1) % 2, :], HH[:, k - 1, :], 1.0, h_ready)
                with dve.Fori(0, 2) as i:
                    for par in range(2):
                        w_low(S + S_U + par + 1 + 2 * i, (par + 1) % 2)
                dve.wait_ge(tab_loaded, 64 * (l + 1))
                dve.sem_inc(passed, 1)

                def rope(par, i, s0, tile, dst):
                    w_low(S + s0 + par + 1 + 2 * i, (par + 1) % 2)
                    dve.drain()
                    dve.wait_ge(rot_ready, 4 * (l * 10 + tile + 1))
                    dve.tensor_tensor(v3(rt1[:, :]), pset(par)[:, :, 0:CW], v3(cosb[:, :]), ALU.mult).then_inc(freed(par), 1)
                    dve.tensor_tensor(rt2[:, :], rot[:, :], sinb[:, :], ALU.mult)
                    dve.drain()
                    for o, c0, c1 in dst:
                        mm = dve.tensor_tensor(o, rt1[:, c0:c1], rt2[:, c0:c1], ALU.add)
                    mm.then_inc(rope_done, 1)

                with dve.Fori(0, 4) as i:
                    for par in range(2):
                        rope(par, i, S_Q, 2 * i + par, [(QY[:, ds(2 * i + par, 1), :].rearrange("p o w -> p (o w)"), 0, LP)])
                dve.wait_ge(x_stored, 16 * (KD + 16 * l))
                for par in range(2):
                    rope(par, 0, S_K, 8 + par, [(kbuf[:, par, 0:NMETA], 0, NMETA), (kbuf[:, par, KOFF:], NMETA, L)])
                w_low(S + S_V + 1, 1)

                pflat = m0p[0:NMETA, :].rearrange("p (h k) -> p h k", h=NH)
                st0 = [stat[0:NMETA, r, :] for r in range(6)]
                sk0 = sink[0:NMETA, ds(l, 1), :].rearrange("p a b -> p (a b)")
                dve.wait_ge(m0_done[0], l + 1)
                for e in range(2):
                    dve.scalar_tensor_tensor(out=pflat[:, e::2, :], in0=PC[0:NMETA, e, 0:P].rearrange("p (h k) -> p h k", h=NH // 2),
                                             scalar=SCALE, in1=mask0[0:NMETA, :].unsqueeze(1).to_broadcast([NMETA, NH // 2, NMETA]),
                                             op0=ALU.mult, op1=ALU.add)
                dve.drain()
                dve.tensor_reduce(st0[0], pflat, AX.X, ALU.max)
                dve.drain()
                dve.tensor_tensor(st0[1], st0[0], sk0, ALU.max)
                dve.drain()
                dve.tensor_tensor(pflat, pflat, st0[1].unsqueeze(2).to_broadcast([NMETA, NH, NMETA]), ALU.subtract)
                dve.tensor_tensor(st0[4], sk0, st0[1], ALU.subtract).then_inc(m0_done[1], 1)
                dve.wait_ge(m0_done[2], l + 1)
                dve.tensor_reduce(st0[3], pflat, AX.X, ALU.add)
                dve.drain()
                dve.tensor_tensor(st0[0], st0[3], st0[5], ALU.add)
                dve.drain()
                dve.reciprocal(st0[1], st0[0])
                dve.drain()
                dve.tensor_tensor(pflat, pflat, st0[1].unsqueeze(2).to_broadcast([NMETA, NH, NMETA]), ALU.mult).then_inc(m0_done[3], 1)
                w_low(S + S_V + 2, 0)
                dve.wait_ge(m0_done[6], l + 1)
                dve.tensor_copy(QY[:, :, 0:NMETA], PO[:, 0:P].rearrange("p (t q) -> p t q", t=KD)).then_inc(m0_done[7], 1)

                def y_store(un, kv, n):
                    dve.wait_ge(pv_done, un + 2)
                    dve.tensor_copy(QY[:, 2 * kv:2 * kv + 2, ds(NMETA + n * P, P)],
                                    PO[:, 0:256].rearrange("p (a b) -> p a b", a=2)).then_inc(y_out, 1)

                def attention(i, first=False):
                    for u8 in range(8):
                        kv = u8 % NKV
                        un = l * 32 + 8 * i + u8
                        mask = mask_cur if u8 < 4 else mask_rest
                        dve.wait_ge(tr_done, un + 1)
                        for g0 in (0, 2):
                            h2 = slice(g0, g0 + 2)
                            for g in range(g0, g0 + 2):
                                dve.wait_ge(scores_done, 4 * un + g + 1)
                                dve.scalar_tensor_tensor(out=s_sb[:, g, :], in0=PS[g % 2][:, 0:KEYS], scalar=SCALE,
                                                         in1=mask[:, :], op0=ALU.mult, op1=ALU.add).then_inc(stt_done, 1)
                            dve.drain()
                            dve.tensor_reduce(stat[:, 0, h2], s_sb[:, h2, :], AX.X, ALU.max)
                            dve.drain()
                            dve.scalar_tensor_tensor(out=stat[:, 2, h2], in0=stat[:, 0, h2], scalar=-1.0,
                                                     in1=nsink[:, 4 * kv + g0:4 * kv + g0 + 2], op0=ALU.mult,
                                                     op1=ALU.min).then_inc(m_ready, 1)
                        dve.drain()
                        dve.tensor_tensor(stat[:, 4, 0:4], sink[:, ds(l, 1), 4 * kv:4 * kv + 4].rearrange("p a b -> p (a b)"),
                                          stat[:, 2, 0:4], ALU.add).then_inc(sink_ready, 1)
                        if u8 % 2 == 1:
                            gi = u8 // 2
                            w_low(S + S_G + gi + 4 * i + 1, (gi + 1) % 2)
                        if u8 == 3:
                            dve.tensor_copy(mask_cur[:, :], mask_rest[:, :])
                        dve.wait_ge(exp_done, un + 1)
                        dve.tensor_tensor(stat[:, 0, 0:4], stat[:, 3, 0:4], stat[:, 5, 0:4], ALU.add)
                        dve.drain()
                        dve.reciprocal(stat[:, 1, 0:4], stat[:, 0, 0:4])
                        dve.drain()
                        dve.tensor_tensor(pm_sb[:, :, :], s_sb[:, :, 0:32],
                                          stat[:, 1, 0:4].unsqueeze(2).to_broadcast([P, 4, 32]), ALU.mult)
                        for g in range(4):
                            mm = dve.tensor_scalar(s_sb[:, g, 32:KEYS], s_sb[:, g, 32:KEYS], stat[:, 1, g:g + 1], None, ALU.mult)
                        mm.then_inc(p_ready, 1)
                        if not (first and u8 == 0):
                            y_store(un - 1, (kv - 1) % NKV, 2 * i + (u8 - 1) // NKV)
                        dve.wait_ge(tr_done, un + 2)
                        dve.tensor_copy(pt_sb[:, 1, :, :], PT[1].rearrange("p (a b) -> p a b", a=4)).then_inc(pt_dve, 1)

                dve.tensor_scalar(nsink[:, :], sink[:, ds(l, 1), :].rearrange("p a b -> p (a b)"), -1.0, None, ALU.mult)
                attention(0, first=True)
                with dve.Fori(1, NB) as i:
                    attention(i)
                y_store(l * 32 + 31, NKV - 1, NBLK - 1)

                with dve.Fori(0, KD) as k:
                    dve.wait_ge(ys_hi, l * KD + k + 1)
                    split_low(HL[:, ds(k, 1), :], QY[:, ds(k, 1), :], HH[:, ds(k, 1), :], 1.0, ys_ready)
                def m1(t):
                    par = t % 2
                    dve.wait_ge(strip_done, S + S_OA + t + 3)
                    dve.wait_ge(gate_loaded[par], 16 * (l * 8 + t // 2 + 1))
                    dve.scalar_tensor_tensor(out=v3(QY[:, t, :]), in0=v3(MT[:, par, :]), scalar=1.0, in1=pset(par)[:, :, 0:CW],
                                             op0=ALU.add, op1=ALU.mult).then_inc(freed(par), 1)

                def gelu(i):
                    yr = X[:, ds(i, 1), 0:L].rearrange("p o (t j) -> p (o j) t", t=CT)
                    xz = X[:, ds(4 + i, 1), 0:L].rearrange("p o (j t) -> p (o j) t", t=CT)
                    tk = lambda t: t.rearrange("p (j t) -> p j t", t=CT)
                    dve.wait_ge(ge[0], l * 4 + i + 1)
                    dve.tensor_scalar(MT[:, 2, 0:L], MT[:, 2, 0:L], 0.044715, 1.0, ALU.mult, ALU.add)
                    dve.drain()
                    dve.tensor_tensor(tk(MT[:, 2, 0:L]), tk(MT[:, 2, 0:L]), yr, ALU.mult).then_inc(ge[1], 1)
                    dve.wait_ge(ge[2], l * 4 + i + 1)
                    dve.scalar_tensor_tensor(out=xz, in0=tk(MT[:, 3, 0:L]), scalar=1.0, in1=yr,
                                             op0=ALU.add, op1=ALU.mult).then_inc(ev_f, 1)
                    dve.wait_ge(ev_hi, l * EVH + i + 1)
                    split_low(BL[:, ds(4 + i, 1), :], X[:, ds(4 + i, 1), :], BL[:, ds(i, 1), :], 0.5, z_ready)

                dve.memset(X[:, 4:8, L:LP], 0.0)
                for t in range(8):
                    w_low(S + S_OA + t + 1, (t + 1) % 2)
                    if 3 <= t < 7:
                        gelu(t - 3)
                    m1(t)
                w_low(S + S_GLU + 1, 1, 4)
                with dve.Fori(0, 2) as i:
                    for par in range(2):
                        k = 2 * i + par
                        dve.drain()
                        if par == 0:
                            dve.wait_ge(free_a, A + a_use(S_GLU) + i + 2)
                        else:
                            dve.wait_ge(free_b, B + b_use(S_GLU + 1) + i + 2)
                        dve.scalar_tensor_tensor(out=MT[:, 3:4, :], in0=MT[:, 2:3, :], scalar=1.0, in1=X[:, ds(4 + k, 1), :],
                                                 op0=ALU.add, op1=ALU.mult).then_inc(ev_f, 1)
                        w_low(S + S_GLU + par + 2 + 2 * i, par, 4)
                        dve.wait_ge(ev_hi, l * EVH + 4 + k + 1)
                        split_low(XR[:, ds(4 + k, 1), :], MT[:, 3:4, :], XR[:, ds(k, 1), :], 0.25, z2_ready)
                def merge(i, ks):
                    for par in range(2):
                        t = 2 * i + par
                        dve.wait_ge(strip_done, S + S_OS + t + 3)
                        dve.wait_ge(gate_loaded[par], 16 * (l * 8 + 4 + i + 1))
                        dve.scalar_tensor_tensor(out=v3(MT[:, 2, :]), in0=v3(MT[:, par, :]), scalar=1.0,
                                                 in1=pset(par)[:, :, 0:CW], op0=ALU.add, op1=ALU.mult).then_inc(freed(par), 1)
                        dve.drain()
                        dve.tensor_tensor(MT[:, 3:4, :], MT[:, 2:3, :], QY[:, ds(t, 1), :], ALU.add).then_inc(ev_f, 1)
                        w_low(S + S_OS + par + 2 + 2 * i, par, ks)
                        dve.wait_ge(ev_hi, l * EVH + 8 + t + 1)
                        split_low(BL[:, ds(t, 1), :], MT[:, 3:4, :], BH[:, ds(t, 1), :], 0.5, mg_ready)

                with dve.Fori(0, 3) as i:
                    merge(i, 4)
                merge(3, KD)
                with dve.Fori(0, 4) as i:
                    for par in range(2):
                        w_low(S + S_OUT + par + 2 + 2 * i, par)
                post_norm(0, 1, 1, pre=2)
                rsqrt(PB, free_b, 2, MT[:, 0, :])

                def up_strip(q, par, i):
                    t = 2 * i + par
                    dve.wait_ge(strip_done, S + S_FF + t + 16 * q + 3)
                    dve.scalar_tensor_tensor(out=v3(MT[:, 2, :]), in0=pset(par)[:, :, 0:CW], scalar=0.0,
                                             in1=v3(MT[:, 0, :]), op0=ALU.max, op1=ALU.mult).then_inc(relu_done, 1)
                    dve.drain()
                    dve.sem_inc(freed(par), 1)
                    dve.wait_ge(ev_hi, l * EVH + 16 + q * 8 + t + 1)
                    split_low(BL[:, ds(t, 1), :], MT[:, 3:4, :], BH[:, ds(t, 1), :], 1.0, hid_ready)

                def mlp(q, first=False):
                    if first:
                        up_strip(0, 0, 0)
                        w_low(S + S_FF + 2, 0)
                        up_strip(0, 1, 0)
                    with dve.Fori(int(first), 4) as i:
                        for par in range(2):
                            w_low(S + S_FF + par + 1 + 2 * i + 16 * q, (par + 1) % 2)
                            up_strip(q, par, i)
                    dve.wait_ge(acc_done, l + 1)
                    dve.sem_inc(passed, 1)
                    with dve.Fori(0, 4) as i:
                        for par in range(2):
                            t = 2 * i + par
                            w_low(S + S_FF + 8 + par + 1 + 2 * i + 16 * q, (par + 1) % 2)
                            dve.wait_ge(strip_done, S + S_FF + 8 + t + 16 * q + 3)
                            xt = X[:, ds(t, 1), :].rearrange("p o (c w) -> p (o c) w", c=NC3)
                            dve.tensor_tensor(xt, xt, pset(par)[:, :, 0:CW], ALU.add).then_inc(freed(par), 1)

                mlp(0, first=True)
                with dve.Fori(1, 4) as q:
                    mlp(q)
                post_norm(1, 3, 3)

            for n in range(1, NBLK, 2):
                dve.wait_ge(out_tr, n + 1)
                dve.tensor_copy(OT[:, n, :].rearrange("p (c w) -> p c w", c=2), PB[:, 0:2, :]).then_inc(free_b, 1)

        @block.gpsimd
        def _(pool):
            def await_(s, v):
                pool.wait_ge(s, v)
                pool.sem_inc(passed, 1)

            pool.sem_inc(mix_acc, 1)
            pool.sem_inc(x_ready, 1)
            pool.sem_inc(y_stored, 128)
            pool.memset(ones[:, :], 1.0)
            pool.memset(X[:, :, L:LP], 0.0)
            pool.drain()
            pool.sem_inc(pool_init, 1)
            await_(const_loaded, 16 * 13)
            pool.tensor_scalar(bgluh[:, :, :], bglu[:, :, :], 0.5, 0.0, ALU.mult, ALU.add)
            def tt(o, a, b, op):
                return pool.tensor_tensor(o, a, b, op)

            def cmul(o, x, re_b, im_b, t1, t2, op=ALU.subtract):
                tt(t1, x, re_b, ALU.mult)
                tt(t2, x, im_b, ALU.mult)
                pool.drain()
                return tt(o, t1, t2[:, :, ::-1] if len(t2.shape) == 3 else t2[:, :, ::-1, :], op)

            with pool.Fori(0, DEPTH) as l:
                await_(h_ready, l * 16 + 8)
                await_(x_stored, 16 * (KD + 16 * l))
                pool.memset(kbuf[:, :, NMETA:KOFF], 0.0).then_inc(pool_init, 1)
                pool.memset(kst[:, :, :], 0.0).then_inc(pool_init, 1)
                pool.memset(Vb[:, 0, :], 0.0).then_inc(pool_init, 1)
                pool.memset(vmeta[:, :], 0.0).then_inc(pool_init, 1)
                pool.memset(ptm_sb[:, :, :], 0.0).then_inc(pool_init, 1)
                c16 = lambda t, i: t[:, 16 * i:16 * i + 16]
                are, aim, ldt, er, th, kk, u1, u2 = (c16(T1p, i) for i in range(8))
                sn, cs, mag, inv, nr, v1, v2, v3_ = (c16(T2p, i) for i in range(8))
                for t, v in ((are, a_pn[0]), (aim, a_pn[1])):
                    pool.dma_start(t, v[ds(l, 1), :, :].rearrange("o q p -> (o q) p"), allow_slow_non_contiguous=True).then_inc(s5_coef, 16)
                for g2 in range(2):
                    pool.dma_start(ldt[NS * g2:NS * g2 + NS, :], dt_v[ds(l, 1), g2, :].to_broadcast([NS, NP]), allow_slow_non_contiguous=True).then_inc(s5_coef, 16)
                await_(s5_coef, 64 * (l + 1))
                pool.memset(u1, float(np.e))
                pool.drain()
                tt(u2, u1, ldt, ALU.pow)
                pool.drain()
                tt(er, are, u2, ALU.mult)
                pool.drain()
                tt(th, aim, u2, ALU.mult)
                pool.drain()
                tt(mag, u1, er, ALU.pow)
                pool.drain()
                pool.tensor_scalar(kk, th, 1.0 / (2 * np.pi), 12582912.0, ALU.mult, ALU.add)
                pool.drain()
                pool.tensor_scalar(kk, kk, -12582912.0, None, ALU.add)
                pool.drain()
                for c in (6.28125, 0.0019340515136718750, 1.2556660464e-06):
                    pool.tensor_scalar(u2, kk, -c, None, ALU.mult)
                    pool.drain()
                    tt(th, th, u2, ALU.add)
                    pool.drain()
                pool.tensor_scalar(th, th, 3.1415925, -3.1415925, ALU.min, ALU.max)
                pool.drain()
                pool.sem_inc(s5_e[0], 1)
                await_(s5_e[1], l + 1)
                A1, A1s = PW[:, 1, :, :], PWs[:, 1, :, :]
                tt(A1[:, :, 0], mag, cs, ALU.mult)
                pool.drain()
                tt(A1[:, :, 1], mag, sn, ALU.mult)
                pool.drain()
                pool.memset(PW[:, 0, :, 0], 1.0)
                pool.drain()
                pool.memset(PW[:, 0, :, 1], 0.0)
                pool.drain()

                def partners(dst, src, lo, hi):
                    pool.tensor_scalar(dst[:, lo:hi, :, 0], src[:, lo:hi, :, 1], -1.0, 0.0, ALU.mult, ALU.add)
                    pool.drain()
                    pool.tensor_scalar(dst[:, lo:hi, :, 1], src[:, lo:hi, :, 1], 1.0, 0.0, ALU.mult, ALU.add)
                    pool.drain()

                q1 = T1p[:, 64:96].rearrange("p (a b) -> p a b", b=2)
                q2 = T1p[:, 96:128].rearrange("p (a b) -> p a b", b=2)
                partners(PWs, PW, 0, 2)
                re1 = PW[:, 1, :, 0:1].to_broadcast([P, NP, 2])
                for t in range(2, CT + 1):
                    cmul(PW[:, t, :, :], PW[:, t - 1, :, :], re1, A1s, q1, q2)
                    pool.drain()
                partners(PWs, PW, 2, CT + 1)
                tt(P8[:, 1, :, :], PW[:, CT, :, :], PW[:, 0, :, 0:1].to_broadcast([P, NP, 2]), ALU.mult)
                pool.drain()
                partners(P8s, P8, 1, 2)
                re8 = P8[:, 1, :, 0:1].to_broadcast([P, NP, 2])
                for t in range(2, RUN + 1):
                    cmul(P8[:, t, :, :], P8[:, t - 1, :, :], re8, P8s[:, 1, :, :], q1, q2)
                    pool.drain()
                partners(P8s, P8, 2, RUN + 1)
                pool.tensor_scalar(nr, A1[:, :, 0], -1.0, None, ALU.add)
                pool.drain()
                tt(v1, are, are, ALU.mult)
                pool.drain()
                tt(v2, aim, aim, ALU.mult)
                pool.drain()
                tt(v1, v1, v2, ALU.add)
                pool.drain()
                pool.memset(v2, -1.0)
                pool.drain()
                tt(inv, v1, v2, ALU.pow)
                pool.drain()
                tt(v1, nr, are, ALU.mult)
                pool.drain()
                tt(v2, A1[:, :, 1], aim, ALU.mult)
                pool.drain()
                tt(v1, v1, v2, ALU.add)
                pool.drain()
                tt(v2, nr, aim, ALU.mult)
                pool.drain()
                tt(v3_, A1[:, :, 1], are, ALU.mult)
                pool.drain()
                tt(v3_, v3_, v2, ALU.subtract)
                pool.drain()
                tt(FB[:, :, 0], v1, inv, ALU.mult)
                pool.drain()
                tt(FB[:, :, 1], v3_, inv, ALU.mult)
                pool.drain()
                pool.tensor_scalar(FBs[:, :, 0], FB[:, :, 1], -1.0, 0.0, ALU.mult, ALU.add)
                pool.drain()
                pool.tensor_scalar(FBs[:, :, 1], FB[:, :, 1], 1.0, 0.0, ALU.mult, ALU.add)
                pool.drain()
                await_(rope_done, l * 10 + 11)
                for k in range(2):
                    await_(u_stored[k], 16 * (2 * l + 2) + 16)
                pool.memset(Mtoe[:, :, :], 0.0)
                pool.memset(St[:, :, :, 0], 0.0)
                pool.drain()
                t1 = T1p[:, :].rearrange("p (a i c) -> p a i c", a=4, i=2)
                t2 = T2p[:, :].rearrange("p (a i c) -> p a i c", a=4, i=2)

                def rb(tab, n):
                    return tab[:, :, 0:1].to_broadcast([P, 4, 2]).unsqueeze(3).to_broadcast([P, 4, 2, n])

                def ib(tab, n):
                    return tab.unsqueeze(3).to_broadcast([P, 4, 2, n])

                def input_matrices(i):
                    b, pr = l * NB + i, ds(4 * i, 4)
                    await_(b_loaded, 112 * (b + 1))
                    cmul(BB[:, :, :, :], Bx[:, :, :, :], rb(FB[:, pr, :], CG), ib(FBs[:, pr, :], CG), t1, t2)
                    pool.drain()
                    for t in range(CT):
                        e = CT - 1 - t
                        cmul(MinT[:, :, :, CG * t:CG * t + CG], BB[:, :, :, :], rb(PW[:, e, pr, :], CG),
                             ib(PWs[:, e, pr, :], CG), t1, t2)
                        pool.drain()
                    pool.sem_inc(s5_min, 1)

                def batch(i):
                    b, pr = l * NB + i, ds(4 * i, 4)
                    await_(s5_ev, 3 * b + 1)
                    if not isinstance(i, int) or i > 0:
                        await_(s5_out, b)
                    for t in range(CT + 1):
                        cmul(W9[:, :, :, CG * t:CG * t + CG], Cc[:, :, :, :], rb(PW[:, t, pr, :], CG),
                             ib(PWs[:, t, pr, :], CG), t1, t2, ALU.add)
                        pool.drain()
                    pool.sem_inc(s5_w, 1)
                    await_(s5_ev, 3 * b + 2)
                    tg = T1p[0:CG, :].rearrange("p (g c) -> p g c", g=8)
                    tt(tg, dsk[0:CG, :].unsqueeze(2).to_broadcast([CG, 8, CG]),
                       ident[0:CG, 0:CG].unsqueeze(1).to_broadcast([CG, 8, CG]), ALU.mult)
                    pool.drain()
                    tt(Gs[0:CG, :, 0:CG], Gs[0:CG, :, 0:CG], tg, ALU.add).then_inc(s5_g, 1)
                    pool.drain()
                    await_(s5_ev, 3 * b + 3)
                    sv = St[:, :, :, 1:NCH + 1].rearrange("q p i (s r) -> q p i s r", s=SEG)

                    def at_r(r, s0, s1):
                        return sv[:, :, :, s0:s1, r].rearrange("q p i s o -> q p i (s o)")

                    def step(dst, src, k, n):
                        a1 = T1p[:, 0:8 * n].rearrange("p (a i c) -> p a i c", a=4, i=2)
                        a2 = T2p[:, 0:8 * n].rearrange("p (a i c) -> p a i c", a=4, i=2)
                        tab, tabs = P8[:, k, pr, :].rearrange("p o a i -> p (o a) i"), P8s[:, k, pr, :].rearrange("p o a i -> p (o a) i")
                        tt(a1, src, rb(tab, n), ALU.mult)
                        tt(a2, src, ib(tabs, n), ALU.mult)
                        pool.drain()
                        tt(a1, a1, a2[:, :, ::-1, :], ALU.subtract)
                        pool.drain()
                        tt(dst, dst, a1, ALU.add)
                        pool.drain()

                    with pool.Fori(0, (RUN - 1) // 3) as r3:
                        for k in range(1, 4):
                            step(at_r(ds(3 * r3 + k, 1), 0, SEG), at_r(ds(3 * r3 + k - 1, 1), 0, SEG), ds(1, 1), SEG)
                    with pool.Fori(0, (SEG - 1) // 3) as s3:
                        ends = sv[:, :, :, :, RUN - 1]
                        for k in range(1, 4):
                            step(ends[:, :, :, ds(3 * s3 + k, 1)], ends[:, :, :, ds(3 * s3 + k - 1, 1)], ds(RUN, 1), 1)
                    with pool.Fori(0, (RUN - 1) // 3) as r3:
                        for k in range(3):
                            step(at_r(ds(3 * r3 + k, 1), 1, SEG), at_r(ds(RUN - 1, 1), 0, SEG - 1), ds(3 * r3 + k + 1, 1), SEG - 1)
                    pool.sem_inc(s5_scan, 1)

                input_matrices(0)
                with pool.Fori(0, NB - 1) as i:
                    batch(i)
                    await_(toe_loaded, 128 * (l * NB + i + 1))
                    input_matrices(i + 1)
                batch(NB - 1)

                def gate(t, par):
                    pool.dma_start(MT[:, par:par + 1, :], gd[ds(t, 1), :, :].rearrange("o p w -> p o w")).then_inc(gate_loaded[par], 16)

                A, B = l * A_PER + A_INIT, l * B_PER + B_INIT
                await_(y_out, l * 32 + 33)
                await_(g_stored, 16 * 16 * (l + 1) + 16)
                for par in range(2):
                    gate(8 + par, par)
                await_(y_stored, 128 * NB * (l + 1) + 128)
                for k in range(4):
                    pool.dma_start(X[:, k, 0:L], yd[k * P:(k + 1) * P, :, :].rearrange("c t j -> c (t j)")).then_inc(yr_loaded, 16)
                with pool.Fori(1, 4) as i:
                    for par in range(2):
                        await_(free_a if par == 0 else free_b,
                                     (A + a_use(S_OA) if par == 0 else B + b_use(S_OA + 1)) + i + 1)
                        gate(8 + 2 * i + par, par)
                for par in range(2):
                    await_(free_a if par == 0 else free_b,
                                 (A + a_use(S_OA) if par == 0 else B + b_use(S_OA + 1)) + 4 + 1)
                    gate(par, par)
                with pool.Fori(1, 4) as i:
                    for par in range(2):
                        await_(free_a if par == 0 else free_b,
                                     (A + a_use(S_OS) if par == 0 else B + b_use(S_OS + 1)) + i + 1)
                        gate(2 * i + par, par)
                await_(mg_ready, l * KD + KD)
                for j in range(2):
                    if j == 1:
                        await_(h_ready, l * 16 + 16)
                        await_(sq_ready, l * 16 + 16)
                        await_(x_stored, 16 * (2 * KD + 16 * l))
                        pool.memset(X[:, :, :], 0.0).then_inc(acc_done, 1)
                        await_(relu_done, l * 32 + 32)
                    pool.memset(MT[:, 0, :], 0.0)
                    pool.drain()
                    with pool.Fori(0, KD - 1) as t:
                        await_(mix_sq, l * 16 + 8 * j + t + 1)
                        tt(MT[:, 0, :], MT[:, 0, :], MT[:, 1, :], ALU.add).then_inc(mix_acc, 1)
                        pool.drain()
                    await_(xo_loaded, 16 * (l * 16 + j * 8 + 8))
                    for k in range(KD) if j == 0 else BY_POOL:
                        await_(post_scaled, l * 16 + j * 8 + k + 1)
                        tt(X[:, k, :], X[:, k, :], XO[:, k, :], ALU.add).then_inc(x_ready, 1)


_INS = ["x", "meta_tokens", "norm_mix_pre", "norm_mix_post", "norm_mlp_pre", "norm_mlp_post", "w_in", "ssm_a_re",
        "ssm_a_im", "ssm_log_dt", "ssm_b_re", "ssm_b_im", "ssm_c_re", "ssm_c_im", "ssm_d", "w_glu", "b_glu",
        "attn_sinks", "w_o_ssm", "w_o_attn", "w_out", "w_up", "w_down"]


def shape_constants():
    inv = (1.0 / (10000.0 ** (np.arange(0, HD, 2, dtype=np.float32) / HD))).astype(np.float32)
    ang = np.arange(L, dtype=np.float32)[None, :] * inv[:, None]
    cos, sin = np.zeros((P, LP), np.float32), np.zeros((P, LP), np.float32)
    cos[:, :L] = np.tile(np.cos(ang), (4, 1))
    sin[:, :L] = np.concatenate([-np.sin(ang), np.sin(ang)] * 2, 0)
    q, k = np.arange(P)[:, None], np.arange(P)[None, :]
    mask = np.full((2, P, KEYS), NEG, np.float32)
    mask[:, :, 0:NMETA] = 0.0
    mask[1, :, 32:160] = np.where(k > q, 0.0, NEG)
    mask[:, :, 160:288] = np.where(k <= q, 0.0, NEG)
    m0 = np.where(np.arange(NMETA)[None, :] <= np.arange(NMETA)[:, None], 0.0, NEG).astype(np.float32)
    return {"cos_t": cos, "sin_t": sin, "mask_t": mask, "mask0_t": m0, "ident_t": np.eye(P, dtype=np.float32)}


def kernel(**inputs):
    import concourse.bacc as bacc
    from concourse.bass_utils import run_bass_kernel_spmd

    nc = bacc.Bacc("TRN2", target_bir_lowering=False, num_devices=1)
    arrays, aps = {}, {}
    named = {n: np.ascontiguousarray(inputs[n]) for n in _INS}
    named["x"] = named["x"].reshape(SEQ, D)
    named.update(shape_constants())
    for n, a in named.items():
        arrays[f"in_{n}"] = a
        aps[n] = nc.dram_tensor(f"in_{n}", a.shape, mybir.dt.from_np(a.dtype), kind="ExternalInput").ap()
    out = nc.dram_tensor("out_dram", (SEQ, D), F32, kind="ExternalOutput").ap()
    g = aps
    build(nc, g["x"], g["meta_tokens"],
          [g["norm_mix_pre"], g["norm_mix_post"], g["norm_mlp_pre"], g["norm_mlp_post"]], g["w_in"], g["ssm_a_re"],
          g["ssm_a_im"], g["ssm_log_dt"], g["ssm_b_re"], g["ssm_b_im"], g["ssm_c_re"], g["ssm_c_im"], g["ssm_d"],
          g["w_glu"], g["b_glu"], g["attn_sinks"], g["w_o_ssm"], g["w_o_attn"], g["w_out"], g["w_up"], g["w_down"],
          g["cos_t"], g["sin_t"], g["mask_t"], g["mask0_t"], g["ident_t"], out)
    r = run_bass_kernel_spmd(nc, [arrays], core_ids=[0])
    return r.results[0]["out_dram"].reshape(1, SEQ, D)
```
